# Optimizing a Trainium2 kernel written in Bass

```python
import jax, jax.numpy as jnp
from jax import lax
import numpy as np

D_MODEL = 1024
BATCH = 1
SEQ = 512
DEPTH = 2

CTX_LEN = 256
GRID_W = 64
MIX_WIDTH = D_MODEL
RET_HEADS = 4
RET_WIDTH = MIX_WIDTH // 4
RET_DV = RET_WIDTH // RET_HEADS
RET_DK = RET_DV // 2
GLA_HEADS = 4
GLA_WIDTH = MIX_WIDTH // 4
GLA_DV = GLA_WIDTH // GLA_HEADS
GLA_DK = GLA_DV // 2
GLA_RANK = 16
GLA_TAU = 16.0
GQA_WIDTH = MIX_WIDTH - RET_WIDTH - GLA_WIDTH
GQA_HEAD_DIM = 64
GQA_HEADS = GQA_WIDTH // GQA_HEAD_DIM
GQA_KV_HEADS = 2
GQA_GROUP = GQA_HEADS // GQA_KV_HEADS
D_FF = 4 * D_MODEL
SCAN_CHUNK = 64
Q_BLOCK = 128
ROPE_BASE = 10000.0
NORM_EPS = 1e-6
IN_SPLIT_SIZES = (RET_HEADS * RET_DK, RET_HEADS * RET_DK, RET_WIDTH, RET_WIDTH,
                  GLA_HEADS * GLA_DK, GLA_HEADS * GLA_DK, GLA_WIDTH, GLA_WIDTH, 2 * GLA_RANK,
                  GQA_WIDTH, GQA_KV_HEADS * GQA_HEAD_DIM, GQA_KV_HEADS * GQA_HEAD_DIM)
IN_WIDTH = sum(IN_SPLIT_SIZES)

kernel_name = 'hybrid_ret_gla_gqa_prefix_dit_block'

def rms_norm(x, g):
    xf = x.astype(jnp.float32)
    y = xf * lax.rsqrt(jnp.mean(xf * xf, axis=-1, keepdims=True) + NORM_EPS)
    return (y * g.astype(jnp.float32)).astype(x.dtype)

def head_rms(x):
    xf = x.astype(jnp.float32)
    return (xf * lax.rsqrt(jnp.mean(xf * xf, axis=-1, keepdims=True) + NORM_EPS)).astype(x.dtype)

def head_layernorm(x):
    xf = x.astype(jnp.float32)
    mu = jnp.mean(xf, axis=-1, keepdims=True)
    xc = xf - mu
    return (xc * lax.rsqrt(jnp.mean(xc * xc, axis=-1, keepdims=True) + NORM_EPS)).astype(x.dtype)

def modulate(h, shift, scale):
    return h * (1.0 + scale) + shift

def split_heads(a, n_heads):
    return a.reshape(a.shape[:-1] + (n_heads, a.shape[-1] // n_heads))

def _rotate(x, ang):
    x1, x2 = jnp.split(x, 2, axis=-1)
    cos = jnp.cos(ang)[:, None, :]
    sin = jnp.sin(ang)[:, None, :]
    return jnp.concatenate([x1 * cos - x2 * sin, x1 * sin + x2 * cos], axis=-1)

def axial_rope(x, row, col):
    d = x.shape[-1]
    n_freq = d // 4
    inv_freq = ROPE_BASE ** (-jnp.arange(n_freq, dtype=jnp.float32) / n_freq)
    xf = x.astype(jnp.float32)
    x_row, x_col = jnp.split(xf, 2, axis=-1)
    out = jnp.concatenate([_rotate(x_row, row[:, None] * inv_freq),
                           _rotate(x_col, col[:, None] * inv_freq)], axis=-1)
    return out.astype(x.dtype)

def chunk_scan(q, k, v, g, s0, inclusive):
    bsz, length, heads, _ = q.shape
    dv = v.shape[-1]
    n_chunks = length // SCAN_CHUNK

    def to_chunks(a):
        a = a.astype(jnp.float32).reshape(bsz, n_chunks, SCAN_CHUNK, heads, a.shape[-1])
        return a.transpose(1, 0, 3, 2, 4)

    mask = jnp.tril(jnp.ones((SCAN_CHUNK, SCAN_CHUNK), dtype=bool), 0 if inclusive else -1)

    def step(state, inp):
        qc, kc, vc, gc = inp
        b = jnp.cumsum(gc, axis=-2)
        b_last = b[..., -1:, :]
        q_dec = qc * jnp.exp(b)
        scores = jnp.einsum('bhid,bhjd->bhij', q_dec, kc * jnp.exp(-b))
        scores = jnp.where(mask, scores, 0.0)
        out = (jnp.einsum('bhij,bhje->bhie', scores, vc)
               + jnp.einsum('bhid,bhde->bhie', q_dec, state))
        state = (jnp.exp(b_last)[..., 0, :, None] * state
                 + jnp.einsum('bhjd,bhje->bhde', kc * jnp.exp(b_last - b), vc))
        return state, out

    s_final, o = lax.scan(step, s0.astype(jnp.float32),
                          (to_chunks(q), to_chunks(k), to_chunks(v), to_chunks(g)))
    o = o.transpose(1, 0, 3, 2, 4).reshape(bsz, length, heads, dv)
    return o.astype(v.dtype), s_final

def bidir_prefix_scan(q_l, k_l, v_l, gf_l, gb_l, q_c, k_c, v_c, gf_c, gb_c):
    bsz, _, heads, dk = q_l.shape
    dv = v_l.shape[-1]
    zero = jnp.zeros((bsz, heads, dk, dv), jnp.float32)
    rev = lambda a: a[:, ::-1]
    oc_f, sc_f = chunk_scan(q_c, k_c, v_c, gf_c, zero, True)
    ol_f, _ = chunk_scan(q_l, k_l, v_l, gf_l, sc_f, True)
    oc_b, sc_b = chunk_scan(rev(q_c), rev(k_c), rev(v_c), rev(gb_c), zero, False)
    ol_b, _ = chunk_scan(rev(q_l), rev(k_l), rev(v_l), rev(gb_l), sc_b, False)
    return ol_f + rev(ol_b), oc_f + rev(oc_b)

def _attend(q, keys, vals):
    s = jnp.einsum('bkgqd,bksd->bkgqs', q, keys).astype(jnp.float32) * (GQA_HEAD_DIM ** -0.5)
    p = jax.nn.softmax(s, axis=-1).astype(vals.dtype)
    return jnp.einsum('bkgqs,bksd->bkgqd', p, vals)

def gqa_latent(q, k_lat, v_lat, k_ctx, v_ctx):
    bsz, length = q.shape[:2]
    keys = jnp.concatenate([k_ctx, k_lat], axis=1).transpose(0, 2, 1, 3)
    vals = jnp.concatenate([v_ctx, v_lat], axis=1).transpose(0, 2, 1, 3)
    n_blocks = length // Q_BLOCK
    qb = q.reshape(bsz, n_blocks, Q_BLOCK, GQA_KV_HEADS, GQA_GROUP, GQA_HEAD_DIM).transpose(1, 0, 3, 4, 2, 5)
    o = lax.map(lambda qblk: _attend(qblk, keys, vals), qb)
    return o.transpose(1, 0, 4, 2, 3, 5).reshape(bsz, length, GQA_WIDTH)

def gqa_context(q, k, v):
    bsz, n = q.shape[:2]
    qg = q.reshape(bsz, n, GQA_KV_HEADS, GQA_GROUP, GQA_HEAD_DIM).transpose(0, 2, 3, 1, 4)
    o = _attend(qg, k.transpose(0, 2, 1, 3), v.transpose(0, 2, 1, 3))
    return o.transpose(0, 3, 1, 2, 4).reshape(bsz, n, GQA_WIDTH)

def token_mix(h_lat, h_ctx, w_in, w_out, ret_decay_logit, gla_gate_w, gla_gate_b, qk_norm_g, row, col, need_ctx):
    cuts = [int(v) for v in np.cumsum(IN_SPLIT_SIZES)[:-1]]
    pl = jnp.split(h_lat @ w_in, cuts, axis=-1)
    pc = jnp.split(h_ctx @ w_in, cuts, axis=-1)
    bsz, n_lat = h_lat.shape[:2]
    n_ctx = h_ctx.shape[1]

    k_scale = RET_DK ** -0.5
    rq_l = axial_rope(split_heads(pl[0], RET_HEADS), row, col)
    rk_l = axial_rope(split_heads(pl[1], RET_HEADS), row, col) * k_scale
    rv_l = split_heads(pl[2], RET_HEADS)
    rq_c = split_heads(pc[0], RET_HEADS)
    rk_c = split_heads(pc[1], RET_HEADS) * k_scale
    rv_c = split_heads(pc[2], RET_HEADS)
    log_gamma = jax.nn.log_sigmoid(ret_decay_logit.astype(jnp.float32))
    gf_l = jnp.broadcast_to(log_gamma[0][:, None], rq_l.shape)
    gb_l = jnp.broadcast_to(log_gamma[1][:, None], rq_l.shape)
    gf_c = jnp.broadcast_to(log_gamma[0][:, None], rq_c.shape)
    gb_c = jnp.broadcast_to(log_gamma[1][:, None], rq_c.shape)
    ro_l, ro_c = bidir_prefix_scan(rq_l, rk_l, rv_l, gf_l, gb_l, rq_c, rk_c, rv_c, gf_c, gb_c)
    y_ret_l = jax.nn.silu(pl[3]) * head_layernorm(ro_l).reshape(bsz, n_lat, RET_WIDTH)

    def gla_gates(a):
        z_f = a[..., :GLA_RANK] @ gla_gate_w[0] + gla_gate_b[0]
        z_b = a[..., GLA_RANK:] @ gla_gate_w[1] + gla_gate_b[1]
        g_f = jax.nn.log_sigmoid(z_f.astype(jnp.float32)) / GLA_TAU
        g_b = jax.nn.log_sigmoid(z_b.astype(jnp.float32)) / GLA_TAU
        return split_heads(g_f, GLA_HEADS), split_heads(g_b, GLA_HEADS)

    q_scale = GLA_DK ** -0.5
    gq_l = split_heads(pl[4], GLA_HEADS) * q_scale
    gk_l = split_heads(pl[5], GLA_HEADS)
    gv_l = split_heads(pl[6], GLA_HEADS)
    gq_c = split_heads(pc[4], GLA_HEADS) * q_scale
    gk_c = split_heads(pc[5], GLA_HEADS)
    gv_c = split_heads(pc[6], GLA_HEADS)
    ggf_l, ggb_l = gla_gates(pl[8])
    ggf_c, ggb_c = gla_gates(pc[8])
    go_l, go_c = bidir_prefix_scan(gq_l, gk_l, gv_l, ggf_l, ggb_l, gq_c, gk_c, gv_c, ggf_c, ggb_c)
    y_gla_l = jax.nn.silu(pl[7]) * head_rms(go_l).reshape(bsz, n_lat, GLA_WIDTH)

    aq_l = axial_rope(rms_norm(split_heads(pl[9], GQA_HEADS), qk_norm_g[0]), row, col)
    ak_l = axial_rope(rms_norm(split_heads(pl[10], GQA_KV_HEADS), qk_norm_g[1]), row, col)
    av_l = split_heads(pl[11], GQA_KV_HEADS)
    ak_c = rms_norm(split_heads(pc[10], GQA_KV_HEADS), qk_norm_g[1])
    av_c = split_heads(pc[11], GQA_KV_HEADS)
    y_gqa_l = gqa_latent(aq_l, ak_l, av_l, ak_c, av_c)

    y_lat = jnp.concatenate([y_ret_l, y_gla_l, y_gqa_l], axis=-1) @ w_out
    if not need_ctx:
        return y_lat, None
    aq_c = rms_norm(split_heads(pc[9], GQA_HEADS), qk_norm_g[0])
    y_ret_c = jax.nn.silu(pc[3]) * head_layernorm(ro_c).reshape(bsz, n_ctx, RET_WIDTH)
    y_gla_c = jax.nn.silu(pc[7]) * head_rms(go_c).reshape(bsz, n_ctx, GLA_WIDTH)
    y_gqa_c = gqa_context(aq_c, ak_c, av_c)
    y_ctx = jnp.concatenate([y_ret_c, y_gla_c, y_gqa_c], axis=-1) @ w_out
    return y_lat, y_ctx

def sq_relu_mlp(h, w1, w2):
    return jnp.square(jax.nn.relu(h @ w1)) @ w2

def setup_inputs(seed: int = 0) -> dict:
    key = jax.random.key(seed)
    ks = jax.random.split(key, 20)
    nrm = lambda k, shape, s: jax.random.normal(k, shape, jnp.float32) * s
    ret_logit0 = jnp.asarray(np.log(2.0 ** (5.0 + np.arange(RET_HEADS)) - 1.0), dtype=jnp.float32)
    return {
        'x': nrm(ks[0], (BATCH, SEQ, D_MODEL), 1.0),
        'c': nrm(ks[1], (BATCH, D_MODEL), 1.0),
        'ctx': nrm(ks[2], (BATCH, CTX_LEN, D_MODEL), 1.0),
        'c_ctx': nrm(ks[3], (D_MODEL,), 1.0),
        'mod_w': nrm(ks[4], (DEPTH, D_MODEL, 6 * D_MODEL), 0.5 * D_MODEL ** -0.5),
        'mod_b': nrm(ks[5], (DEPTH, 6 * D_MODEL), 0.01),
        'attn_norm_g': 1.0 + nrm(ks[6], (DEPTH, D_MODEL), 0.05),
        'mlp_norm_g': 1.0 + nrm(ks[7], (DEPTH, D_MODEL), 0.05),
        'w_in': nrm(ks[8], (DEPTH, D_MODEL, IN_WIDTH), D_MODEL ** -0.5),
        'w_out': nrm(ks[9], (DEPTH, MIX_WIDTH, D_MODEL), MIX_WIDTH ** -0.5),
        'ret_decay_logit': ret_logit0 + nrm(ks[10], (DEPTH, 2, RET_HEADS), 0.01),
        'gla_gate_w': nrm(ks[11], (DEPTH, 2, GLA_RANK, GLA_HEADS * GLA_DK), GLA_RANK ** -0.5),
        'gla_gate_b': nrm(ks[12], (DEPTH, 2, GLA_HEADS * GLA_DK), 0.1),
        'qk_norm_g': 1.0 + nrm(ks[13], (DEPTH, 2, GQA_HEAD_DIM), 0.05),
        'mlp_w1': nrm(ks[14], (DEPTH, D_MODEL, D_FF), D_MODEL ** -0.5),
        'mlp_w2': nrm(ks[15], (DEPTH, D_FF, D_MODEL), D_FF ** -0.5),
        'final_norm_g': 1.0 + nrm(ks[16], (D_MODEL,), 0.05),
    }

def reference(x, c, ctx, c_ctx, mod_w, mod_b, attn_norm_g, mlp_norm_g, w_in, w_out, ret_decay_logit,
              gla_gate_w, gla_gate_b, qk_norm_g, mlp_w1, mlp_w2, final_norm_g):
    n_lat = x.shape[1]
    rows = n_lat // GRID_W
    row = jnp.repeat(jnp.arange(rows, dtype=jnp.float32), GRID_W)
    col = (jnp.arange(rows * GRID_W) % GRID_W).astype(jnp.float32)
    silu_c = jax.nn.silu(c)
    silu_cc = jax.nn.silu(c_ctx)
    for i in range(DEPTH):
        need_ctx = i < DEPTH - 1
        sh_a, sc_a, gt_a, sh_m, sc_m, gt_m = [m[:, None, :] for m in
                                              jnp.split(silu_c @ mod_w[i] + mod_b[i], 6, axis=-1)]
        csh_a, csc_a, cgt_a, csh_m, csc_m, cgt_m = jnp.split(silu_cc @ mod_w[i] + mod_b[i], 6, axis=-1)
        h_lat = modulate(rms_norm(x, attn_norm_g[i]), sh_a, sc_a)
        h_ctx = modulate(rms_norm(ctx, attn_norm_g[i]), csh_a, csc_a)
        y_lat, y_ctx = token_mix(h_lat, h_ctx, w_in[i], w_out[i], ret_decay_logit[i], gla_gate_w[i],
                                 gla_gate_b[i], qk_norm_g[i], row, col, need_ctx)
        x = x + gt_a * y_lat
        x = x + gt_m * sq_relu_mlp(modulate(rms_norm(x, mlp_norm_g[i]), sh_m, sc_m), mlp_w1[i], mlp_w2[i])
        if need_ctx:
            ctx = ctx + cgt_a * y_ctx
            ctx = ctx + cgt_m * sq_relu_mlp(modulate(rms_norm(ctx, mlp_norm_g[i]), csh_m, csc_m),
                                            mlp_w1[i], mlp_w2[i])
    return rms_norm(x, final_norm_g)


_drawn_inputs = setup_inputs


def setup_inputs(seed=0):
    import zlib

    import numpy as np

    out = dict(_drawn_inputs(seed))
    spreads = {}
    factors = {'attn_norm_g': 2.922, 'gla_gate_b': 8.0, 'qk_norm_g': 8.0}
    for name, (base, spread) in spreads.items():
        noise = np.random.default_rng([zlib.crc32(name.encode()), seed]).standard_normal(out[name].shape)
        drawn = base * np.exp(spread * noise) if base else spread * noise
        out[name] = __import__('jax').numpy.asarray(drawn.astype(out[name].dtype))
    for name, factor in factors.items():
        out[name] = (out[name] * factor).astype(out[name].dtype)
    return out
```

```python
from contextlib import ExitStack

import concourse.bass as bass
from concourse import mybir

F32 = mybir.dt.float32
F32R = mybir.dt.float32r
ALU = mybir.AluOpType
ACT = mybir.ActivationFunctionType
AX = mybir.AxisListType

P = 128
D = 1024
KT = D // P
CTX, LAT = 256, 512
T = CTX + LAT
TT = T // P
DEPTH = 2
CH = 64
NCH = T // CH
FF = 4 * D
NFG = FF // D
EPS = 1e-6
RING = 4
SLAB = 256
DK, DV = 32, 64
HD = 64
HQ = 8
KSCALE = DK ** -0.5
TAU = 16.0
W_IN = 2336
W_IN_SLABS = [(0, 256), (256, 256), (512, 256), (768, 256), (1024, 256), (1280, 256), (1536, 32),
              (1568, 256), (1824, 256), (2080, 256)]
N_MOD = 6 * D // P
SH_A, SC_A, GT_A, SH_M, SC_M, GT_M = (KT * i for i in range(6))

COLS_C = 0
COLS_FG = 16
COLS_L = 24
L_MODB, L_AG, L_MG, L_QG, L_KG, L_GB, L_RD, L_N = 0, 48, 56, 64, 65, 66, 68, 70


def layer_program():
    win = [("w", "in", s) for s in range(len(W_IN_SLABS))]
    phases = {}
    phases["start"] = [("m", 0, n) for n in range(8)]
    rest = [("m", 0, n) for n in range(8, 24)]
    mixed = []
    for s, slab in enumerate(win):
        mixed.append(slab)
        take = 2 if s < 6 else 1
        mixed += rest[:take]
        rest = rest[take:]
    assert not rest
    phases["in0"] = mixed
    mods = iter([("m", 1, n) for n in range(8)])
    phases["out0"] = [("w", "out", 0), next(mods), next(mods), ("w", "out", 1), next(mods), next(mods), next(mods),
                      next(mods), next(mods), ("w", "out", 2), ("w", "out", 3), next(mods)]
    phases["mlp0"] = [("w", "1", 0), ("w", "1", 1), ("m", 1, 8), ("w", "1", 2), ("w", "1", 3), ("m", 1, 9),
                      ("w", "2", 0), ("w", "2", 1), ("m", 1, 10), ("w", "2", 2), ("w", "2", 3), ("m", 1, 11)]
    phases["in1"] = win
    phases["out1"] = [("w", "out", s) for s in range(4)]
    phases["mlp1"] = [("w", "1", s) for s in range(4)] + [("w", "2", s) for s in range(4)]
    return phases


def build(nc, d):
    phases = layer_program()
    order = ["start", "in0", "out0", "mlp0", "in1", "out1", "mlp1"]
    repeats = {p: NFG if p.startswith("mlp") else 1 for p in order}
    first_slab, first_w, first_m = {}, {}, {}
    ns = nw = nm = 0
    for p in order:
        first_slab[p], first_w[p], first_m[p] = ns, nw, nm
        ns += repeats[p] * len(phases[p])
        nw += repeats[p] * sum(s[0] == "w" for s in phases[p])
        nm += repeats[p] * sum(s[0] == "m" for s in phases[p])
    flat = [s[0] for p in order for _ in range(repeats[p]) for s in phases[p]]

    ctx = ExitStack()
    with ctx:
        def sb(name, shape, dt=F32, stack=ctx):
            return stack.enter_context(nc.sbuf_tensor(name, shape, dt))

        sems = {}

        def sem(name):
            if name not in sems:
                sems[name] = ctx.enter_context(nc.semaphore(name))
            return sems[name]

        xT = sb("xT", [P, KT, T])
        raw = sb("raw", [P, RING, KT, SLAB])
        w_hi = sb("w_hi", [P, 2, KT, P], F32R)
        w_lo = sb("w_lo", [P, 2, KT, P], F32R)
        rope = sb("rope", [P, 4, LAT])
        scan_mask = sb("scan_mask", [P, T])
        squares = sb("squares", [P, 5, P])
        cols = sb("cols", [P, COLS_L + DEPTH * L_N])
        gate_w = sb("gate_w", [32, DEPTH, 2, P])
        modv = sb("modv", [P, DEPTH, N_MOD, 2])
        silu_c = sb("silu_c", [P, KT, 2])
        gain = sb("gain", [P, KT, 2])
        lgam = sb("lgam", [P, DEPTH, 2])
        small = sb("small", [P, 64])
        decs = sb("decs", [P, 2, NCH])
        with ExitStack() as own:
            nsq = sb("nsq", [P, 2, T], F32, own)
            nacc = sb("nacc", [P, T], F32, own)
            nrs = sb("nrs", [P, T], F32, own)
        s_diag = sb("s_diag", [P, 2, NCH, 2 * DV])
        mask_f, mask_b, ident, ones, blocks = (squares[:, i, :] for i in range(5))

        with ExitStack() as own:
            g2 = sb("g2", [P, 2, T], F32, own)
            bcum = sb("bcum", [P, 2, T], F32, own)
            q_dec = sb("q_dec", [P, 2, T], F32, own)
            k_dec = sb("k_dec", [P, 2, T], F32, own)
            k2T = sb("k2T", [P, 2, TT, P], F32, own)
            state = sb("state", [P, 2, NCH, DV], F32, own)
            probs = sb("probs", [P, 2, 2, P], F32, own)
            ptmp = sb("ptmp", [P, 2, 2, P], F32, own)
        with ExitStack() as own:
            rope_sw = sb("rope_sw", [P, LAT], F32, own)
            rope_t = sb("rope_t", [P, LAT], F32, own)
            qsq = sb("qsq", [P, 2, T], F32, own)
            qrs = sb("qrs", [P, 2, T], F32, own)
            k_dup = sb("k_dup", [P, 2, T], F32, own)
            prow = sb("prow", [P, 2, T], F32, own)
            pT = sb("pT", [P, 2, T], F32, own)
            yq = sb("yq", [P, 2, HQ * HD], F32, own)
        h_hi = sb("h_hi", [P, KT, T], F32R)
        h_lo = sb("h_lo", [P, KT, T], F32R)
        with ExitStack() as own:
            u_hi = sb("u_hi", [P, KT, T], F32R, own)
            u_lo = sb("u_lo", [P, KT, T], F32R, own)
            u_full = sb("u_full", [P, 2, T], F32, own)
        with ExitStack() as own:
            nout = sb("nout", [P, 2, LAT], F32, own)
        ret_q = sb("ret_q", [P, T])
        ret_k = sb("ret_k", [P, T])
        gla_q = sb("gla_q", [P, T])
        gla_k = sb("gla_k", [P, T])
        low = sb("low", [32, T])
        ret_v = sb("ret_v", [P, TT, 256])
        gla_v = sb("gla_v", [P, TT, 256])
        att_v = sb("att_v", [P, TT, P])
        att_k = sb("att_k", [P, T])
        y = sb("y", [P, 8, T])

        pair = [ctx.enter_context(nc.psum_tensor(f"pair{i}", [P, 1024], F32)) for i in range(4)]

        raw_ready = [sem(f"raw_ready{i}") for i in range(RING)]
        cols_ready, consts_ready, x_ready = sem("cols_ready"), sem("consts_ready"), sem("x_ready")
        w_hi_ready, w_lo_ready = sem("w_hi_ready"), sem("w_lo_ready")
        unit_done, unit_evacuated = sem("unit_done"), sem("unit_evacuated")
        mod_done, mod_evacuated = sem("mod_done"), sem("mod_evacuated")
        h_hi_ready, h_lo_ready = sem("h_hi_ready"), sem("h_lo_ready")
        relu_ready, u_hi_ready, u_lo_ready = sem("relu_ready"), sem("u_hi_ready"), sem("u_lo_ready")
        dve_step, act_step = sem("dve_step"), sem("act_step")
        steps = {"dve": 0, "act": 0}

        def dve_link(ins):
            steps["dve"] += 1
            ins.then_inc(dve_step, 1)
            nc.vector.wait_ge(dve_step, steps["dve"])

        def act_link(ins):
            steps["act"] += 1
            ins.then_inc(act_step, 1)
            nc.scalar.wait_ge(act_step, steps["act"])

        def phase_w(phase):
            return sum(s[0] == "w" for s in phases[phase])

        def at(phase, j, i):
            n = first_slab[phase] + j
            per = len(phases[phase])
            kinds = [s[0] for s in phases[phase]]
            assert repeats[phase] == 1 or per % RING == 0
            w = first_w[phase] + kinds[:j].count("w") + i * kinds.count("w")
            m = first_m[phase] + kinds[:j].count("m") + i * kinds.count("m")
            return n % RING, 16 * (n // RING + 1) + 16 * (per // RING) * i, 2 * w, m

        units_before_norm = {1: 2 * first_w["mlp0"], 2: 2 * first_w["in1"], 3: 2 * first_w["mlp1"],
                             4: 2 * (first_w["mlp1"] + 8 * NFG)}

        def cuts(t_from):
            return ((t_from, 512 - t_from), (512, T - 512))

        def units_of(item):
            return 1 if item[1:] == ("in", 6) else 2

        def spans(layer, item, half):
            if layer == 1 and not (item[1] == "in" and (item[2], half) in CTX_UNITS):
                return [(CTX, LAT, 0)]
            return [(0, 512, 0), (512, 256, 512)]

        CTX_UNITS = {(0, 1), (1, 0), (1, 1), (3, 1), (4, 0), (4, 1), (6, 0), (9, 0), (9, 1)}
        TOKEN_MAJOR = {(1, 0), (1, 1), (4, 0), (4, 1), (9, 1)}

        block = ctx.enter_context(nc.Block())

        @block.sync
        def _(sp):
            sp.dma_start(cols[:], d["cols"]).then_inc(cols_ready, 16)

            def load(phase, j, i):
                item = phases[phase][j]
                slot, _, _, _ = at(phase, j, i)
                n = first_slab[phase] + j
                if n >= RING:
                    before = flat[:n - RING + 1]
                    per = len(phases[phase])
                    for r in range(1, repeats[phase]):
                        now, nxt = flat[:n + (r - 1) * per - RING + 1], flat[:n + r * per - RING + 1]
                        assert nxt.count("w") - now.count("w") == phase_w(phase), "slab pattern changes into the loop"
                    if repeats[phase] > 1:
                        later = flat[:n + len(phases[phase]) - RING + 1]
                        dw, dm = later.count("w") - before.count("w"), later.count("m") - before.count("m")
                    else:
                        dw = dm = 0
                    split_by, used_by = 2 * before.count("w") + 2 * dw * i, before.count("m") + dm * i
                layer = int(phase[-1]) if phase != "start" else 0
                dst = raw[:, slot].rearrange("p k c -> p (k c)")
                if item[0] == "m":
                    src = d["mod_w"][item[1], item[2] + (4 * i if phase == "mlp0" else 0)]
                elif item[1] == "in":
                    c0, wd = W_IN_SLABS[item[2]]
                    dst, src = dst[:, 0:KT * wd], d["w_in"][layer, :, KT * c0:KT * (c0 + wd)]
                elif item[1] == "out":
                    src = d["w_out"][layer, item[2]]
                else:
                    src = d["w_" + item[1]][layer * NFG + i, item[2]]
                if repeats[phase] > 1:
                    sp.compute_val(split_by)
                    if dm:
                        sp.compute_val(used_by)
                    sp.compute_val(src.offset * 4)
                if n >= RING:
                    if before.count("m"):
                        sp.wait_ge(mod_done, used_by)
                    if before.count("w"):
                        sp.wait_ge(w_lo_ready, split_by)
                sp.dma_start(dst, src).then_inc(raw_ready[slot], 16)

            for p in order:
                if repeats[p] > 1:
                    with sp.Fori(0, repeats[p]) as i:
                        for j in range(len(phases[p])):
                            load(p, j, i)
                else:
                    for j in range(len(phases[p])):
                        load(p, j, 0)
                        if p == "start" and j == 3:
                            sp.dma_start(xT[:], d["xT"]).then_inc(x_ready, 16)
                            sp.dma_start(squares[:], d["squares"]).then_inc(consts_ready, 16)
                            sp.dma_start(scan_mask[:], d["scan_mask"]).then_inc(consts_ready, 16)
                            sp.dma_start(gate_w[:], d["gate_w"]).then_inc(consts_ready, 16)
                            sp.dma_start(rope[:], d["rope"]).then_inc(consts_ready, 16)
            for k in range(KT):
                sp.wait_ge(sem("out_ready"), k + 1)
                sp.dma_start(d["out"][:, k, :], nout[:, k % 2, :]).then_inc(sem(f"out_stored{k % 2}"), 16)
            sp.wait_ge(sem("out_stored0"), 16 * KT // 2)
            sp.wait_ge(sem("out_stored1"), 16 * KT // 2)

        @block.tensor
        def _(pe):
            mm = nc.tensor.matmul

            def mod_slab(phase, j, i):
                slot, ready, _, m = at(phase, j, i)
                if phase == "start" and j == 0:
                    pe.wait_ge(sem("silu_c_ready"), 1)
                pe.wait_ge(raw_ready[slot], ready)
                if phase != "start" or j >= 2:
                    pe.wait_ge(mod_evacuated, m - 1)
                par = (first_m[phase] + [s[0] for s in phases[phase]][:j].count("m")) % 2
                for t in range(2):
                    o = pair[3][:, 512 * par + 2 * t:512 * par + 2 * t + 2]
                    for k in range(KT):
                        last = mm(o, raw[:, slot, k, t * P:(t + 1) * P], silu_c[:, k, :], start=(k == 0), stop=(k == KT - 1))
                last.then_inc(mod_done, 1)

            def unit(phase, j, i, half, first):
                item = phases[phase][j]
                layer = int(phase[-1])
                _, _, u, _ = at(phase, j, i)
                u = u + half
                pe.wait_ge(w_lo_ready, u + 1)
                if not (phase == "in0" and j == 0):
                    pe.wait_ge(unit_evacuated, u - 1)
                par = half
                out = pair[par]
                a_hi, a_lo = (u_hi, u_lo) if item[1] == "2" else (h_hi, h_lo)
                if item[1] == "in" and (item[2], half) in TOKEN_MAJOR:
                    for t in range(TT):
                        for k in range(KT):
                            for n, (a, w) in enumerate(((a_hi, w_hi), (a_hi, w_lo), (a_lo, w_hi))):
                                last = mm(out[:, t * P:(t + 1) * P], a[:, k, t * P:(t + 1) * P], w[:, par, k, :],
                                          start=(k == 0 and n == 0), stop=(k == KT - 1 and n == 2))
                    last.then_inc(unit_done, 1)
                    return
                m = 32 if units_of(item) == 1 else P
                for k in range(KT):
                    if first:
                        if item[1] == "2":
                            pe.wait_ge(u_lo_ready, (KT * NFG * layer + k + 1) + KT * i)
                        else:
                            nh = KT * h_count[phase] + k + 1
                            pe.wait_ge(h_lo_ready, nh)
                    for n, (w, a) in enumerate(((w_hi, a_hi), (w_hi, a_lo), (w_lo, a_hi))):
                        for t0, width, c0 in spans(layer, item, half):
                            last = mm(out[0:m, c0:c0 + width], w[:, par, k, 0:m], a[:, k, t0:t0 + width],
                                      start=(k == 0 and n == 0), stop=(k == KT - 1 and n == 2))
                last.then_inc(unit_done, 2 if units_of(item) == 1 else 1)

            h_count = {"in0": 0, "out0": 1, "mlp0": 2, "in1": 3, "out1": 4, "mlp1": 5}

            def products(phase, i=0):
                for j, item in enumerate(phases[phase]):
                    if item[0] == "m":
                        mod_slab(phase, j, i)
                    else:
                        for half in range(units_of(item)):
                            unit(phase, j, i, half, half == 0 and (item[2] == 0))

            def norm_sum(n):
                pe.wait_ge(sem("norm_sq_used"), KT * (n + 1))
                for t0, width in cuts(CTX if n >= 3 else 0):
                    last = mm(pair[2][:, t0:t0 + width], ones, nacc[:, t0:t0 + width], start=True, stop=True)
                last.then_inc(sem("norm_sum_ready"), 1)

            def scans(layer, ty):
                S = lambda name: sem(f"{name}_{layer}_{ty}")
                v = (ret_v, gla_v)[ty]
                first = 0 if layer == 0 else CTX // P
                if ty == 1:
                    pe.wait_ge(unit_evacuated, 2 * first_w[f"in{layer}"] + 20)
                    for dr in range(2):
                        if dr == 0:
                            pe.wait_ge(sem(f"y_done_{layer}_0"), 1)
                        for t0, width in ((0, 512), (512, 256)):
                            last = mm(pair[2 + dr][:, t0:t0 + width], gate_w[:, layer, dr, :], low[:, t0:t0 + width],
                                      start=True, stop=True)
                        last.then_inc(S("z_ready"), 1)
                for dr in range(2):
                    pe.wait_ge(S("k2_ready"), dr + 1)
                    for t in range(TT):
                        last = nc.tensor.transpose(pair[dr][:, t * P:(t + 1) * P], bcum[:, dr, t * P:(t + 1) * P], ident)
                    last.then_inc(S("k2T_in_psum"), 1)
                for dr in range(2):
                    pe.wait_ge(S(f"k2T_ready{dr}"), 1)
                    for c in range(NCH):
                        r0 = CH * (c % 2)
                        for h in range(4):
                            o = pair[2 + dr][32 * h:32 * h + 32, 512 * (c % 2) + DV * (c // 2):512 * (c % 2) + DV * (c // 2) + DV]
                            last = mm(o, k2T[r0:r0 + CH, dr, c // 2, 32 * h:32 * h + 32],
                                      v[r0:r0 + CH, c // 2, DV * h:DV * h + DV], start=True, stop=True,
                                      skip_group_check=True)
                    last.then_inc(S("kv_ready"), 1)
                rounds = [(t, hp) for t in range(first, TT) for hp in range(2)]

                def scores(r):
                    t, hp = rounds[r]
                    if r >= 2:
                        pe.wait_ge(S("probs_ready"), r - 1)
                    for h in (2 * hp, 2 * hp + 1):
                        rows = slice(32 * h, 32 * h + 32)
                        for dr in range(2):
                            c0 = 512 * (h % 2) + P * dr
                            last = mm(pair[hp][:, c0:c0 + P], k_dec[rows, dr, t * P:(t + 1) * P],
                                      q_dec[rows, dr, t * P:(t + 1) * P], start=True, stop=True, skip_group_check=True)
                    last.then_inc(S("scores_ready"), 1)

                def outputs(r):
                    t, hp = rounds[r]
                    pe.wait_ge(S("probs_ready"), r + 1)
                    opens = t == first or t == 4
                    for h in (2 * hp, 2 * hp + 1):
                        last = mm(pair[2 + hp][64 * (h % 2):64 * (h % 2) + 64, t * P:(t + 1) * P],
                                  v[:, t, DV * h:DV * h + DV], probs[:, r % 2, h % 2, :], start=opens, stop=False,
                                  skip_group_check=True)
                    last.then_inc(S("probs_used"), 1)
                    rows = slice(64 * hp, 64 * hp + 64)
                    for c in (2 * t, 2 * t + 1):
                        for dr in range(2):
                            if c == (0, CTX // CH - 1)[dr]:
                                continue
                            last = mm(pair[2 + hp][:, c * CH:(c + 1) * CH], s_diag[rows, dr, c, :],
                                      q_dec[rows, dr, c * CH:(c + 1) * CH], start=False, stop=True,
                                      skip_group_check=True)
                    if r == len(rounds) - 1:
                        last.then_inc(S("o_ready"), 1)

                pe.wait_ge(S("k2T_ready0"), 1)
                pe.wait_ge(S("k2T_ready1"), 1)
                scores(0)
                pe.wait_ge(S("s_diag_ready"), 8)
                for r in range(len(rounds)):
                    if r + 1 < len(rounds):
                        scores(r + 1)
                    outputs(r)
                for n in range(2 if ty == 0 else 1):
                    for hp in range(2):
                        pe.wait_ge(S("stat_in_ready"), 2 * n + hp + 1)
                        src = (g2, bcum)[n] if ty == 0 else bcum
                        for t0, width in cuts(CTX * layer):
                            last = mm(pair[hp][:, t0:t0 + width], blocks, src[:, hp, t0:t0 + width], start=True, stop=True)
                        last.then_inc(S("stat_ready"), 1)

            def attention(layer):
                S = lambda name: sem(f"{name}_{layer}")
                for n in range(5):
                    pe.wait_ge(S("qsq_ready"), n + 1)
                    if n >= 2:
                        pe.wait_ge(S("qrs_ready"), n - 1)
                    for t0, width in cuts(CTX * layer if n < 4 else 0):
                        last = mm(pair[n % 2][:, t0:t0 + width], blocks, qsq[:, n % 2, t0:t0 + width], start=True, stop=True)
                    last.then_inc(S("qsum_ready"), 1)
                pe.wait_ge(S("qrs_ready"), 5)
                pe.wait_ge(S("ak_ready"), 1)
                pe.wait_ge(S("k_dup_ready"), 1)
                items = [(t, h) for t in range(0 if layer == 0 else CTX // P, TT) for h in range(HQ)]

                def keys_of(t):
                    return CTX if t < CTX // P else T

                def score(n):
                    t, h = items[n]
                    if n >= 2:
                        pe.wait_ge(S("prow_ready"), n - 1)
                    rows = slice(HD * (h % 2), HD * (h % 2) + HD)
                    nk = keys_of(t)
                    for k0 in range(0, nk, 512):
                        width = min(512, nk - k0)
                        last = mm(pair[n % 2][:, k0:k0 + width], y[rows, 4 + h // 2, t * P:(t + 1) * P],
                                  k_dup[rows, h // 4, k0:k0 + width], start=True, stop=True)
                    last.then_inc(S("att_scores_ready"), 1)

                def turn(n):
                    t, h = items[n]
                    pe.wait_ge(S("prow_ready"), n + 1)
                    if n >= 1:
                        pe.wait_ge(S("pT_ready_a"), n)
                        pe.wait_ge(S("pT_ready_d"), n)
                    per = keys_of(t) // P // 2
                    for k in range(2 * per):
                        c0 = 512 * (k // per) + P * (k % per)
                        last = nc.tensor.transpose(pair[2][:, c0:c0 + P], prow[:, n % 2, k * P:(k + 1) * P], ident)
                    last.then_inc(S("pT_in_psum"), 1)

                def weigh(n):
                    t, h = items[n]
                    pe.wait_ge(S("pT_ready_a"), n + 1)
                    pe.wait_ge(S("pT_ready_d"), n + 1)
                    if h == 0 and n >= HQ:
                        pe.wait_ge(S("yq_ready"), n // HQ)
                    kt = keys_of(t) // P
                    for k in range(kt):
                        last = mm(pair[3][:, HD * h:HD * h + HD], pT[:, n % 2, k * P:(k + 1) * P],
                                  att_v[:, k, HD * (h // 4):HD * (h // 4) + HD], start=(k == 0), stop=(k == kt - 1))
                    last.then_inc(S("att_out_ready"), 1)

                def turn_back(b):
                    pe.wait_ge(S("yq_ready"), b + 1)
                    if b >= 1:
                        pe.wait_ge(S("y_att_ready"), b)
                    for g in range(4):
                        last = nc.tensor.transpose(pair[3][:, 512 + g * P:512 + (g + 1) * P], yq[:, b % 2, g * P:(g + 1) * P],
                                                   ident)
                    last.then_inc(S("yT_in_psum"), 1)

                score(0)
                for n in range(len(items)):
                    if n + 1 < len(items):
                        score(n + 1)
                    turn(n)
                    if n >= 1:
                        weigh(n - 1)
                    if n >= 2 and (n - 2) % HQ == HQ - 1:
                        turn_back((n - 2) // HQ)
                weigh(len(items) - 1)
                turn_back(len(items) // HQ - 1)

            products("start")
            pe.wait_ge(consts_ready, 64)
            norm_sum(0)
            for layer in range(DEPTH):
                products(f"in{layer}")
                pe.wait_ge(unit_evacuated, 2 * first_w[f"in{layer}"] + 20)
                if layer == 0:
                    pe.wait_ge(mod_evacuated, first_m["out0"])
                scans(layer, 0)
                scans(layer, 1)
                attention(layer)
                products(f"out{layer}")
                norm_sum(2 * layer + 1)
                with pe.Fori(0, NFG) as i:
                    products(f"mlp{layer}", i)
                norm_sum(2 * layer + 2)

        @block.scalar
        def _(act):
            F = nc.scalar.activation

            def split_hi(phase, j, i, half):
                item = phases[phase][j]
                slot, ready, u, _ = at(phase, j, i)
                u = u + half
                act.wait_ge(raw_ready[slot], ready)
                if not (phase == "in0" and j == 0):
                    act.wait_ge(unit_done, u - 1)
                if units_of(item) == 1:
                    src = raw[:, slot].rearrange("p k c -> p (k c)")[:, 0:KT * 32].rearrange("p (k c) -> p k c", k=KT)
                    F(w_hi[:, 0, :, 0:32], src, ACT.Copy).then_inc(w_hi_ready, 2)
                else:
                    F(w_hi[:, half], raw[:, slot, :, half * P:(half + 1) * P], ACT.Copy).then_inc(w_hi_ready, 1)

            def run(phase, i=0):
                ul = [(j, half) for j, item in enumerate(phases[phase]) if item[0] == "w" for half in range(units_of(item))]
                layer = int(phase[-1])
                t_from = 0 if layer == 0 else CTX
                split_hi(phase, *ul[0][:1], i, 0)
                for n, (j, half) in enumerate(ul):
                    if n + 1 < len(ul):
                        split_hi(phase, ul[n + 1][0], i, ul[n + 1][1])
                    item = phases[phase][j]
                    if item[1] == "1":
                        m = 2 * item[2] + half
                        cnt = (KT * NFG * layer + m + 1) + KT * i
                        _, _, u, _ = at(phase, j, i)
                        act.wait_ge(unit_done, u + half + 1)
                        full = u_full[:, half, t_from:]
                        if not (layer == 0 and m < 2):
                            act.wait_ge(u_lo_ready, cnt - 2)
                        F(full, pair[half][:, 0:T - t_from], ACT.Relu).then_inc(relu_ready, 1)
                        act.wait_ge(unit_evacuated, u + half + 1)
                        F(u_hi[:, m, t_from:], full, ACT.Copy).then_inc(u_hi_ready, 1)

            def norm(n, lat_only, final=False):
                t_from = CTX if lat_only else 0
                for k in range(KT):
                    if n == 0:
                        if k == 0:
                            act.wait_ge(x_ready, 16)
                    else:
                        act.wait_ge(unit_evacuated, units_before_norm[n] - KT + k + 1)
                    if k >= 2:
                        act.wait_ge(sem("norm_sq_used"), KT * n + k - 1)
                    F(nsq[:, k % 2, t_from:], xT[:, k, t_from:], ACT.Square).then_inc(sem("norm_sq_ready"), 1)
                act.wait_ge(sem("norm_sum_ready"), n + 1)
                act_link(F(nrs[:, t_from:], pair[2][:, t_from:T], ACT.Ln, bias=EPS, scale=1.0 / D))
                F(nrs[:, t_from:], nrs[:, t_from:], ACT.Exp, scale=-0.5).then_inc(sem("norm_rs_ready"), 1)
                if final:
                    return
                l, sh = n // 2, (SH_A, SH_M)[n % 2]
                for k in range(KT):
                    act.wait_ge(sem("norm_t_ready"), KT * n + k + 1)
                    for t0, t1, s in ([] if lat_only else [(0, CTX, 1)]) + [(CTX, T, 0)]:
                        last = F(h_hi[:, k, t0:t1], nsq[:, k % 2, t0:t1], ACT.Identity, bias=modv[:, l, sh + k, s:s + 1])
                    last.then_inc(h_hi_ready, 1)

            def scans(layer, ty):
                S = lambda name: sem(f"{name}_{layer}_{ty}")
                t_from = 0 if layer == 0 else CTX
                if ty == 1:
                    for dr in range(2):
                        act.wait_ge(S("negabs_ready"), dr + 1)
                        act_link(F(bcum[:, dr], bcum[:, dr], ACT.Exp))
                        F(bcum[:, dr], bcum[:, dr], ACT.Ln, bias=1.0).then_inc(S("softplus_ready"), 1)
                s = 1.0 if ty == 0 else 1.0 / TAU
                for dr in range(2):
                    act.wait_ge(S("bcum_ready"), dr + 1)
                    F(q_dec[:, dr], bcum[:, dr], ACT.Exp, scale=s).then_inc(S("decays_ready"), 1)
                    F(k_dec[:, dr], bcum[:, dr], ACT.Exp, scale=-s).then_inc(S("decays_ready"), 1)
                act.wait_ge(S("k2T_in_psum"), 2)
                F(k2T[:, 1].rearrange("p t c -> p (t c)"), pair[1][:, 0:T], ACT.Copy).then_inc(S("k2T_ready1"), 1)
                for hp in range(2):
                    act.wait_ge(S("s_diag_ready"), 8)
                    F(state[:, hp].rearrange("p c e -> p (c e)")[:, t_from:], y[:, 2 * ty + hp, t_from:], ACT.Exp,
                      scale=-1.0).then_inc(S("gate_exp_ready"), 1)
                act.wait_ge(S("o_ready"), 1)
                for hp in range(2):
                    if ty == 0:
                        F(g2[:, hp, t_from:], pair[2 + hp][:, t_from:T], ACT.Copy).then_inc(S("stat_in_ready"), 1)
                    else:
                        F(bcum[:, hp, t_from:], pair[2 + hp][:, t_from:T], ACT.Square).then_inc(S("stat_in_ready"), 1)
                if ty == 0:
                    for hp in range(2):
                        act.wait_ge(S("centred_ready"), hp + 1)
                        F(bcum[:, hp, t_from:], g2[:, hp, t_from:], ACT.Square).then_inc(S("stat_in_ready"), 1)
                base = 2 if ty == 0 else 0
                for hp in range(2):
                    act.wait_ge(S("stat_ready"), base + hp + 1)
                    act_link(F(q_dec[:, hp, t_from:], pair[hp][:, t_from:T], ACT.Ln, bias=EPS))
                    F(q_dec[:, hp, t_from:], q_dec[:, hp, t_from:], ACT.Exp, scale=-0.5).then_inc(S("head_rs_ready"), 1)

            def attention(layer):
                S = lambda name: sem(f"{name}_{layer}")
                act.wait_ge(sem(f"y_done_{layer}_1"), 1)
                for n in range(5):
                    src = y[:, 4 + n, CTX * layer:] if n < 4 else att_k[:]
                    if n >= 2:
                        act.wait_ge(S("qsum_ready"), n - 1)
                    F(qsq[:, n % 2, CTX * layer if n < 4 else 0:], src, ACT.Square).then_inc(S("qsq_ready"), 1)
                    if n >= 1:
                        root(S, n - 1, CTX * layer)
                root(S, 4, 0)
                act.wait_ge(S("ak_ready"), 1)
                for kv in range(2):
                    for half in range(2):
                        last = F(k_dup[64 * half:64 * half + 64, kv], att_k[64 * kv:64 * kv + 64], ACT.Copy)
                last.then_inc(S("k_dup_ready"), 1)
                items = [(t, h) for t in range(0 if layer == 0 else CTX // P, TT) for h in range(HQ)]

                def copy_pT(n):
                    nk = CTX if items[n][0] < CTX // P else T
                    act.wait_ge(S("pT_in_psum"), n + 1)
                    F(pT[:, n % 2, nk // 2:nk], pair[2][:, 512:512 + nk // 2], ACT.Copy).then_inc(S("pT_ready_a"), 1)

                for n, (t, h) in enumerate(items):
                    nk = CTX if t < CTX // P else T
                    act.wait_ge(S("negmax_ready"), n + 1)
                    if n >= 2:
                        act.wait_ge(S("pT_in_psum"), n - 1)
                    F(prow[:, n % 2, 0:nk], pair[n % 2][:, 0:nk], ACT.Exp, bias=small[:, 16 + n % 2:17 + n % 2],
                      scale=HD ** -0.5, accum_out=small[:, 32 + n % 16:33 + n % 16]).then_inc(S("prow_ready"), 1)
                    if n >= 1:
                        copy_pT(n - 1)
                copy_pT(len(items) - 1)

            def root(S, n, t_from):
                act.wait_ge(S("qsum_ready"), n + 1)
                if n >= 2:
                    act.wait_ge(S("qrs_used"), n - 1)
                act_link(F(qrs[:, n % 2, t_from:], pair[n % 2][:, t_from:T], ACT.Ln, bias=EPS))
                F(qrs[:, n % 2, t_from:], qrs[:, n % 2, t_from:], ACT.Exp, scale=-0.5).then_inc(S("qrs_ready"), 1)

            def split_y(layer):
                t_from = 0 if layer == 0 else CTX
                act.wait_ge(sem(f"y_att_ready_{layer}"), (TT, LAT // P)[layer])
                for k in range(KT):
                    F(h_hi[:, k, t_from:], y[:, k, t_from:], ACT.Copy).then_inc(h_hi_ready, 1)

            act.wait_ge(sem("ln_first"), 1)
            act_link(F(lgam[:, :, :], small[:, 0:4].rearrange("p (l d) -> p l d", l=2), ACT.Exp))
            F(lgam[:, :, :], lgam[:, :, :], ACT.Ln, bias=1.0).then_inc(sem("lgam_softplus"), 1)
            F(silu_c[:], cols[:, 0:16].rearrange("p (k s) -> p k s", s=2), ACT.Exp, scale=-1.0).then_inc(sem("exp_c_ready"), 1)
            norm(0, False)
            for layer in range(DEPTH):
                run(f"in{layer}")
                scans(layer, 0)
                scans(layer, 1)
                attention(layer)
                split_y(layer)
                run(f"out{layer}")
                norm(2 * layer + 1, layer == 1)
                with act.Fori(0, NFG) as i:
                    run(f"mlp{layer}", i)
                norm(2 * layer + 2, layer == 1, final=(layer == 1))

        @block.vector
        def _(dve):
            V = nc.vector
            shuffles = {w: [(p // (2 * w)) * 2 * w + (p % (2 * w) + w) % (2 * w) for p in range(32)] for w in (8, 16)}

            def split_lo(phase, j, i, half):
                item = phases[phase][j]
                slot, ready, u, _ = at(phase, j, i)
                u = u + half
                dve.wait_ge(raw_ready[slot], ready)
                if units_of(item) == 1:
                    dve.wait_ge(w_hi_ready, u + 2)
                    src = raw[:, slot].rearrange("p k c -> p (k c)")[:, 0:KT * 32].rearrange("p (k c) -> p k c", k=KT)
                    V.tensor_tensor(w_lo[:, 0, :, 0:32], src, w_hi[:, 0, :, 0:32].bitcast(F32),
                                    ALU.subtract).then_inc(w_lo_ready, 2)
                else:
                    dve.wait_ge(w_hi_ready, u + 1)
                    V.tensor_tensor(w_lo[:, half], raw[:, slot, :, half * P:(half + 1) * P], w_hi[:, half].bitcast(F32),
                                    ALU.subtract).then_inc(w_lo_ready, 1)

            def in_target(s, half):
                if s in (1, 4):
                    return (ret_v if s == 1 else gla_v)[:, :, half * P:(half + 1) * P]
                if s == 9:
                    return att_k[:] if half == 0 else att_v[:]
                if s in (2, 5):
                    return y[:, (0 if s == 2 else 2) + half]
                if s in (7, 8):
                    return y[:, 4 + 2 * (s - 7) + half]
                return {0: (ret_q, ret_k), 3: (gla_q, gla_k)}[s][half][:]

            def evacuate(phase, j, i, half):
                item = phases[phase][j]
                layer = int(phase[-1])
                _, _, u, _ = at(phase, j, i)
                u = u + half
                ps = pair[half]
                sp = spans(layer, item, half)
                lat = len(sp) == 1
                if item[1] == "in":
                    if units_of(item) == 1:
                        dve.wait_ge(unit_done, u + 2)
                        V.tensor_copy(low[:], ps[0:32, 0:T]).then_inc(unit_evacuated, 2)
                        return
                    dve.wait_ge(unit_done, u + 1)
                    dst = in_target(item[2], half)
                    if (item[2], half) in TOKEN_MAJOR:
                        V.tensor_copy(dst, ps[:, 0:T].rearrange("p (t c) -> p t c", t=TT)).then_inc(unit_evacuated, 1)
                    elif lat:
                        V.tensor_copy(dst[:, CTX:T], ps[:, 0:LAT]).then_inc(unit_evacuated, 1)
                    else:
                        V.tensor_copy(dst, ps[:, 0:T]).then_inc(unit_evacuated, 1)
                    return
                m = 2 * item[2] + half
                dve.wait_ge(unit_done, u + 1)
                t_from = CTX if lat else 0
                if item[1] == "1":
                    cnt = (KT * NFG * layer + m + 1) + KT * i
                    dve.wait_ge(relu_ready, cnt)
                    full = u_full[:, half, t_from:]
                    V.tensor_tensor(full, full, ps[:, 0:T - t_from], ALU.mult).then_inc(unit_evacuated, 1)
                    dve.wait_ge(u_hi_ready, cnt)
                    V.tensor_tensor(u_lo[:, m, t_from:], full, u_hi[:, m, t_from:].bitcast(F32),
                                    ALU.subtract).then_inc(u_lo_ready, 1)
                    return
                gt = (GT_A if item[1] == "out" else GT_M) + m
                for t0, t1, s in ([] if lat else [(0, CTX, 1)]) + [(CTX, T, 0)]:
                    c0 = t0 - t_from
                    last = V.scalar_tensor_tensor(out=xT[:, m, t0:t1], in0=ps[:, c0:c0 + t1 - t0],
                                                  scalar=modv[:, layer, gt, s:s + 1], in1=xT[:, m, t0:t1],
                                                  op0=ALU.mult, op1=ALU.add)
                last.then_inc(unit_evacuated, 1)

            def evacuate_mod(phase, j, i):
                item = phases[phase][j]
                _, _, _, m = at(phase, j, i)
                par = (first_m[phase] + [s[0] for s in phases[phase]][:j].count("m")) % 2
                dve.wait_ge(mod_done, m + 1)
                l = item[1]
                ps = pair[3][:, 512 * par:512 * par + 4].rearrange("p (t s) -> p t s", s=2)
                base = COLS_L + L_N * l + L_MODB
                n = item[2] + (4 * i if phase == "mlp0" else 0)
                if phase == "mlp0":
                    out = modv[:, l].rearrange("p (n t) s -> p n (t s)", t=2)[:, bass.ds(n, 1), :].rearrange("p n (t s) -> p (n t) s", s=2)
                    bias = cols[:, base:base + N_MOD].rearrange("p (n t) -> p n t", t=2)[:, bass.ds(n, 1), :]
                    bias = bias.rearrange("p n (t s) -> p (n t) s", s=1)
                else:
                    out = modv[:, l, 2 * n:2 * n + 2, :]
                    bias = cols[:, base + 2 * n:base + 2 * n + 2].rearrange("p (t s) -> p t s", s=1)
                V.tensor_tensor(out, ps, bias.to_broadcast([P, 2, 2]), ALU.add).then_inc(mod_evacuated, 1)

            def run(phase, i=0):
                items = phases[phase]
                seq = []
                for j, item in enumerate(items):
                    seq += [("m", j, 0)] if item[0] == "m" else [("w", j, h) for h in range(units_of(item))]
                ul = [s for s in seq if s[0] == "w"]
                if ul:
                    split_lo(phase, ul[0][1], i, 0)
                for n, (kind, j, half) in enumerate(seq):
                    if n + 1 < len(seq) and seq[n + 1][0] == "w":
                        split_lo(phase, seq[n + 1][1], i, seq[n + 1][2])
                    if kind == "w":
                        evacuate(phase, j, i, half)
                    else:
                        evacuate_mod(phase, j, i)

            def norm(n, lat_only, final=False):
                t_from = CTX if lat_only else 0
                rows = slice(t_from, T)
                l, sc = n // 2, (SC_A, SC_M)[n % 2]
                if not final:
                    g = cols[:, COLS_L + L_N * l + (L_AG, L_MG)[n % 2]:][:, 0:KT].rearrange("p (k s) -> p k s", s=1)
                    dve.wait_ge(mod_evacuated, {0: 8, 1: 24, 2: 48, 3: 48}[n])
                    dve_link(V.scalar_tensor_tensor(out=gain[:], in0=modv[:, l, sc:sc + KT, :], scalar=1.0,
                                                    in1=g.to_broadcast([P, KT, 2]), op0=ALU.add, op1=ALU.mult))
                for k in range(1, KT):
                    dve.wait_ge(sem("norm_sq_ready"), KT * n + k + 1)
                    a = nsq[:, 0, rows] if k == 1 else nacc[:, rows]
                    ins = V.tensor_tensor(nacc[:, rows], a, nsq[:, k % 2, rows], ALU.add)
                    ins.then_inc(sem("norm_sq_used"), 2 if k == 1 else 1)
                    dve.wait_ge(sem("norm_sq_used"), KT * n + k + 1)
                dve.wait_ge(sem("norm_rs_ready"), n + 1)
                for k in range(KT):
                    if final:
                        if k >= 2:
                            dve.wait_ge(sem(f"out_stored{k % 2}"), 16 * (k // 2))
                        V.scalar_tensor_tensor(out=nout[:, k % 2, :], in0=xT[:, k, CTX:T],
                                               scalar=cols[:, COLS_FG + k:COLS_FG + k + 1], in1=nrs[:, CTX:T],
                                               op0=ALU.mult, op1=ALU.mult).then_inc(sem("out_ready"), 1)
                        continue
                    segs = ([] if lat_only else [(0, CTX, 1)]) + [(CTX, T, 0)]
                    if k >= 2:
                        dve.wait_ge(h_lo_ready, h_base[n] + k - 1)
                    for t0, t1, s in segs:
                        last = V.scalar_tensor_tensor(out=nsq[:, k % 2, t0:t1], in0=xT[:, k, t0:t1],
                                                      scalar=gain[:, k, s:s + 1], in1=nrs[:, t0:t1],
                                                      op0=ALU.mult, op1=ALU.mult)
                    last.then_inc(sem("norm_t_ready"), 1)
                    if k >= 1:
                        low_part(n, k - 1, segs)
                if not final:
                    low_part(n, KT - 1, segs)

            def low_part(n, k, segs):
                l, sh = n // 2, (SH_A, SH_M)[n % 2]
                dve.wait_ge(h_hi_ready, h_base[n] + k + 1)
                for t0, t1, s in segs:
                    last = V.scalar_tensor_tensor(out=h_lo[:, k, t0:t1], in0=nsq[:, k % 2, t0:t1],
                                                  scalar=modv[:, l, sh + k, s:s + 1], in1=h_hi[:, k, t0:t1].bitcast(F32),
                                                  op0=ALU.add, op1=ALU.subtract)
                last.then_inc(h_lo_ready, 1)

            h_base = {0: 0, 1: 16, 2: 24, 3: 40}

            def rotate(x, table, width, done=None):
                lat = x[:, CTX:T]
                dve_link(V.stream_shuffle(rope_sw[:], lat, shuffles[width]))
                dve_link(V.tensor_tensor(rope_t[:], lat, rope[:, table, :], ALU.mult))
                dve_link(V.tensor_tensor(rope_sw[:], rope_sw[:], rope[:, table + 1, :], ALU.mult))
                last = V.tensor_tensor(lat, rope_t[:], rope_sw[:], ALU.add)
                if done is None:
                    dve_link(last)
                else:
                    last.then_inc(done, 1)

            def scans(layer, ty):
                S = lambda name: sem(f"{name}_{layer}_{ty}")
                t_from = 0 if layer == 0 else CTX
                q, k = ((ret_q, ret_k), (gla_q, gla_k))[ty]
                if ty == 0:
                    rotate(q, 0, 8)
                    rotate(k, 0, 8)
                    for dr in range(2):
                        dve_link(V.tensor_copy(g2[:, dr], lgam[:, layer, dr:dr + 1].to_broadcast([P, T])))
                else:
                    gb = COLS_L + L_N * layer + L_GB
                    for dr in range(2):
                        dve.wait_ge(S("z_ready"), dr + 1)
                        dve_link(V.tensor_scalar(g2[:, dr], pair[2 + dr][:, 0:T], cols[:, gb + dr:gb + dr + 1], None, ALU.add))
                        V.scalar_tensor_tensor(out=bcum[:, dr], in0=g2[:, dr], scalar=-1.0, in1=g2[:, dr], op0=ALU.mult,
                                               op1=ALU.min).then_inc(S("negabs_ready"), 1)
                    for dr in range(2):
                        dve.wait_ge(S("softplus_ready"), dr + 1)
                        dve_link(V.scalar_tensor_tensor(out=g2[:, dr], in0=g2[:, dr], scalar=0.0, in1=bcum[:, dr],
                                                        op0=ALU.min, op1=ALU.subtract))
                V.tensor_tensor_scan(bcum[:, 0], scan_mask[:], g2[:, 0], 0.0, ALU.mult, ALU.add).then_inc(S("bcum_ready"), 1)
                V.tensor_tensor_scan(bcum[:, 1, ::-1], scan_mask[:], g2[:, 1, ::-1], 0.0, ALU.mult,
                                     ALU.add).then_inc(S("bcum_ready"), 1)
                qs, ks = ((1.0, KSCALE), (KSCALE, 1.0))[ty]
                for dr in range(2):
                    dve.wait_ge(S("decays_ready"), 2 * dr + 2)
                    whole = (CH - 1, 0)[dr]
                    dve_link(V.tensor_copy(decs[:, dr, :], q_dec[:, dr].rearrange("p (c i) -> p c i", i=CH)[:, :, whole]))
                    V.scalar_tensor_tensor(out=q_dec[:, dr, t_from:], in0=q[:, t_from:], scalar=qs, in1=q_dec[:, dr, t_from:],
                                           op0=ALU.mult, op1=ALU.mult)
                    dve_link(V.scalar_tensor_tensor(out=k_dec[:, dr], in0=k[:], scalar=ks, in1=k_dec[:, dr],
                                                    op0=ALU.mult, op1=ALU.mult))
                    V.tensor_tensor(bcum[:, dr].rearrange("p (c i) -> p c i", i=CH),
                                    k_dec[:, dr].rearrange("p (c i) -> p c i", i=CH),
                                    decs[:, dr, :].rearrange("p (c i) -> p c i", i=1).to_broadcast([P, NCH, CH]),
                                    ALU.mult).then_inc(S("k2_ready"), 1)
                dve.wait_ge(S("k2T_in_psum"), 1)
                V.tensor_copy(k2T[:, 0].rearrange("p t c -> p (t c)"), pair[0][:, 0:T]).then_inc(S("k2T_ready0"), 1)
                for dr in range(2):
                    dve.wait_ge(S("kv_ready"), dr + 1)
                    path = list(range(NCH)) if dr == 0 else [3, 2, 1, 0] + list(range(NCH - 1, 3, -1))
                    dve_link(V.memset(state[:, dr, path[0], :], 0.0))
                    for a, b in zip(path, path[1:]):
                        kv = pair[2 + dr][:, 512 * (a % 2) + DV * (a // 2):512 * (a % 2) + DV * (a // 2) + DV]
                        ins = V.scalar_tensor_tensor(out=state[:, dr, b, :], in0=state[:, dr, a, :],
                                                     scalar=decs[:, dr, a:a + 1], in1=kv, op0=ALU.mult, op1=ALU.add)
                        if b == path[-1]:
                            ins.then_inc(S("state_ready"), 1)
                        else:
                            dve_link(ins)
                rounds = 2 * (T - t_from) // P
                for r in range(rounds):
                    dve.wait_ge(S("scores_ready"), r + 1)
                    for dr in range(2):
                        src = pair[r % 2][:, :].rearrange("p (b c) -> p b c", b=2)[:, :, P * dr:P * dr + P]
                        msk = (mask_f, mask_b)[dr].rearrange("p (b c) -> p b c", b=1).to_broadcast([P, 2, P])
                        last = V.tensor_tensor(ptmp[:, dr], src, msk, ALU.mult)
                    dve_link(last)
                    if r >= 2:
                        dve.wait_ge(S("probs_used"), r - 1)
                    V.tensor_tensor(probs[:, r % 2], ptmp[:, 0], ptmp[:, 1], ALU.add).then_inc(S("probs_ready"), 1)
                    dve.wait_ge(S("probs_ready"), r + 1)
                rows = slice(t_from, T)
                for hp in range(2):
                    e = state[:, hp].rearrange("p c e -> p (c e)")[:, rows]
                    gt = y[:, 2 * ty + hp, rows]
                    dve.wait_ge(S("gate_exp_ready"), hp + 1)
                    dve_link(V.tensor_scalar(e, e, 1.0, None, ALU.add))
                    dve_link(V.reciprocal(e, e))
                    dve_link(V.tensor_tensor(gt, gt, e, ALU.mult))
                if ty == 0:
                    for hp in range(2):
                        dve.wait_ge(S("stat_ready"), hp + 1)
                        V.tensor_tensor(g2[:, hp, rows], g2[:, hp, rows], pair[hp][:, rows],
                                        ALU.subtract).then_inc(S("centred_ready"), 1)
                for hp in range(2):
                    gt = y[:, 2 * ty + hp, rows]
                    dve.wait_ge(S("head_rs_ready"), hp + 1)
                    dve_link(V.tensor_tensor(gt, gt, q_dec[:, hp, rows], ALU.mult))
                    o = g2[:, hp, rows] if ty == 0 else pair[2 + hp][:, rows]
                    last = V.tensor_tensor(gt, gt, o, ALU.mult)
                last.then_inc(sem(f"y_done_{layer}_{ty}"), 1)
                dve.wait_ge(sem(f"y_done_{layer}_{ty}"), 1)

            def attention(layer):
                S = lambda name: sem(f"{name}_{layer}")
                for n in range(5):
                    x = y[:, 4 + n] if n < 4 else att_k[:]
                    gc = COLS_L + L_N * layer + (L_QG if n < 4 else L_KG)
                    dve.wait_ge(S("qrs_ready"), n + 1)
                    t0 = CTX * layer if n < 4 else 0
                    ins = V.scalar_tensor_tensor(out=x[:, t0:], in0=x[:, t0:], scalar=cols[:, gc:gc + 1],
                                                 in1=qrs[:, n % 2, t0:], op0=ALU.mult, op1=ALU.mult)
                    ins.then_inc(S("qrs_used"), 1)
                    dve.wait_ge(S("qrs_used"), n + 1)
                    rotate(x, 2, 16, S("ak_ready") if n == 4 else None)
                items = [(t, h) for t in range(0 if layer == 0 else CTX // P, TT) for h in range(HQ)]

                def copy_pT(n):
                    nk = CTX if items[n][0] < CTX // P else T
                    dve.wait_ge(S("pT_in_psum"), n + 1)
                    V.tensor_copy(pT[:, n % 2, 0:nk // 2], pair[2][:, 0:nk // 2]).then_inc(S("pT_ready_d"), 1)

                def take_out(b):
                    dve.wait_ge(S("att_out_ready"), HQ * (b + 1))
                    dve.wait_ge(S("prow_ready"), HQ * (b + 1))
                    r = small[:, 32 + 8 * (b % 2):40 + 8 * (b % 2)]
                    dve_link(V.reciprocal(small[:, 48:56], r))
                    V.tensor_tensor(yq[:, b % 2].rearrange("p (h e) -> p h e", h=HQ),
                                    pair[3][:, 0:512].rearrange("p (h e) -> p h e", h=HQ),
                                    small[:, 48:56].rearrange("p (h e) -> p h e", e=1).to_broadcast([P, HQ, HD]),
                                    ALU.mult).then_inc(S("yq_ready"), 1)
                    dve.wait_ge(S("yq_ready"), b + 1)

                def put_back(b):
                    t = items[HQ * b][0]
                    dve.wait_ge(S("yT_in_psum"), b + 1)
                    V.tensor_copy(y[:, 4:8, t * P:(t + 1) * P],
                                  pair[3][:, 512:1024].rearrange("p (g c) -> p g c", g=4)).then_inc(S("y_att_ready"), 1)

                for n, (t, h) in enumerate(items):
                    nk = CTX if t < CTX // P else T
                    dve.wait_ge(S("att_scores_ready"), n + 1)
                    if n >= 2:
                        dve.wait_ge(S("prow_ready"), n - 1)
                    dve_link(V.tensor_reduce(small[:, 18 + n % 2:19 + n % 2], pair[n % 2][:, 0:nk], AX.X, ALU.max))
                    V.tensor_scalar(small[:, 16 + n % 2:17 + n % 2], small[:, 18 + n % 2:19 + n % 2], -(HD ** -0.5), None,
                                    ALU.mult).then_inc(S("negmax_ready"), 1)
                    if n >= 1:
                        copy_pT(n - 1)
                    if n >= 2 and (n - 2) % HQ == HQ - 1:
                        take_out((n - 2) // HQ)
                    if n >= 4 and (n - 4) % HQ == HQ - 1:
                        put_back((n - 4) // HQ)
                last_n = len(items) - 1
                copy_pT(last_n)
                take_out(last_n // HQ)
                put_back(last_n // HQ)
                dve.wait_ge(S("y_att_ready"), last_n // HQ + 1)

            def split_y(layer):
                t_from = 0 if layer == 0 else CTX
                for k in range(KT):
                    dve.wait_ge(h_hi_ready, (8, 32)[layer] + k + 1)
                    V.tensor_tensor(h_lo[:, k, t_from:], y[:, k, t_from:], h_hi[:, k, t_from:].bitcast(F32),
                                    ALU.subtract).then_inc(h_lo_ready, 1)

            V.memset(small[:], 0.0).then_inc(sem("small_clear"), 1)
            dve.wait_ge(sem("small_clear"), 1)
            dve.wait_ge(cols_ready, 16)
            for l in range(DEPTH):
                rd = COLS_L + L_N * l + L_RD
                last = V.scalar_tensor_tensor(out=small[:, 2 * l:2 * l + 2], in0=cols[:, rd:rd + 2], scalar=-1.0,
                                              in1=cols[:, rd:rd + 2], op0=ALU.mult, op1=ALU.min)
            last.then_inc(sem("ln_first"), 1)
            dve.wait_ge(sem("exp_c_ready"), 1)
            dve_link(V.tensor_scalar(silu_c[:], silu_c[:], 1.0, None, ALU.add))
            dve_link(V.reciprocal(silu_c[:], silu_c[:]))
            V.tensor_tensor(silu_c[:], silu_c[:], cols[:, 0:16].rearrange("p (k s) -> p k s", s=2),
                            ALU.mult).then_inc(sem("silu_c_ready"), 1)
            dve.wait_ge(sem("lgam_softplus"), 1)
            for l in range(DEPTH):
                rd = COLS_L + L_N * l + L_RD
                dve_link(V.scalar_tensor_tensor(out=lgam[:, l, :], in0=cols[:, rd:rd + 2], scalar=0.0, in1=lgam[:, l, :],
                                                op0=ALU.min, op1=ALU.subtract))
            run("start")
            norm(0, False)
            dve.wait_ge(consts_ready, 64)
            for layer in range(DEPTH):
                run(f"in{layer}")
                dve.wait_ge(unit_evacuated, 2 * first_w[f"in{layer}"] + 20)
                scans(layer, 0)
                scans(layer, 1)
                attention(layer)
                split_y(layer)
                dve.wait_ge(mod_evacuated, (24, 48)[layer])
                run(f"out{layer}")
                norm(2 * layer + 1, layer == 1)
                with dve.Fori(0, NFG) as i:
                    run(f"mlp{layer}", i)
                norm(2 * layer + 2, layer == 1, final=(layer == 1))

        @block.gpsimd
        def _(pool):
            for layer in range(DEPTH):
                pool.wait_ge(h_lo_ready, (KT, 4 * KT)[layer])
                nc.gpsimd.memset(s_diag[:], 0.0).then_inc(sem("s_diag_clear"), 1)
                pool.wait_ge(sem("s_diag_clear"), layer + 1)
                for ty in range(2):
                    for dr in range(2):
                        pool.wait_ge(sem(f"state_ready_{layer}_{ty}"), dr + 1)
                        for h in range(4):
                            rows = slice(32 * h, 32 * h + 32)
                            nc.gpsimd.tensor_copy(s_diag[rows, dr, :, DV * (h % 2):DV * (h % 2) + DV],
                                                  state[rows, dr]).then_inc(sem(f"s_diag_ready_{layer}_{ty}"), 1)


def kernel(**inputs):
    import numpy as np
    import concourse.bacc as bacc
    from concourse import mybir
    from concourse.bass_utils import run_bass_kernel_spmd as run

    a = {k: np.asarray(v) for k, v in inputs.items()}
    f = np.float32

    def tiles(m):
        return np.ascontiguousarray(m.reshape(KT, P, -1).transpose(1, 0, 2))

    def slabs(w, groups):
        lead, cols = w.shape[:-2], w.shape[-1]
        w = w.reshape(lead + (groups, KT, P, cols // SLAB, SLAB))
        n = len(lead)
        w = w.transpose(tuple(range(n + 1)) + (n + 3, n + 2, n + 1, n + 4))
        return np.ascontiguousarray(w).reshape(lead + (groups, cols // SLAB, P, KT * SLAB))

    arrays = {}
    arrays["xT"] = tiles(np.concatenate([a["ctx"][0], a["x"][0]], axis=0).T)
    arrays["mod_w"] = slabs(a["mod_w"], 1)[:, 0]
    arrays["w_out"] = slabs(a["w_out"], 1)[:, 0]
    w1 = a["mlp_w1"].reshape(DEPTH, D, NFG, D).transpose(0, 2, 1, 3)
    arrays["w_1"] = slabs(w1, 1)[:, :, 0].reshape(DEPTH * NFG, 4, P, KT * SLAB)
    arrays["w_2"] = slabs(a["mlp_w2"], NFG).reshape(DEPTH * NFG, 4, P, KT * SLAB)
    win = a["w_in"].reshape(DEPTH, KT, P, W_IN).transpose(0, 2, 1, 3)
    arrays["w_in"] = np.concatenate([win[..., c:c + w].reshape(DEPTH, P, KT * w) for c, w in W_IN_SLABS], axis=2)

    def col(v):
        return v.reshape(-1, P).T
    parts = [np.stack([col(a["c"][0]), col(a["c_ctx"])], axis=2).reshape(P, 2 * KT), col(a["final_norm_g"])]
    for l in range(DEPTH):
        parts += [col(a["mod_b"][l]), col(a["attn_norm_g"][l]), col(a["mlp_norm_g"][l]),
                  np.tile(a["qk_norm_g"][l, 0], 2)[:, None], np.tile(a["qk_norm_g"][l, 1], 2)[:, None],
                  a["gla_gate_b"][l].T, np.repeat(a["ret_decay_logit"][l].T, DK, axis=0)]
    arrays["cols"] = np.ascontiguousarray(np.concatenate(parts, axis=1))
    gw = np.zeros((32, DEPTH, 2, P), f)
    gw[0:16, :, 0] = a["gla_gate_w"][:, 0].transpose(1, 0, 2)
    gw[16:32, :, 1] = a["gla_gate_w"][:, 1].transpose(1, 0, 2)
    arrays["gate_w"] = gw

    tok = np.arange(LAT)
    row, column = (tok // 64).astype(f), (tok % 64).astype(f)
    table = np.zeros((P, 4, LAT), f)
    for n, width in ((0, 8), (2, 16)):
        freq = (f(10000.0) ** (-np.arange(width, dtype=f) / f(width))).astype(f)
        for p in range(P):
            q = p % (4 * width)
            ang = (row if q < 2 * width else column) * freq[q % width]
            table[p, n] = np.cos(ang)
            table[p, n + 1] = np.sin(ang) * (-1 if q % (2 * width) < width else 1)
    arrays["rope"] = table
    i, j = np.meshgrid(np.arange(P), np.arange(P), indexing="xy")
    same = i // CH == j // CH
    arrays["squares"] = np.ascontiguousarray(np.stack(
        [same & (j <= i), same & (j > i), i == j, np.ones((P, P)), (i // 64 == j // 64) / 64.0], axis=1).astype(f))
    arrays["scan_mask"] = np.ascontiguousarray(np.tile((np.arange(T) % CH != 0).astype(f), (P, 1)))

    nc = bacc.Bacc("TRN2", target_bir_lowering=False, num_devices=1)
    drams = {k: nc.dram_tensor(f"in_{k}", v.shape, mybir.dt.float32, kind="ExternalInput").ap() for k, v in arrays.items()}
    drams["out"] = nc.dram_tensor("out", (P, KT, LAT), mybir.dt.float32, kind="ExternalOutput").ap()
    build(nc, drams)
    r = run(nc, [{f"in_{k}": v for k, v in arrays.items()}], core_ids=[0])
    return r.results[0]["out"].transpose(2, 1, 0).reshape(1, LAT, D)
```

```python
from contextlib import ExitStack

import concourse.bass as bass
from concourse import mybir

F32 = mybir.dt.float32
F32R = mybir.dt.float32r
ALU = mybir.AluOpType
ACT = mybir.ActivationFunctionType
AX = mybir.AxisListType

P = 128
D = 1024
KT = D // P
CTX, LAT = 256, 512
T = CTX + LAT
TT = T // P
DEPTH = 2
CH = 64
NCH = T // CH
FF = 4 * D
NFG = FF // D
EPS = 1e-6
RING = 4
SLAB = 256
DK, DV = 32, 64
HD = 64
HQ = 8
QB = 256
KSCALE = DK ** -0.5
TAU = 16.0
W_IN = 2336
W_IN_SLABS = [(256, 256), (0, 256), (512, 256), (1024, 256), (1536, 32), (768, 256), (1280, 256),
              (2080, 256), (1568, 256), (1824, 256)]
(RET_V, RET_QK, RET_G, GLA_V, GLA_LOW, GLA_QK, GLA_G, ATT_KV, ATT_Q01, ATT_Q23) = range(10)
N_MOD = 6 * D // P
SH_A, SC_A, GT_A, SH_M, SC_M, GT_M = (KT * i for i in range(6))

COLS_C = 0
COLS_FG = 16
COLS_L = 24
L_MODB, L_AG, L_MG, L_QG, L_KG, L_GB, L_RD, L_N = 0, 48, 56, 64, 65, 66, 68, 70


def layer_program():
    win = [("w", "in", s) for s in range(len(W_IN_SLABS))]
    phases = {}
    phases["start"] = [("pm"[n % 2], 0, n) for n in range(8)]
    rest = [("m", 0, n) for n in range(8, 24)]
    mixed = []
    for s, slab in enumerate(win):
        take = units_of(slab)
        mixed += rest[:1] + [slab] + rest[1:take]
        rest = rest[take:]
    assert not rest
    phases["in0"] = mixed
    m = [("m", 1, n) for n in range(8)]
    w = [("w", "out", s) for s in range(4)]
    phases["out0"] = [m[0], w[0], m[1], m[2], w[1], m[3], m[4], w[2], m[5], m[6], w[3], m[7]]
    phases["mlp0"] = []
    for matrix in "12":
        w1 = [("w", matrix, s) for s in range(4)]
        m1 = [("m", 1, 8 + 2 * (matrix == "2") + s) for s in range(2)]
        phases["mlp0"] += [w1[0], m1[0], w1[1], w1[2], m1[1], w1[3]]
    phases["in1"] = win
    phases["out1"] = w
    phases["mlp1"] = [("w", "1", s) for s in range(4)] + [("w", "2", s) for s in range(4)]
    return phases


def units_of(item):
    return 1 if item[1:] == ("in", GLA_LOW) else 2


def work_items(slabs):
    out, seen, summed, values = [], [], [], []
    made = 0
    for j, item in enumerate(slabs):
        if item[0] == "p":
            out += [("s", j + 1), ("p", j), ("m", j + 1)]
        elif item[0] == "m":
            if not (j and slabs[j - 1][0] == "p") and ("s", j) not in out:
                seen.append(j)
        else:
            for half in range(units_of(item)):
                out.append(("u", j, half))
                if values:
                    out.append(("t", values.pop()))
                if item[1] == "in" and (item[2] in (RET_V, GLA_V) or (item[2], half) == (ATT_KV, 1)):
                    values.append(made)
                    made += 1
                out += [("m", summed.pop())] if summed else []
                if half == 1 and not seen and slabs[j + 1:] and slabs[j + 1][0] == "m":
                    seen.append(j + 1)
                if seen:
                    summed.append(seen.pop(0))
                    out.append(("s", summed[0]))
    for j in seen:
        out += [("m", k) for k in summed] + [("s", j)]
        summed = [j]
    return out + [("m", k) for k in summed]


def build(nc, d):
    phases = layer_program()
    order = ["start", "in0", "out0", "mlp0", "in1", "out1", "mlp1"]
    repeats = {p: NFG if p.startswith("mlp") else 1 for p in order}
    first_slab, first_w, first_m = {}, {}, {}
    ns = nw = nm = 0
    is_mod = lambda s: s[0] != "w"
    for p in order:
        first_slab[p], first_w[p], first_m[p] = ns, nw, nm
        ns += repeats[p] * len(phases[p])
        nw += repeats[p] * sum(s[0] == "w" for s in phases[p])
        nm += repeats[p] * sum(is_mod(s) for s in phases[p])
    flat = [s[0] for p in order for _ in range(repeats[p]) for s in phases[p]]

    ctx = ExitStack()
    with ctx:
        def sb(name, shape, dt=F32, stack=ctx):
            return stack.enter_context(nc.sbuf_tensor(name, shape, dt))

        sems = {}

        def sem(name):
            if name not in sems:
                sems[name] = ctx.enter_context(nc.semaphore(name))
            return sems[name]

        xT = sb("xT", [P, KT, T])
        raw = sb("raw", [P, RING, KT, SLAB])
        w_hi = sb("w_hi", [P, 2, KT, P], F32R)
        w_lo = sb("w_lo", [P, 2, KT, P], F32R)
        rope = sb("rope", [P, 4, LAT])
        squares = sb("squares", [P, 5, P])
        cols = sb("cols", [P, COLS_L + DEPTH * L_N])
        gate_w = sb("gate_w", [32, DEPTH, 2, P])
        modv = sb("modv", [P, DEPTH, N_MOD, 2])
        silu_c = sb("silu_c", [P, KT, 2])
        gain = sb("gain", [P, KT, 2])
        lgam = sb("lgam", [P, DEPTH, 2])
        small = sb("small", [P, 4])
        mod_acc = sb("mod_acc", [P, 2, 2, SLAB])
        ones_r = sb("ones_r", [P, P], F32R)
        decs = sb("decs", [P, 2, NCH])
        with ExitStack() as own:
            nsq = sb("nsq", [P, 2, T], F32, own)
            nacc = sb("nacc", [P, T], F32, own)
            nrs = sb("nrs", [P, T], F32, own)
        s_diag = sb("s_diag", [P, 2, NCH, 2 * DV])
        mask_f, mask_b, ident, ones, blocks = (squares[:, i, :] for i in range(5))

        with ExitStack() as own:
            g2 = sb("g2", [P, 2, T], F32, own)
            bcum = sb("bcum", [P, 2, T], F32, own)
            q_dec = sb("q_dec", [P, 2, T], F32, own)
            k_dec = sb("k_dec", [P, 2, T], F32, own)
            k2T = sb("k2T", [P, 2, TT, P], F32, own)
            state = sb("state", [P, 2, NCH, DV], F32, own)
            probs = sb("probs", [P, 2, 2, P], F32, own)
            ptmp = sb("ptmp", [P, 2, 2, P], F32, own)
            scan_mask = sb("scan_mask", [P, T], F32, own)
        with ExitStack() as own:
            with ExitStack() as prepare:
                rope_sw = sb("rope_sw", [P, LAT], F32, prepare)
                rope_t = sb("rope_t", [P, LAT], F32, prepare)
                qsq = sb("qsq", [P, 2, T], F32, prepare)
                qrs = sb("qrs", [P, 2, T], F32, prepare)
            mx = sb("mx", [P, 2, QB], F32, own)
            neg_diag = sb("neg_diag", [P, 2, QB], F32R, own)
            pexp = sb("pexp", [P, 2, TT * QB], F32, own)
            kk_hi = sb("kk_hi", [P, 2, T], F32R, own)
            kk_lo = sb("kk_lo", [P, 2, T], F32R, own)
            qq = sb("qq", [P, 2, 2, T], F32R, own)
            v_ones = sb("v_ones", [P, TT, 2, P], F32, own)
            rsum = sb("rsum", [HD, 2, QB], F32, own)
        h_hi = sb("h_hi", [P, KT, T], F32R)
        h_lo = sb("h_lo", [P, KT, T], F32R)
        with ExitStack() as own:
            u_hi = sb("u_hi", [P, KT, T], F32R, own)
            u_lo = sb("u_lo", [P, KT, T], F32R, own)
            u_full = sb("u_full", [P, 2, T], F32, own)
        with ExitStack() as own:
            nout = sb("nout", [P, 2, LAT], F32, own)
        ret_q = sb("ret_q", [P, T])
        ret_k = sb("ret_k", [P, T])
        gla_q = sb("gla_q", [P, T])
        gla_k = sb("gla_k", [P, T])
        low = sb("low", [32, T])
        ret_v = sb("ret_v", [P, TT, 256])
        gla_v = sb("gla_v", [P, TT, 256])
        att_v = sb("att_v", [P, TT, P])
        att_k = sb("att_k", [P, T])
        y = sb("y", [P, 8, T])

        psum = ctx.enter_context(nc.psum_tensor("psum", [P, 8 * 512], F32))
        pair = [psum[:, 1024 * i:1024 * (i + 1)] for i in range(4)]

        raw_ready = [sem(f"raw_ready{i}") for i in range(RING)]
        cols_ready, consts_ready, x_ready = sem("cols_ready"), sem("consts_ready"), sem("x_ready")
        w_hi_ready, w_lo_ready = sem("w_hi_ready"), sem("w_lo_ready")
        unit_done, unit_evacuated = sem("unit_done"), sem("unit_evacuated")
        mod_done, mod_evacuated = sem("mod_done"), sem("mod_evacuated")
        mod_acc_ready, mod_acc_step = sem("mod_acc_ready"), sem("mod_acc_step")
        h_hi_ready, h_lo_ready = sem("h_hi_ready"), sem("h_lo_ready")
        relu_ready, u_hi_ready, u_lo_ready = sem("relu_ready"), sem("u_hi_ready"), sem("u_lo_ready")
        dve_step, act_step = sem("dve_step"), sem("act_step")
        steps = {"dve": 0, "act": 0}

        def dve_link(ins):
            steps["dve"] += 1
            ins.then_inc(dve_step, 1)
            nc.vector.wait_ge(dve_step, steps["dve"])

        def act_link(ins):
            steps["act"] += 1
            ins.then_inc(act_step, 1)
            nc.scalar.wait_ge(act_step, steps["act"])

        def phase_w(phase):
            return sum(s[0] == "w" for s in phases[phase])

        def at(phase, j, i):
            n = first_slab[phase] + j
            per = len(phases[phase])
            kinds = [s[0] for s in phases[phase]]
            assert repeats[phase] == 1 or per % RING == 0
            per_w = kinds.count("w")
            w = first_w[phase] + kinds[:j].count("w") + i * per_w
            m = first_m[phase] + j - kinds[:j].count("w") + i * (per - per_w)
            return n % RING, 16 * (n // RING + 1) + 16 * (per // RING) * i, 2 * w, m

        units_before_norm = {1: 2 * first_w["mlp0"], 2: 2 * first_w["in1"], 3: 2 * first_w["mlp1"],
                             4: 2 * (first_w["mlp1"] + 8 * NFG)}

        def cuts(t_from):
            return ((t_from, 512 - t_from), (512, T - 512))

        def spans(layer, item, half):
            if layer == 1 and not (item[1] == "in" and (item[2], half) in CTX_UNITS):
                return [(CTX, LAT, 0)]
            return [(0, 512, 0), (512, 256, 512)]

        CTX_UNITS = {(RET_V, 0), (RET_V, 1), (RET_QK, 1), (GLA_V, 0), (GLA_V, 1), (GLA_QK, 1), (GLA_LOW, 0), (ATT_KV, 0),
                     (ATT_KV, 1)}
        value_place = [4, 5, 6, 7, 7]
        turned = [ret_v[:, :, 0:P], ret_v[:, :, P:2 * P], gla_v[:, :, 0:P], gla_v[:, :, P:2 * P], att_v[:]]
        work = {p: work_items(phases[p]) for p in order}

        OUT_BANK, MAX_BANK = 6 * 512, 7 * 512

        def score_place(n):
            return psum[:, 3 * 512 * (n % 2):3 * 512 * (n % 2 + 1)]

        def attention_items(layer):
            return [(h, b, CTX // P if b == 0 else TT) for h in range(HQ) for b in range(layer, T // QB)]

        def before(layer, name):
            per_layer = {"qsq_ready": 5, "qsum_ready": 5, "qrs_ready": 5, "qrs_used": 5, "q_ready": 4, "qq_hi_ready": 4,
                         "qq_lo_ready": 4, "k_ready": 1, "kk_hi_ready": 1, "kk_lo_ready": 1, "v_ones_ready": 1}
            return layer * per_layer.get(name, len(attention_items(0)))

        def ahead(kind, phase, j, i):
            return flat[:first_slab[phase] + j].count(kind) + i * [s[0] for s in phases[phase]].count(kind)

        def first_weights(phase):
            return [s[0] for s in phases[phase]].index("w")

        def split_next(split, phase, n, i):
            later = [o for o in work[phase][n + 1:] if o[0] == "u"]
            if later:
                split(phase, later[0][1], i, later[0][2])
            elif repeats[phase] > 1 and not (isinstance(i, int) and i == repeats[phase] - 1):
                split(phase, first_weights(phase), i + 1, 0)
            elif order.index(phase) + 1 < len(order):
                following = order[order.index(phase) + 1]
                split(following, first_weights(following), 0, 0)

        def place_states(copy, h, dr):
            rows = slice(32 * h, 32 * h + 32)
            return copy(s_diag[rows, dr, :, DV * (h % 2):DV * (h % 2) + DV], state[rows, dr])

        def value_unit(layer, n):
            p = f"in{layer}"
            j = phases[p].index(("w", "in", (RET_V, RET_V, GLA_V, GLA_V, ATT_KV)[n]))
            return at(p, j, 0)[2] + (0, 1, 0, 1, 1)[n]

        def mod_number(phase, j):
            return j - [s[0] for s in phases[phase]][:j].count("w")

        block = ctx.enter_context(nc.Block())

        @block.sync
        def _(sp):
            sp.dma_start(cols[:], d["cols"]).then_inc(cols_ready, 16)
            sp.dma_start(squares[:], d["squares"]).then_inc(cols_ready, 16)

            def load(phase, j, i):
                item = phases[phase][j]
                slot, _, _, _ = at(phase, j, i)
                n = first_slab[phase] + j
                if n >= RING:
                    used = lambda kind, r: flat[:n + r * len(phases[phase]) - RING + 1].count(kind)
                    if isinstance(i, int):
                        before, step = {kind: used(kind, i) for kind in "wmp"}, {kind: 0 for kind in "wmp"}
                    else:
                        step = {kind: used(kind, 2) - used(kind, 1) for kind in "wmp"}
                        before = {kind: used(kind, 1) - step[kind] for kind in "wmp"}
                    waits = [(sm, each * before[kind] - less + each * step[kind] * i)
                             for sm, each, less, kind in ((mod_done, 2, 1, "p"), (mod_acc_ready, 1, 0, "m"),
                                                          (w_lo_ready, 2, 0, "w")) if before[kind]]
                layer = int(phase[-1]) if phase != "start" else 0
                dst = raw[:, slot].rearrange("p k c -> p (k c)")
                if item[0] != "w":
                    src = d["mod_w"][item[1], item[2] + (4 * i if phase == "mlp0" else 0)]
                elif item[1] == "in":
                    c0, wd = W_IN_SLABS[item[2]]
                    dst, src = dst[:, 0:KT * wd], d["w_in"][layer, :, KT * c0:KT * (c0 + wd)]
                elif item[1] == "out":
                    src = d["w_out"][layer, item[2]]
                else:
                    src = d["w_" + item[1]][layer * NFG + i, item[2]]
                if not isinstance(i, int):
                    for _, value in waits:
                        if not isinstance(value, int):
                            sp.compute_val(value)
                    sp.compute_val(src.offset * 4)
                if n >= RING:
                    for sm, value in waits:
                        sp.wait_ge(sm, value)
                sp.dma_start(dst, src).then_inc(raw_ready[slot], 16)

            for p in order:
                if repeats[p] > 1:
                    for j in range(len(phases[p])):
                        load(p, j, 0)
                    with sp.Fori(1, repeats[p]) as i:
                        for j in range(len(phases[p])):
                            load(p, j, i)
                else:
                    for j in range(len(phases[p])):
                        load(p, j, 0)
                        if p == "start" and j == 3:
                            sp.dma_start(xT[:], d["xT"]).then_inc(x_ready, 16)
                            sp.dma_start(gate_w[:], d["gate_w"]).then_inc(consts_ready, 16)
                            sp.dma_start(rope[:], d["rope"]).then_inc(consts_ready, 16)
            for k in range(KT):
                sp.wait_ge(sem("out_ready"), k + 1)
                sp.dma_start(d["out"][:, k, :], nout[:, k % 2, :]).then_inc(sem(f"out_stored{k % 2}"), 16)
            sp.wait_ge(sem("out_stored0"), 16 * KT // 2)
            sp.wait_ge(sem("out_stored1"), 16 * KT // 2)

        @block.tensor
        def _(pe):
            mm = nc.tensor.matmul

            def mod_slab(phase, j, i):
                slot, ready, _, m = at(phase, j, i)
                kind = phases[phase][j][0]
                if phase == "start" and j == 0:
                    pe.wait_ge(sem("silu_c_ready"), 1)
                if kind == "p":
                    pe.wait_ge(raw_ready[slot], ready)
                if phase != "start" or j >= 2:
                    pe.wait_ge(mod_evacuated, m - 1)
                par = (first_m[phase] + mod_number(phase, j)) % 2
                if kind == "m":
                    pe.wait_ge(mod_acc_ready, ahead("m", phase, j, i) + 1)
                    acc = mod_acc[:, ahead("m", phase, j, 0) % 2]
                    for t in range(2):
                        for s in range(2):
                            last = mm(pair[3][:, 512 * par + 2 * t + s:512 * par + 2 * t + s + 1],
                                      acc[:, s, t * P:(t + 1) * P], ones[:, 0:1], start=True, stop=True)
                    last.then_inc(mod_done, 1)
                    return
                for t in range(2):
                    o = pair[3][:, 512 * par + 2 * t:512 * par + 2 * t + 2]
                    for k in range(KT):
                        last = mm(o, raw[:, slot, k, t * P:(t + 1) * P], silu_c[:, k, :], start=(k == 0), stop=(k == KT - 1))
                last.then_inc(mod_done, 1)

            def unit(phase, j, i, half, first):
                item = phases[phase][j]
                layer = int(phase[-1])
                _, _, u, _ = at(phase, j, i)
                u = u + half
                pe.wait_ge(w_lo_ready, u + 1)
                if not (phase == "in0" and item[2] == 0):
                    pe.wait_ge(unit_evacuated, u - 1)
                par = half
                out = pair[par]
                a_hi, a_lo = (u_hi, u_lo) if item[1] == "2" else (h_hi, h_lo)
                m = 32 if units_of(item) == 1 else P
                for k in range(KT):
                    if first:
                        if item[1] == "2":
                            pe.wait_ge(u_lo_ready, (KT * NFG * layer + k + 1) + KT * i)
                        else:
                            nh = KT * h_count[phase] + k + 1
                            pe.wait_ge(h_lo_ready, nh)
                    for n, (w, a) in enumerate(((w_hi, a_hi), (w_hi, a_lo), (w_lo, a_hi))):
                        for t0, width, c0 in spans(layer, item, half):
                            last = mm(out[0:m, c0:c0 + width], w[:, par, k, 0:m], a[:, k, t0:t0 + width],
                                      start=(k == 0 and n == 0), stop=(k == KT - 1 and n == 2))
                last.then_inc(unit_done, 2 if units_of(item) == 1 else 1)

            h_count = {"in0": 0, "out0": 1, "mlp0": 2, "in1": 3, "out1": 4, "mlp1": 5}

            def turn_values(layer, n):
                u_made = value_unit(layer, n)
                pe.wait_ge(unit_evacuated, u_made + 1)
                if n or layer:
                    pe.wait_ge(sem("values_copied"), 5 * layer + n)
                for t in range(TT):
                    last = nc.tensor.transpose(pair[2][:, t * P:(t + 1) * P], y[:, value_place[n], t * P:(t + 1) * P], ident)
                last.then_inc(sem("values_turned"), 1)

            def products(phase, i=0):
                for kind, j, *half in work[phase]:
                    if kind == "t":
                        turn_values(int(phase[-1]), j)
                    elif kind == "u":
                        unit(phase, j, i, half[0], half[0] == 0 and phases[phase][j][2] == 0)
                    elif kind != "s":
                        mod_slab(phase, j, i)

            def norm_sum(n):
                pe.wait_ge(sem("norm_sq_used"), KT * (n + 1))
                for t0, width in cuts(CTX if n >= 3 else 0):
                    last = mm(pair[2][:, t0:t0 + width], ones, nacc[:, t0:t0 + width], start=True, stop=True)
                last.then_inc(sem("norm_sum_ready"), 1)

            def scans(layer, ty):
                S = lambda name: sem(f"{name}_{layer}_{ty}")
                v = (ret_v, gla_v)[ty]
                first = 0 if layer == 0 else CTX // P
                if ty == 1:
                    pe.wait_ge(unit_evacuated, 2 * first_w[f"in{layer}"] + 20)
                    for dr in range(2):
                        if dr == 0:
                            pe.wait_ge(sem(f"y_done_{layer}_0"), 1)
                        for t0, width in ((0, 512), (512, 256)):
                            last = mm(pair[2 + dr][:, t0:t0 + width], gate_w[:, layer, dr, :], low[:, t0:t0 + width],
                                      start=True, stop=True)
                        last.then_inc(S("z_ready"), 1)
                for dr in range(2):
                    pe.wait_ge(S("k2_ready"), dr + 1)
                    for t in range(TT):
                        last = nc.tensor.transpose(pair[dr][:, t * P:(t + 1) * P], bcum[:, dr, t * P:(t + 1) * P], ident)
                    last.then_inc(S("k2T_in_psum"), 1)
                for dr in range(2):
                    pe.wait_ge(S(f"k2T_ready{dr}"), 1)
                    for c in range(NCH):
                        r0 = CH * (c % 2)
                        for h in range(4):
                            o = pair[2 + dr][32 * h:32 * h + 32, 512 * (c % 2) + DV * (c // 2):512 * (c % 2) + DV * (c // 2) + DV]
                            last = mm(o, k2T[r0:r0 + CH, dr, c // 2, 32 * h:32 * h + 32],
                                      v[r0:r0 + CH, c // 2, DV * h:DV * h + DV], start=True, stop=True,
                                      skip_group_check=True)
                    last.then_inc(S("kv_ready"), 1)
                rounds = [(t, hp) for t in range(first, TT) for hp in range(2)]

                def scores(r):
                    t, hp = rounds[r]
                    if r >= 2:
                        pe.wait_ge(S("probs_ready"), r - 1)
                    for h in (2 * hp, 2 * hp + 1):
                        rows = slice(32 * h, 32 * h + 32)
                        for dr in range(2):
                            c0 = 512 * (h % 2) + P * dr
                            last = mm(pair[hp][:, c0:c0 + P], k_dec[rows, dr, t * P:(t + 1) * P],
                                      q_dec[rows, dr, t * P:(t + 1) * P], start=True, stop=True, skip_group_check=True)
                    last.then_inc(S("scores_ready"), 1)

                def outputs(r):
                    t, hp = rounds[r]
                    pe.wait_ge(S("probs_ready"), r + 1)
                    opens = t == first or t == 4
                    for h in (2 * hp, 2 * hp + 1):
                        last = mm(pair[2 + hp][64 * (h % 2):64 * (h % 2) + 64, t * P:(t + 1) * P],
                                  v[:, t, DV * h:DV * h + DV], probs[:, r % 2, h % 2, :], start=opens, stop=False,
                                  skip_group_check=True)
                    last.then_inc(S("probs_used"), 1)
                    rows = slice(64 * hp, 64 * hp + 64)
                    for c in (2 * t, 2 * t + 1):
                        for dr in range(2):
                            if c == (0, CTX // CH - 1)[dr]:
                                continue
                            last = mm(pair[2 + hp][:, c * CH:(c + 1) * CH], s_diag[rows, dr, c, :],
                                      q_dec[rows, dr, c * CH:(c + 1) * CH], start=False, stop=True,
                                      skip_group_check=True)
                    if r == len(rounds) - 1:
                        last.then_inc(S("o_ready"), 1)

                pe.wait_ge(S("k2T_ready0"), 1)
                pe.wait_ge(S("k2T_ready1"), 1)
                scores(0)
                pe.wait_ge(S("s_diag_ready"), 2)
                pe.wait_ge(S("s_diag_ready_a"), 6)
                for r in range(len(rounds)):
                    if r + 1 < len(rounds):
                        scores(r + 1)
                    outputs(r)
                for n in range(2 if ty == 0 else 1):
                    for hp in range(2):
                        pe.wait_ge(S("stat_in_ready"), 2 * n + hp + 1)
                        src = (g2, bcum)[n] if ty == 0 else bcum
                        for t0, width in cuts(CTX * layer):
                            last = mm(pair[hp][:, t0:t0 + width], blocks, src[:, hp, t0:t0 + width], start=True, stop=True)
                        last.then_inc(S("stat_ready"), 1)

            def attention(layer):
                S = lambda name: sem(name)
                for n in range(5):
                    pe.wait_ge(S("qsq_ready"), before(layer, "qsq_ready") + n + 1)
                    if n >= 2:
                        pe.wait_ge(S("qrs_ready"), before(layer, "qrs_ready") + n - 1)
                    for t0, width in cuts(CTX * layer if n else 0):
                        last = mm(pair[n % 2][:, t0:t0 + width], blocks, qsq[:, n % 2, t0:t0 + width], start=True, stop=True)
                    last.then_inc(S("qsum_ready"), 1)
                pe.wait_ge(S("qrs_ready"), before(layer, "qrs_ready") + 5)
                pe.wait_ge(sem("ones_r_ready"), 1)
                items = attention_items(layer)

                def scores(n):
                    h, b, tiles = items[n]
                    if n == 0:
                        pe.wait_ge(S("kk_lo_ready"), before(layer, "kk_lo_ready") + 1)
                    pe.wait_ge(S("qq_lo_ready"), before(layer, "qq_lo_ready") + h // 2 + 1)
                    if n >= 2:
                        pe.wait_ge(S("exp_ready"), before(layer, "exp_ready") + n - 1)
                    for k in range(tiles):
                        for m, kk in enumerate((kk_hi, kk_lo)):
                            last = mm(score_place(n)[:, k * QB:(k + 1) * QB], kk[:, h // 4, k * P:(k + 1) * P],
                                      qq[:, h // 2 % 2, h % 2, b * QB:(b + 1) * QB], start=(k % 2 == 0 and m == 0),
                                      stop=False, skip_group_check=True)
                    last.then_inc(S("att_scores_ready"), 1)

                def turn_max(n):
                    pe.wait_ge(S("mx_ready"), before(layer, "mx_ready") + n + 1)
                    if n >= 1:
                        pe.wait_ge(S("neg_diag_ready"), before(layer, "neg_diag_ready") + n)
                    for i in range(2):
                        last = nc.tensor.transpose(psum[:, MAX_BANK + P * i:MAX_BANK + P * (i + 1)],
                                                   mx[:, n % 2, P * i:P * (i + 1)], ident)
                    last.then_inc(S("mx_turned"), 1)

                def subtract_max(n):
                    pe.wait_ge(S("neg_diag_ready"), before(layer, "neg_diag_ready") + n + 1)
                    for k in range(items[n][2]):
                        last = mm(score_place(n)[:, k * QB:(k + 1) * QB], ones_r[:], neg_diag[:, n % 2, :], start=False,
                                  stop=True, skip_group_check=True)
                    last.then_inc(S("shifted"), 1)

                def weigh(n, part):
                    h, b, tiles = items[n]
                    if part == 0:
                        pe.wait_ge(S("exp_ready"), before(layer, "exp_ready") + n + 1)
                        if n == 0:
                            pe.wait_ge(S("v_ones_ready"), before(layer, "v_ones_ready") + 1)
                            pe.wait_ge(sem("v_ones_set"), layer + 1)
                        else:
                            pe.wait_ge(S("sums_read"), before(layer, "sums_read") + n)
                            pe.wait_ge(S("out_read"), before(layer, "out_read") + n)
                    for k in range(part * tiles // 2, (part + 1) * tiles // 2):
                        last = mm(psum[:, OUT_BANK:OUT_BANK + QB], v_ones[:, k, h // 4, :],
                                  pexp[:, n % 2, k * QB:(k + 1) * QB], start=(k == 0), stop=(k == tiles - 1),
                                  skip_group_check=True)
                    if part == 1:
                        last.then_inc(S("att_out_ready"), 1)

                scores(0)
                for n in range(len(items) + 2):
                    if n < len(items):
                        turn_max(n)
                    if n >= 2:
                        weigh(n - 2, 0)
                    if n + 1 < len(items):
                        scores(n + 1)
                    if n >= 2:
                        weigh(n - 2, 1)
                    if n < len(items):
                        subtract_max(n)

            pe.wait_ge(cols_ready, 32)
            products("start")
            pe.wait_ge(consts_ready, 32)
            norm_sum(0)
            for layer in range(DEPTH):
                products(f"in{layer}")
                pe.wait_ge(unit_evacuated, 2 * first_w[f"in{layer}"] + 20)
                if layer == 0:
                    pe.wait_ge(mod_evacuated, first_m["out0"])
                scans(layer, 0)
                scans(layer, 1)
                attention(layer)
                products(f"out{layer}")
                norm_sum(2 * layer + 1)
                with pe.Fori(0, NFG - 1) as i:
                    products(f"mlp{layer}", i)
                products(f"mlp{layer}", NFG - 1)
                norm_sum(2 * layer + 2)

        @block.scalar
        def _(act):
            F = nc.scalar.activation

            def split_hi(phase, j, i, half):
                item = phases[phase][j]
                slot, ready, u, _ = at(phase, j, i)
                u = u + half
                act.wait_ge(raw_ready[slot], ready)
                if not (phase == "in0" and item[2] == 0):
                    act.wait_ge(unit_done, u - 1)
                if units_of(item) == 1:
                    src = raw[:, slot].rearrange("p k c -> p (k c)")[:, 0:KT * 32].rearrange("p (k c) -> p k c", k=KT)
                    F(w_hi[:, 0, :, 0:32], src, ACT.Copy).then_inc(w_hi_ready, 2)
                else:
                    F(w_hi[:, half], raw[:, slot, :, half * P:(half + 1) * P], ACT.Copy).then_inc(w_hi_ready, 1)

            def run(phase, i=0):
                t_from = 0 if phase.endswith("0") else CTX
                layer = int(phase[-1]) if phase != "start" else 0
                for n, (kind, j, *half) in enumerate(work[phase]):
                    if kind == "t":
                        act.wait_ge(sem("values_turned"), 5 * layer + j + 1)
                        F(turned[j], pair[2][:, 0:T].rearrange("p (t c) -> p t c", t=TT), ACT.Copy).then_inc(
                            sem("values_copied"), 1)
                        continue
                    if kind != "u":
                        continue
                    half = half[0]
                    split_next(split_hi, phase, n, i)
                    item = phases[phase][j]
                    if item[1] == "1":
                        m = 2 * item[2] + half
                        cnt = (KT * NFG * layer + m + 1) + KT * i
                        _, _, u, _ = at(phase, j, i)
                        act.wait_ge(unit_done, u + half + 1)
                        full = u_full[:, half, t_from:]
                        if not (layer == 0 and m < 2):
                            act.wait_ge(u_lo_ready, cnt - 2)
                        F(full, pair[half][:, 0:T - t_from], ACT.Relu).then_inc(relu_ready, 1)
                        act.wait_ge(unit_evacuated, u + half + 1)
                        F(u_hi[:, m, t_from:], full, ACT.Copy).then_inc(u_hi_ready, 1)

            def norm(n, lat_only, final=False):
                t_from = CTX if lat_only else 0
                for k in range(KT):
                    if n == 0:
                        if k == 0:
                            act.wait_ge(x_ready, 16)
                    else:
                        act.wait_ge(unit_evacuated, units_before_norm[n] - KT + k + 1)
                    if k >= 2:
                        act.wait_ge(sem("norm_sq_used"), KT * n + k - 1)
                    F(nsq[:, k % 2, t_from:], xT[:, k, t_from:], ACT.Square).then_inc(sem("norm_sq_ready"), 1)
                act.wait_ge(sem("norm_sum_ready"), n + 1)
                act_link(F(nrs[:, t_from:], pair[2][:, t_from:T], ACT.Ln, bias=EPS, scale=1.0 / D))
                F(nrs[:, t_from:], nrs[:, t_from:], ACT.Exp, scale=-0.5).then_inc(sem("norm_rs_ready"), 1)
                if final:
                    return
                l, sh = n // 2, (SH_A, SH_M)[n % 2]
                for k in range(KT):
                    act.wait_ge(sem("norm_t_ready"), KT * n + k + 1)
                    for t0, t1, s in ([] if lat_only else [(0, CTX, 1)]) + [(CTX, T, 0)]:
                        last = F(h_hi[:, k, t0:t1], nsq[:, k % 2, t0:t1], ACT.Identity, bias=modv[:, l, sh + k, s:s + 1])
                    last.then_inc(h_hi_ready, 1)

            def scans(layer, ty):
                S = lambda name: sem(f"{name}_{layer}_{ty}")
                t_from = 0 if layer == 0 else CTX
                if ty == 1:
                    for dr in range(2):
                        act.wait_ge(S("negabs_ready"), dr + 1)
                        act_link(F(bcum[:, dr], bcum[:, dr], ACT.Exp))
                        F(bcum[:, dr], bcum[:, dr], ACT.Ln, bias=1.0).then_inc(S("softplus_ready"), 1)
                s = 1.0 if ty == 0 else 1.0 / TAU
                for dr in range(2):
                    act.wait_ge(S("bcum_ready"), dr + 1)
                    F(q_dec[:, dr], bcum[:, dr], ACT.Exp, scale=s).then_inc(S("decays_ready"), 1)
                    F(k_dec[:, dr], bcum[:, dr], ACT.Exp, scale=-s).then_inc(S("decays_ready"), 1)
                act.wait_ge(S("k2T_in_psum"), 2)
                F(k2T[:, 1].rearrange("p t c -> p (t c)"), pair[1][:, 0:T], ACT.Copy).then_inc(S("k2T_ready1"), 1)
                act.wait_ge(sem("s_diag_clear"), layer + 1)
                for dr in range(2):
                    act.wait_ge(S("state_ready"), dr + 1)
                    for h in range(3):
                        place_states(lambda o, i: F(o, i, ACT.Copy), h, dr).then_inc(S("s_diag_ready_a"), 1)
                act.wait_ge(S("s_diag_ready"), 2)
                act.wait_ge(S("s_diag_ready_a"), 6)
                for hp in range(2):
                    F(state[:, hp].rearrange("p c e -> p (c e)")[:, t_from:], y[:, 2 * ty + hp, t_from:], ACT.Exp,
                      scale=-1.0).then_inc(S("gate_exp_ready"), 1)
                act.wait_ge(S("o_ready"), 1)
                for hp in range(2):
                    if ty == 0:
                        F(g2[:, hp, t_from:], pair[2 + hp][:, t_from:T], ACT.Copy).then_inc(S("stat_in_ready"), 1)
                    else:
                        F(bcum[:, hp, t_from:], pair[2 + hp][:, t_from:T], ACT.Square).then_inc(S("stat_in_ready"), 1)
                if ty == 0:
                    for hp in range(2):
                        act.wait_ge(S("centred_ready"), hp + 1)
                        F(bcum[:, hp, t_from:], g2[:, hp, t_from:], ACT.Square).then_inc(S("stat_in_ready"), 1)
                base = 2 if ty == 0 else 0
                for hp in range(2):
                    act.wait_ge(S("stat_ready"), base + hp + 1)
                    act_link(F(q_dec[:, hp, t_from:], pair[hp][:, t_from:T], ACT.Ln, bias=EPS))
                    F(q_dec[:, hp, t_from:], q_dec[:, hp, t_from:], ACT.Exp, scale=-0.5).then_inc(S("head_rs_ready"), 1)

            def attention(layer):
                S = lambda name: sem(name)
                act.wait_ge(sem(f"y_done_{layer}_1"), 1)
                for n in range(5):
                    src = y[:, 3 + n, CTX * layer:] if n else att_k[:]
                    if n >= 2:
                        act.wait_ge(S("qsum_ready"), before(layer, "qsum_ready") + n - 1)
                    F(qsq[:, n % 2, CTX * layer if n else 0:], src, ACT.Square).then_inc(S("qsq_ready"), 1)
                    if n >= 1:
                        root(S, layer, n - 1, CTX * layer if n > 1 else 0)
                    if n == 1:
                        F(v_ones[:, :, :, 0:HD], att_v.rearrange("p t (g e) -> p t g e", g=2), ACT.Copy).then_inc(
                            S("v_ones_ready"), 1)
                root(S, layer, 4, CTX * layer)
                act.wait_ge(S("k_ready"), before(layer, "k_ready") + 1)
                for kv in range(2):
                    for half in range(2):
                        last = F(kk_hi[64 * half:64 * half + 64, kv], att_k[64 * kv:64 * kv + 64], ACT.Copy)
                last.then_inc(S("kk_hi_ready"), 1)
                items = attention_items(layer)
                per = len(items) // 4

                def split_q(p):
                    act.wait_ge(S("q_ready"), before(layer, "q_ready") + p + 1)
                    if p >= 2:
                        act.wait_ge(S("att_scores_ready"), before(layer, "att_scores_ready") + per * (p - 1))
                    for half in range(2):
                        rows = slice(64 * half, 64 * half + 64)
                        last = F(qq[rows, p % 2, half, CTX * layer:], y[rows, 4 + p, CTX * layer:], ACT.Copy)
                    last.then_inc(S("qq_hi_ready"), 1)

                split_q(0)
                act.wait_ge(S("qrs_used"), before(layer, "qrs_used") + 5)
                for n in range(len(items) + 2):
                    if n >= 2:
                        act.wait_ge(S("att_out_ready"), before(layer, "att_out_ready") + n - 1)
                        if n >= 4:
                            act.wait_ge(S("y_att_ready"), before(layer, "y_att_ready") + n - 3)
                        F(rsum[:, n % 2], psum[HD:P, OUT_BANK:OUT_BANK + QB], ACT.Ln).then_inc(S("sums_read"), 1)
                    if n < len(items):
                        act.wait_ge(S("shifted"), before(layer, "shifted") + n + 1)
                        width = QB * items[n][2]
                        F(pexp[:, n % 2, 0:width], score_place(n)[:, 0:width], ACT.Exp, scale=HD ** -0.5).then_inc(
                            S("exp_ready"), 1)
                    if n >= 2:
                        act.wait_ge(S("sums_read"), before(layer, "sums_read") + n - 1)
                        F(rsum[:, n % 2], rsum[:, n % 2], ACT.Exp, scale=-1.0).then_inc(S("rsum_ready"), 1)
                    if n % per == 1 and n // per + 1 < HQ // 2:
                        split_q(n // per + 1)

            def root(S, layer, n, t_from):
                act.wait_ge(S("qsum_ready"), before(layer, "qsum_ready") + n + 1)
                if n >= 2:
                    act.wait_ge(S("qrs_used"), before(layer, "qrs_used") + n - 1)
                act_link(F(qrs[:, n % 2, t_from:], pair[n % 2][:, t_from:T], ACT.Ln, bias=EPS))
                F(qrs[:, n % 2, t_from:], qrs[:, n % 2, t_from:], ACT.Exp, scale=-0.5).then_inc(S("qrs_ready"), 1)

            def split_y(layer):
                t_from = 0 if layer == 0 else CTX
                act.wait_ge(sem("y_att_ready"), before(layer, "y_att_ready") + len(attention_items(layer)))
                for k in range(KT):
                    F(h_hi[:, k, t_from:], y[:, k, t_from:], ACT.Copy).then_inc(h_hi_ready, 1)

            nc.scalar.preload_act_table_set("natural_log_exp_and_others")
            act.wait_ge(cols_ready, 32)
            F(ones_r[:], ones, ACT.Copy).then_inc(sem("ones_r_ready"), 1)
            act.wait_ge(sem("ln_first"), 1)
            act_link(F(lgam[:, :, :], small[:, 0:4].rearrange("p (l d) -> p l d", l=2), ACT.Exp))
            F(lgam[:, :, :], lgam[:, :, :], ACT.Ln, bias=1.0).then_inc(sem("lgam_softplus"), 1)
            F(silu_c[:], cols[:, 0:16].rearrange("p (k s) -> p k s", s=2), ACT.Exp, scale=-1.0).then_inc(sem("exp_c_ready"), 1)
            split_hi("in0", first_weights("in0"), 0, 0)
            norm(0, False)
            for layer in range(DEPTH):
                run(f"in{layer}")
                scans(layer, 0)
                scans(layer, 1)
                attention(layer)
                split_y(layer)
                run(f"out{layer}")
                norm(2 * layer + 1, layer == 1)
                with act.Fori(0, NFG - 1) as i:
                    run(f"mlp{layer}", i)
                run(f"mlp{layer}", NFG - 1)
                norm(2 * layer + 2, layer == 1, final=(layer == 1))

        @block.vector
        def _(dve):
            V = nc.vector
            shuffles = {w: [(p // (2 * w)) * 2 * w + (p % (2 * w) + w) % (2 * w) for p in range(32)] for w in (8, 16)}

            def split_lo(phase, j, i, half):
                item = phases[phase][j]
                slot, ready, u, _ = at(phase, j, i)
                u = u + half
                dve.wait_ge(raw_ready[slot], ready)
                if units_of(item) == 1:
                    dve.wait_ge(w_hi_ready, u + 2)
                    src = raw[:, slot].rearrange("p k c -> p (k c)")[:, 0:KT * 32].rearrange("p (k c) -> p k c", k=KT)
                    V.tensor_tensor(w_lo[:, 0, :, 0:32], src, w_hi[:, 0, :, 0:32].bitcast(F32),
                                    ALU.subtract).then_inc(w_lo_ready, 2)
                else:
                    dve.wait_ge(w_hi_ready, u + 1)
                    V.tensor_tensor(w_lo[:, half], raw[:, slot, :, half * P:(half + 1) * P], w_hi[:, half].bitcast(F32),
                                    ALU.subtract).then_inc(w_lo_ready, 1)

            def in_target(s, half):
                if s == ATT_KV:
                    return att_k[:] if half == 0 else y[:, value_place[4]]
                if s in (RET_QK, GLA_QK):
                    return {RET_QK: (ret_q, ret_k), GLA_QK: (gla_q, gla_k)}[s][half][:]
                return y[:, {RET_V: 4, GLA_V: 6, RET_G: 0, GLA_G: 2, ATT_Q01: 4, ATT_Q23: 6}[s] + half]

            def evacuate(phase, j, i, half):
                item = phases[phase][j]
                layer = int(phase[-1])
                _, _, u, _ = at(phase, j, i)
                u = u + half
                ps = pair[half]
                sp = spans(layer, item, half)
                lat = len(sp) == 1
                if item[1] == "in":
                    if units_of(item) == 1:
                        dve.wait_ge(unit_done, u + 2)
                        V.tensor_copy(low[:], ps[0:32, 0:T]).then_inc(unit_evacuated, 2)
                        return
                    dve.wait_ge(unit_done, u + 1)
                    dst = in_target(item[2], half)
                    if item[2] in (ATT_KV, ATT_Q01, ATT_Q23):
                        turned_by_now = {ATT_KV: 4, ATT_Q01: 4, ATT_Q23: 5}[item[2]]
                        dve.wait_ge(sem("values_turned"), 5 * layer + turned_by_now)
                    if lat:
                        V.tensor_copy(dst[:, CTX:T], ps[:, 0:LAT]).then_inc(unit_evacuated, 1)
                    else:
                        V.tensor_copy(dst, ps[:, 0:T]).then_inc(unit_evacuated, 1)
                    return
                m = 2 * item[2] + half
                dve.wait_ge(unit_done, u + 1)
                t_from = CTX if lat else 0
                if item[1] == "1":
                    cnt = (KT * NFG * layer + m + 1) + KT * i
                    dve.wait_ge(relu_ready, cnt)
                    full = u_full[:, half, t_from:]
                    V.tensor_tensor(full, full, ps[:, 0:T - t_from], ALU.mult).then_inc(unit_evacuated, 1)
                    dve.wait_ge(u_hi_ready, cnt)
                    V.tensor_tensor(u_lo[:, m, t_from:], full, u_hi[:, m, t_from:].bitcast(F32),
                                    ALU.subtract).then_inc(u_lo_ready, 1)
                    return
                gt = (GT_A if item[1] == "out" else GT_M) + m
                for t0, t1, s in ([] if lat else [(0, CTX, 1)]) + [(CTX, T, 0)]:
                    c0 = t0 - t_from
                    last = V.scalar_tensor_tensor(out=xT[:, m, t0:t1], in0=ps[:, c0:c0 + t1 - t0],
                                                  scalar=modv[:, layer, gt, s:s + 1], in1=xT[:, m, t0:t1],
                                                  op0=ALU.mult, op1=ALU.add)
                last.then_inc(unit_evacuated, 1)

            def sum_mod(phase, j, i):
                slot, ready, _, m = at(phase, j, i)
                n = ahead("m", phase, j, i)
                if repeats[phase] > 1:
                    dve.wait_ge(mod_done, m - 1)
                else:
                    mods = [k for k in flat if k != "w"]
                    earlier = [x for x in range(m) if mods[x] == "m"]
                    if len(earlier) >= 2:
                        dve.wait_ge(mod_done, earlier[-2] + 1)
                    elif not earlier:
                        dve.wait_ge(sem("silu_c_ready"), 1)
                dve.wait_ge(raw_ready[slot], ready)
                for k in range(KT):
                    for s in range(2):
                        a = mod_acc[:, ahead("m", phase, j, 0) % 2, s, :]
                        if k == 0:
                            ins = V.tensor_scalar(a, raw[:, slot, k, :], silu_c[:, k, s:s + 1], None, ALU.mult)
                        else:
                            dve.wait_ge(mod_acc_step, 2 * (KT - 1) * n + 2 * (k - 1) + s + 1)
                            ins = V.scalar_tensor_tensor(out=a, in0=raw[:, slot, k, :], scalar=silu_c[:, k, s:s + 1],
                                                         in1=a, op0=ALU.mult, op1=ALU.add)
                        if k < KT - 1:
                            ins.then_inc(mod_acc_step, 1)
                ins.then_inc(mod_acc_ready, 1)

            def evacuate_mod(phase, j, i):
                item = phases[phase][j]
                _, _, _, m = at(phase, j, i)
                par = (first_m[phase] + mod_number(phase, j)) % 2
                dve.wait_ge(mod_done, m + 1)
                l = item[1]
                ps = pair[3][:, 512 * par:512 * par + 4].rearrange("p (t s) -> p t s", s=2)
                base = COLS_L + L_N * l + L_MODB
                n = item[2] + (4 * i if phase == "mlp0" else 0)
                if phase == "mlp0":
                    out = modv[:, l].rearrange("p (n t) s -> p n (t s)", t=2)[:, bass.ds(n, 1), :].rearrange("p n (t s) -> p (n t) s", s=2)
                    bias = cols[:, base:base + N_MOD].rearrange("p (n t) -> p n t", t=2)[:, bass.ds(n, 1), :]
                    bias = bias.rearrange("p n (t s) -> p (n t) s", s=1)
                else:
                    out = modv[:, l, 2 * n:2 * n + 2, :]
                    bias = cols[:, base + 2 * n:base + 2 * n + 2].rearrange("p (t s) -> p t s", s=1)
                V.tensor_tensor(out, ps, bias.to_broadcast([P, 2, 2]), ALU.add).then_inc(mod_evacuated, 1)

            def run(phase, i=0):
                todo = None
                items = work[phase]
                early = None
                for n, (kind, j, *half) in enumerate(items):
                    if kind == "u":
                        split_next(split_lo, phase, n, i)
                        if todo is not None:
                            evacuate_mod(phase, todo, i)
                            todo = None
                        behind = [later[0] for later in items[n + 1:]]
                        if "s" in behind and "u" not in behind[:behind.index("s")]:
                            early = n + 1 + behind.index("s")
                            sum_mod(phase, items[early][1], i)
                        evacuate(phase, j, i, half[0])
                    elif kind == "s" and n != early:
                        sum_mod(phase, j, i)
                    elif kind in "mp":
                        if todo is not None:
                            evacuate_mod(phase, todo, i)
                        todo = j
                if todo is not None:
                    evacuate_mod(phase, todo, i)

            def norm(n, lat_only, final=False):
                t_from = CTX if lat_only else 0
                rows = slice(t_from, T)
                l, sc = n // 2, (SC_A, SC_M)[n % 2]
                if not final:
                    g = cols[:, COLS_L + L_N * l + (L_AG, L_MG)[n % 2]:][:, 0:KT].rearrange("p (k s) -> p k s", s=1)
                    dve.wait_ge(mod_evacuated, {0: 8, 1: 24, 2: 48, 3: 48}[n])
                    dve_link(V.scalar_tensor_tensor(out=gain[:], in0=modv[:, l, sc:sc + KT, :], scalar=1.0,
                                                    in1=g.to_broadcast([P, KT, 2]), op0=ALU.add, op1=ALU.mult))
                for k in range(1, KT):
                    dve.wait_ge(sem("norm_sq_ready"), KT * n + k + 1)
                    a = nsq[:, 0, rows] if k == 1 else nacc[:, rows]
                    ins = V.tensor_tensor(nacc[:, rows], a, nsq[:, k % 2, rows], ALU.add)
                    ins.then_inc(sem("norm_sq_used"), 2 if k == 1 else 1)
                    dve.wait_ge(sem("norm_sq_used"), KT * n + k + 1)
                dve.wait_ge(sem("norm_rs_ready"), n + 1)
                for k in range(KT):
                    if final:
                        if k >= 2:
                            dve.wait_ge(sem(f"out_stored{k % 2}"), 16 * (k // 2))
                        V.scalar_tensor_tensor(out=nout[:, k % 2, :], in0=xT[:, k, CTX:T],
                                               scalar=cols[:, COLS_FG + k:COLS_FG + k + 1], in1=nrs[:, CTX:T],
                                               op0=ALU.mult, op1=ALU.mult).then_inc(sem("out_ready"), 1)
                        continue
                    segs = ([] if lat_only else [(0, CTX, 1)]) + [(CTX, T, 0)]
                    if k >= 2:
                        dve.wait_ge(h_lo_ready, h_base[n] + k - 1)
                    for t0, t1, s in segs:
                        last = V.scalar_tensor_tensor(out=nsq[:, k % 2, t0:t1], in0=xT[:, k, t0:t1],
                                                      scalar=gain[:, k, s:s + 1], in1=nrs[:, t0:t1],
                                                      op0=ALU.mult, op1=ALU.mult)
                    last.then_inc(sem("norm_t_ready"), 1)
                    if k >= 1:
                        low_part(n, k - 1, segs)
                if not final:
                    low_part(n, KT - 1, segs)

            def low_part(n, k, segs):
                l, sh = n // 2, (SH_A, SH_M)[n % 2]
                dve.wait_ge(h_hi_ready, h_base[n] + k + 1)
                for t0, t1, s in segs:
                    last = V.scalar_tensor_tensor(out=h_lo[:, k, t0:t1], in0=nsq[:, k % 2, t0:t1],
                                                  scalar=modv[:, l, sh + k, s:s + 1], in1=h_hi[:, k, t0:t1].bitcast(F32),
                                                  op0=ALU.add, op1=ALU.subtract)
                last.then_inc(h_lo_ready, 1)

            h_base = {0: 0, 1: 16, 2: 24, 3: 40}

            def rotate(x, table, width, done=None):
                lat = x[:, CTX:T]
                dve_link(V.stream_shuffle(rope_sw[:], lat, shuffles[width]))
                dve_link(V.tensor_tensor(rope_t[:], lat, rope[:, table, :], ALU.mult))
                dve_link(V.tensor_tensor(rope_sw[:], rope_sw[:], rope[:, table + 1, :], ALU.mult))
                last = V.tensor_tensor(lat, rope_t[:], rope_sw[:], ALU.add)
                if done is None:
                    dve_link(last)
                else:
                    last.then_inc(done, 1)

            def scans(layer, ty):
                S = lambda name: sem(f"{name}_{layer}_{ty}")
                t_from = 0 if layer == 0 else CTX
                q, k = ((ret_q, ret_k), (gla_q, gla_k))[ty]
                if ty == 0:
                    rotate(q, 0, 8)
                    rotate(k, 0, 8)
                    for dr in range(2):
                        dve_link(V.tensor_copy(g2[:, dr], lgam[:, layer, dr:dr + 1].to_broadcast([P, T])))
                else:
                    gb = COLS_L + L_N * layer + L_GB
                    for dr in range(2):
                        dve.wait_ge(S("z_ready"), dr + 1)
                        dve_link(V.tensor_scalar(g2[:, dr], pair[2 + dr][:, 0:T], cols[:, gb + dr:gb + dr + 1], None, ALU.add))
                        V.scalar_tensor_tensor(out=bcum[:, dr], in0=g2[:, dr], scalar=-1.0, in1=g2[:, dr], op0=ALU.mult,
                                               op1=ALU.min).then_inc(S("negabs_ready"), 1)
                    for dr in range(2):
                        dve.wait_ge(S("softplus_ready"), dr + 1)
                        dve_link(V.scalar_tensor_tensor(out=g2[:, dr], in0=g2[:, dr], scalar=0.0, in1=bcum[:, dr],
                                                        op0=ALU.min, op1=ALU.subtract))
                if ty == 0:
                    dve.wait_ge(sem("scan_mask_ready"), layer + 1)
                V.tensor_tensor_scan(bcum[:, 0], scan_mask[:], g2[:, 0], 0.0, ALU.mult, ALU.add).then_inc(S("bcum_ready"), 1)
                V.tensor_tensor_scan(bcum[:, 1, ::-1], scan_mask[:], g2[:, 1, ::-1], 0.0, ALU.mult,
                                     ALU.add).then_inc(S("bcum_ready"), 1)
                qs, ks = ((1.0, KSCALE), (KSCALE, 1.0))[ty]
                for dr in range(2):
                    dve.wait_ge(S("decays_ready"), 2 * dr + 2)
                    whole = (CH - 1, 0)[dr]
                    dve_link(V.tensor_copy(decs[:, dr, :], q_dec[:, dr].rearrange("p (c i) -> p c i", i=CH)[:, :, whole]))
                    V.scalar_tensor_tensor(out=q_dec[:, dr, t_from:], in0=q[:, t_from:], scalar=qs, in1=q_dec[:, dr, t_from:],
                                           op0=ALU.mult, op1=ALU.mult)
                    dve_link(V.scalar_tensor_tensor(out=k_dec[:, dr], in0=k[:], scalar=ks, in1=k_dec[:, dr],
                                                    op0=ALU.mult, op1=ALU.mult))
                    V.tensor_tensor(bcum[:, dr].rearrange("p (c i) -> p c i", i=CH),
                                    k_dec[:, dr].rearrange("p (c i) -> p c i", i=CH),
                                    decs[:, dr, :].rearrange("p (c i) -> p c i", i=1).to_broadcast([P, NCH, CH]),
                                    ALU.mult).then_inc(S("k2_ready"), 1)
                dve.wait_ge(S("k2T_in_psum"), 1)
                V.tensor_copy(k2T[:, 0].rearrange("p t c -> p (t c)"), pair[0][:, 0:T]).then_inc(S("k2T_ready0"), 1)
                for dr in range(2):
                    dve.wait_ge(S("kv_ready"), dr + 1)
                    path = list(range(NCH)) if dr == 0 else [3, 2, 1, 0] + list(range(NCH - 1, 3, -1))
                    dve_link(V.memset(state[:, dr, path[0], :], 0.0))
                    for a, b in zip(path, path[1:]):
                        kv = pair[2 + dr][:, 512 * (a % 2) + DV * (a // 2):512 * (a % 2) + DV * (a // 2) + DV]
                        ins = V.scalar_tensor_tensor(out=state[:, dr, b, :], in0=state[:, dr, a, :],
                                                     scalar=decs[:, dr, a:a + 1], in1=kv, op0=ALU.mult, op1=ALU.add)
                        if b == path[-1]:
                            ins.then_inc(S("state_ready"), 1)
                        else:
                            dve_link(ins)
                rounds = 2 * (T - t_from) // P
                for r in range(rounds):
                    dve.wait_ge(S("scores_ready"), r + 1)
                    for dr in range(2):
                        src = pair[r % 2][:, :].rearrange("p (b c) -> p b c", b=2)[:, :, P * dr:P * dr + P]
                        msk = (mask_f, mask_b)[dr].rearrange("p (b c) -> p b c", b=1).to_broadcast([P, 2, P])
                        last = V.tensor_tensor(ptmp[:, dr], src, msk, ALU.mult)
                    dve_link(last)
                    if r >= 2:
                        dve.wait_ge(S("probs_used"), r - 1)
                    V.tensor_tensor(probs[:, r % 2], ptmp[:, 0], ptmp[:, 1], ALU.add).then_inc(S("probs_ready"), 1)
                    dve.wait_ge(S("probs_ready"), r + 1)
                    if 1 <= r <= 4:
                        hp, part = (r - 1) // 2, (r - 1) % 2
                        w = (T - t_from) // 2
                        c0 = t_from + w * part
                        e = state[:, hp].rearrange("p c e -> p (c e)")[:, c0:c0 + w]
                        gt = y[:, 2 * ty + hp, c0:c0 + w]
                        dve.wait_ge(S("gate_exp_ready"), hp + 1)
                        dve_link(V.tensor_scalar(e, e, 1.0, None, ALU.add))
                        dve_link(V.reciprocal(e, e))
                        dve_link(V.tensor_tensor(gt, gt, e, ALU.mult))
                rows = slice(t_from, T)
                if ty == 0:
                    for hp in range(2):
                        dve.wait_ge(S("stat_ready"), hp + 1)
                        V.tensor_tensor(g2[:, hp, rows], g2[:, hp, rows], pair[hp][:, rows],
                                        ALU.subtract).then_inc(S("centred_ready"), 1)
                for hp in range(2):
                    gt = y[:, 2 * ty + hp, rows]
                    dve.wait_ge(S("head_rs_ready"), hp + 1)
                    dve_link(V.tensor_tensor(gt, gt, q_dec[:, hp, rows], ALU.mult))
                    o = g2[:, hp, rows] if ty == 0 else pair[2 + hp][:, rows]
                    last = V.tensor_tensor(gt, gt, o, ALU.mult)
                last.then_inc(sem(f"y_done_{layer}_{ty}"), 1)
                dve.wait_ge(sem(f"y_done_{layer}_{ty}"), 1)

            def attention(layer):
                S = lambda name: sem(name)
                for n in range(5):
                    x = y[:, 3 + n] if n else att_k[:]
                    gc = COLS_L + L_N * layer + (L_QG if n else L_KG)
                    dve.wait_ge(S("qrs_ready"), before(layer, "qrs_ready") + n + 1)
                    t0 = CTX * layer if n else 0
                    ins = V.scalar_tensor_tensor(out=x[:, t0:], in0=x[:, t0:], scalar=cols[:, gc:gc + 1],
                                                 in1=qrs[:, n % 2, t0:], op0=ALU.mult, op1=ALU.mult)
                    ins.then_inc(S("qrs_used"), 1)
                    dve.wait_ge(S("qrs_used"), before(layer, "qrs_used") + n + 1)
                    done = S("q_ready" if n else "k_ready")
                    rotate(x, 2, 16, done)
                    dve.wait_ge(done, before(layer, "q_ready") + n if n else layer + 1)
                dve.wait_ge(S("kk_hi_ready"), before(layer, "kk_hi_ready") + 1)
                for kv in range(2):
                    src = slice(64 * kv, 64 * kv + 64)
                    for half in range(2):
                        last = V.tensor_tensor(kk_lo[64 * half:64 * half + 64, kv], att_k[src], kk_hi[src, kv].bitcast(F32),
                                               ALU.subtract)
                last.then_inc(S("kk_lo_ready"), 1)
                items = attention_items(layer)
                per = len(items) // 4

                def split_q(p):
                    dve.wait_ge(S("qq_hi_ready"), before(layer, "qq_hi_ready") + p + 1)
                    for half in range(2):
                        rows, other = slice(64 * half, 64 * half + 64), slice(64 - 64 * half, 128 - 64 * half)
                        last = V.tensor_tensor(qq[other, p % 2, half, CTX * layer:], y[rows, 4 + p, CTX * layer:],
                                               qq[rows, p % 2, half, CTX * layer:].bitcast(F32), ALU.subtract)
                    last.then_inc(S("qq_lo_ready"), 1)

                def largest(n):
                    dve.wait_ge(S("att_scores_ready"), before(layer, "att_scores_ready") + n + 1)
                    width = QB * items[n][2]
                    V.tensor_reduce(mx[:, n % 2], score_place(n)[:, 0:width].rearrange("p (k q) -> p q k", q=QB), AX.X,
                                    ALU.max).then_inc(S("mx_ready"), 1)

                def negate_max(n):
                    dve.wait_ge(S("mx_turned"), before(layer, "mx_turned") + n + 1)
                    top = small[:, 2 * (n % 2):2 * (n % 2) + 2]
                    dve_link(V.tensor_reduce(top, psum[:, MAX_BANK:MAX_BANK + 2 * P].rearrange("p (i k) -> p i k", i=2),
                                             AX.X, ALU.max))
                    if n >= 2:
                        dve.wait_ge(S("shifted"), before(layer, "shifted") + n - 1)
                    for i in range(2):
                        last = V.tensor_scalar(neg_diag[:, n % 2, P * i:P * (i + 1)], ident, top[:, i:i + 1], -1.0,
                                               ALU.mult, ALU.mult)
                    last.then_inc(S("neg_diag_ready"), 1)

                def take_out(n):
                    h, b, _ = items[n]
                    dst = y[64 * (h % 2):64 * (h % 2) + 64, 4 + h // 2, b * QB:(b + 1) * QB]
                    dve.wait_ge(S("att_out_ready"), before(layer, "att_out_ready") + n + 1)
                    V.tensor_copy(dst, psum[0:HD, OUT_BANK:OUT_BANK + QB]).then_inc(S("out_read"), 1)
                    dve.wait_ge(S("out_read"), before(layer, "out_read") + n + 1)
                    dve.wait_ge(S("rsum_ready"), before(layer, "rsum_ready") + n + 1)
                    V.tensor_tensor(dst, dst, rsum[:, n % 2], ALU.mult).then_inc(S("y_att_ready"), 1)

                split_q(0)
                largest(0)
                for n in range(len(items) + 2):
                    if n < len(items):
                        negate_max(n)
                    if n + 1 < len(items):
                        largest(n + 1)
                    if n >= 2:
                        take_out(n - 2)
                    if n % per == 1 and n // per + 1 < HQ // 2:
                        split_q(n // per + 1)
                dve.wait_ge(S("y_att_ready"), before(layer, "y_att_ready") + len(items))

            def split_y(layer):
                t_from = 0 if layer == 0 else CTX
                for k in range(KT):
                    dve.wait_ge(h_hi_ready, (8, 32)[layer] + k + 1)
                    V.tensor_tensor(h_lo[:, k, t_from:], y[:, k, t_from:], h_hi[:, k, t_from:].bitcast(F32),
                                    ALU.subtract).then_inc(h_lo_ready, 1)

            V.memset(small[:], 0.0).then_inc(sem("small_clear"), 1)
            dve.wait_ge(sem("small_clear"), 1)
            dve.wait_ge(cols_ready, 32)
            for l in range(DEPTH):
                rd = COLS_L + L_N * l + L_RD
                last = V.scalar_tensor_tensor(out=small[:, 2 * l:2 * l + 2], in0=cols[:, rd:rd + 2], scalar=-1.0,
                                              in1=cols[:, rd:rd + 2], op0=ALU.mult, op1=ALU.min)
            last.then_inc(sem("ln_first"), 1)
            dve.wait_ge(sem("exp_c_ready"), 1)
            dve_link(V.tensor_scalar(silu_c[:], silu_c[:], 1.0, None, ALU.add))
            dve_link(V.reciprocal(silu_c[:], silu_c[:]))
            V.tensor_tensor(silu_c[:], silu_c[:], cols[:, 0:16].rearrange("p (k s) -> p k s", s=2),
                            ALU.mult).then_inc(sem("silu_c_ready"), 1)
            dve.wait_ge(sem("lgam_softplus"), 1)
            for l in range(DEPTH):
                rd = COLS_L + L_N * l + L_RD
                dve_link(V.scalar_tensor_tensor(out=lgam[:, l, :], in0=cols[:, rd:rd + 2], scalar=0.0, in1=lgam[:, l, :],
                                                op0=ALU.min, op1=ALU.subtract))
            run("start")
            split_lo("in0", first_weights("in0"), 0, 0)
            norm(0, False)
            dve.wait_ge(consts_ready, 32)
            for layer in range(DEPTH):
                run(f"in{layer}")
                dve.wait_ge(unit_evacuated, 2 * first_w[f"in{layer}"] + 20)
                scans(layer, 0)
                scans(layer, 1)
                attention(layer)
                split_y(layer)
                dve.wait_ge(mod_evacuated, (24, 48)[layer])
                run(f"out{layer}")
                norm(2 * layer + 1, layer == 1)
                with dve.Fori(0, NFG - 1) as i:
                    run(f"mlp{layer}", i)
                run(f"mlp{layer}", NFG - 1)
                norm(2 * layer + 2, layer == 1, final=(layer == 1))

        @block.gpsimd
        def _(pool):
            for layer in range(DEPTH):
                pool.wait_ge(h_lo_ready, (KT, 4 * KT)[layer])
                nc.gpsimd.memset(s_diag[:], 0.0).then_inc(sem("s_diag_clear"), 1)
                pool.wait_ge(sem("s_diag_clear"), layer + 1)
                pool.wait_ge(unit_done, 2 * first_w[f"in{layer}"] + 20)
                nc.gpsimd.memset(scan_mask[:], 1.0).then_inc(sem("scan_mask_filled"), 1)
                pool.wait_ge(sem("scan_mask_filled"), layer + 1)
                nc.gpsimd.memset(scan_mask.rearrange("p (c i) -> p c i", i=CH)[:, :, 0], 0.0).then_inc(sem("scan_mask_ready"), 1)
                for ty in range(2):
                    for dr in range(2):
                        pool.wait_ge(sem(f"state_ready_{layer}_{ty}"), dr + 1)
                        place_states(nc.gpsimd.tensor_copy, 3, dr).then_inc(sem(f"s_diag_ready_{layer}_{ty}"), 1)
                pool.wait_ge(sem(f"y_done_{layer}_1"), 1)
                nc.gpsimd.memset(v_ones[:, :, :, HD:P], 1.0).then_inc(sem("v_ones_set"), 1)


def kernel(**inputs):
    import numpy as np
    import concourse.bacc as bacc
    from concourse import mybir
    from concourse.bass_utils import run_bass_kernel_spmd as run

    a = {k: np.asarray(v) for k, v in inputs.items()}
    f = np.float32

    def tiles(m):
        return np.ascontiguousarray(m.reshape(KT, P, -1).transpose(1, 0, 2))

    def slabs(w, groups):
        lead, cols = w.shape[:-2], w.shape[-1]
        w = w.reshape(lead + (groups, KT, P, cols // SLAB, SLAB))
        n = len(lead)
        w = w.transpose(tuple(range(n + 1)) + (n + 3, n + 2, n + 1, n + 4))
        return np.ascontiguousarray(w).reshape(lead + (groups, cols // SLAB, P, KT * SLAB))

    arrays = {}
    arrays["xT"] = tiles(np.concatenate([a["ctx"][0], a["x"][0]], axis=0).T)
    arrays["mod_w"] = slabs(a["mod_w"], 1)[:, 0]
    arrays["w_out"] = slabs(a["w_out"], 1)[:, 0]
    w1 = a["mlp_w1"].reshape(DEPTH, D, NFG, D).transpose(0, 2, 1, 3)
    arrays["w_1"] = slabs(w1, 1)[:, :, 0].reshape(DEPTH * NFG, 4, P, KT * SLAB)
    arrays["w_2"] = slabs(a["mlp_w2"], NFG).reshape(DEPTH * NFG, 4, P, KT * SLAB)
    win = a["w_in"].reshape(DEPTH, KT, P, W_IN).transpose(0, 2, 1, 3)
    arrays["w_in"] = np.concatenate([win[..., c:c + w].reshape(DEPTH, P, KT * w) for c, w in sorted(W_IN_SLABS)], axis=2)

    def col(v):
        return v.reshape(-1, P).T
    parts = [np.stack([col(a["c"][0]), col(a["c_ctx"])], axis=2).reshape(P, 2 * KT), col(a["final_norm_g"])]
    for l in range(DEPTH):
        parts += [col(a["mod_b"][l]), col(a["attn_norm_g"][l]), col(a["mlp_norm_g"][l]),
                  np.tile(a["qk_norm_g"][l, 0], 2)[:, None], np.tile(a["qk_norm_g"][l, 1], 2)[:, None],
                  a["gla_gate_b"][l].T, np.repeat(a["ret_decay_logit"][l].T, DK, axis=0)]
    arrays["cols"] = np.ascontiguousarray(np.concatenate(parts, axis=1))
    gw = np.zeros((32, DEPTH, 2, P), f)
    gw[0:16, :, 0] = a["gla_gate_w"][:, 0].transpose(1, 0, 2)
    gw[16:32, :, 1] = a["gla_gate_w"][:, 1].transpose(1, 0, 2)
    arrays["gate_w"] = gw

    tok = np.arange(LAT)
    row, column = (tok // 64).astype(f), (tok % 64).astype(f)
    table = np.zeros((P, 4, LAT), f)
    for n, width in ((0, 8), (2, 16)):
        freq = (f(10000.0) ** (-np.arange(width, dtype=f) / f(width))).astype(f)
        for p in range(P):
            q = p % (4 * width)
            ang = (row if q < 2 * width else column) * freq[q % width]
            table[p, n] = np.cos(ang)
            table[p, n + 1] = np.sin(ang) * (-1 if q % (2 * width) < width else 1)
    arrays["rope"] = table
    i, j = np.meshgrid(np.arange(P), np.arange(P), indexing="xy")
    same = i // CH == j // CH
    arrays["squares"] = np.ascontiguousarray(np.stack(
        [same & (j <= i), same & (j > i), i == j, np.ones((P, P)), (i // 64 == j // 64) / 64.0], axis=1).astype(f))

    nc = bacc.Bacc("TRN2", target_bir_lowering=False, num_devices=1)
    drams = {k: nc.dram_tensor(f"in_{k}", v.shape, mybir.dt.float32, kind="ExternalInput").ap() for k, v in arrays.items()}
    drams["out"] = nc.dram_tensor("out", (P, KT, LAT), mybir.dt.float32, kind="ExternalOutput").ap()
    build(nc, drams)
    r = run(nc, [{f"in_{k}": v for k, v in arrays.items()}], core_ids=[0])
    return r.results[0]["out"].transpose(2, 1, 0).reshape(1, LAT, D)
```

```python
from contextlib import ExitStack

import concourse.bass as bass
from concourse import mybir

F32 = mybir.dt.float32
F32R = mybir.dt.float32r
ALU = mybir.AluOpType
ACT = mybir.ActivationFunctionType
AX = mybir.AxisListType

P = 128
D = 1024
KT = D // P
CTX, LAT = 256, 512
T = CTX + LAT
TT = T // P
DEPTH = 2
CH = 64
NCH = T // CH
FF = 4 * D
NFG = FF // D
EPS = 1e-6
RING = 4
SLAB = 256
DK, DV = 32, 64
HD = 64
HQ = 8
QB = 256
KSCALE = DK ** -0.5
TAU = 16.0
W_IN = 2336
W_IN_SLABS = [(256, 256), (1024, 256), (2080, 256), (1568, 256), (1824, 256), (0, 256), (768, 256), (512, 256),
              (1280, 256), (1536, 32)]
(RET_V, GLA_V, ATT_KV, ATT_Q01, ATT_Q23, RET_QK, GLA_QK, RET_G, GLA_G, GLA_LOW) = range(10)
N_MOD = 6 * D // P
SH_A, SC_A, GT_A, SH_M, SC_M, GT_M = (KT * i for i in range(6))

COLS_C = 0
COLS_FG = 16
COLS_L = 24
L_MODB, L_AG, L_MG, L_QG, L_KG, L_GB, L_RD, L_N = 0, 48, 56, 64, 65, 66, 68, 70


def layer_program():
    win = [("w", "in", s) for s in range(len(W_IN_SLABS))]
    phases = {}
    phases["start"] = [("pm"[n % 2], 0, n) for n in range(8)]
    rest = [("m", 0, n) for n in range(8, 20)]
    mixed = []
    for s, take in enumerate((1, 2, 2, 0, 0, 2, 2, 2, 1, 0)):
        ahead = 1 if s and take else 0
        mixed += rest[:ahead] + [win[s]] + rest[ahead:take]
        rest = rest[take:]
    assert not rest
    phases["in0"] = mixed
    phases["prep0"] = [("p", 0, 20 + n) for n in range(2)]
    w = [("w", "out", s) for s in range(4)]
    m = [("m", 0, 22), ("m", 0, 23)] + [("m", 1, n) for n in range(4)]
    phases["out0"] = [w[0], m[0], m[1], w[1], m[2], m[3], w[2], m[4], m[5], w[3]]
    phases["mlp0"] = []
    for matrix in "12":
        w1 = [("w", matrix, s) for s in range(4)]
        m1 = [("m", 1, 4 + 2 * (matrix == "2") + s) for s in range(2)]
        phases["mlp0"] += [w1[0], m1[0], w1[1], w1[2], m1[1], w1[3]]
    phases["in1"] = win[:RET_QK]
    for s in range(4):
        phases["in1"] += [win[RET_QK + s], ("m", 1, 20 + s)]
    phases["in1"].append(win[GLA_LOW])
    phases["out1"] = w
    phases["mlp1"] = [("w", "1", s) for s in range(4)] + [("w", "2", s) for s in range(4)]
    return phases


def units_of(item):
    return 1 if item[1:] == ("in", GLA_LOW) else 2


def work_items(slabs):
    out, seen, summed, values, normed = [], [], [], [], []
    made = 0
    for j, item in enumerate(slabs):
        if item[0] == "p":
            out += [("s", j + 1), ("p", j), ("m", j + 1)] if slabs[j + 1:] and slabs[j + 1][0] == "m" else [("p", j)]
        elif item[0] == "m":
            if not (j and slabs[j - 1][0] == "p") and ("s", j) not in out:
                seen.append(j)
        else:
            for half in range(units_of(item)):
                out.append(("u", j, half))
                if values:
                    out.append(("t", values.pop()))
                if normed:
                    out.append(("a", normed.pop()))
                if item[1] == "in" and item[2] in (ATT_Q01, ATT_Q23) or item[1:] == ("in", ATT_KV) and half == 0:
                    normed.append({ATT_KV: 0, ATT_Q01: 1 + half, ATT_Q23: 3 + half}[item[2]])
                if item[1] == "in" and (item[2] in (RET_V, GLA_V) or (item[2], half) == (ATT_KV, 1)):
                    values.append(made)
                    made += 1
                out += [("m", summed.pop())] if summed else []
                if half == 1 and not seen and slabs[j + 1:] and slabs[j + 1][0] == "m":
                    seen.append(j + 1)
                if seen:
                    summed.append(seen.pop(0))
                    out.append(("s", summed[0]))
    for j in seen:
        out += [("m", k) for k in summed] + [("s", j)]
        summed = [j]
    return out + [("m", k) for k in summed]


def build(nc, d):
    phases = layer_program()
    order = ["start", "in0", "prep0", "out0", "mlp0", "in1", "out1", "mlp1"]
    repeats = {p: NFG if p.startswith("mlp") else 1 for p in order}
    first_slab, first_w, first_m = {}, {}, {}
    ns = nw = nm = 0
    is_mod = lambda s: s[0] != "w"
    for p in order:
        first_slab[p], first_w[p], first_m[p] = ns, nw, nm
        ns += repeats[p] * len(phases[p])
        nw += repeats[p] * sum(s[0] == "w" for s in phases[p])
        nm += repeats[p] * sum(is_mod(s) for s in phases[p])
    flat = [s[0] for p in order for _ in range(repeats[p]) for s in phases[p]]

    ctx = ExitStack()
    with ctx:
        def sb(name, shape, dt=F32, stack=ctx):
            return stack.enter_context(nc.sbuf_tensor(name, shape, dt))

        sems = {}

        def sem(name):
            if name not in sems:
                sems[name] = ctx.enter_context(nc.semaphore(name))
            return sems[name]

        xT = sb("xT", [P, KT, T])
        raw = sb("raw", [P, RING, KT, SLAB])
        w_hi = sb("w_hi", [P, 2, KT, P], F32R)
        w_lo = sb("w_lo", [P, 2, KT, P], F32R)
        rope = sb("rope", [P, 4, LAT])
        squares = sb("squares", [P, 5, P])
        cols = sb("cols", [P, COLS_L + DEPTH * L_N])
        gate_w = sb("gate_w", [32, DEPTH, 2, P])
        modv = sb("modv", [P, DEPTH, N_MOD, 2])
        silu_c = sb("silu_c", [P, KT, 2])
        gain = sb("gain", [P, KT, 2])
        lgam = sb("lgam", [P, DEPTH, 2])
        small = sb("small", [P, 4])
        mod_acc = sb("mod_acc", [P, 2, 2, SLAB])
        ones_r = sb("ones_r", [P, P], F32R)
        decs = sb("decs", [P, 2, NCH])
        with ExitStack() as own:
            nsq = sb("nsq", [P, 2, T], F32, own)
            nacc = sb("nacc", [P, T], F32, own)
            nrs = sb("nrs", [P, T], F32, own)
        s_diag = sb("s_diag", [P, 2, NCH, 2 * DV])
        mask_f, mask_b, ident, ones, blocks = (squares[:, i, :] for i in range(5))

        with ExitStack() as own:
            g2 = sb("g2", [P, 2, T], F32, own)
            bcum = sb("bcum", [P, 2, T], F32, own)
            q_dec = sb("q_dec", [P, 2, T], F32, own)
            k_dec = sb("k_dec", [P, 2, T], F32, own)
            k2T = sb("k2T", [P, 2, TT, P], F32, own)
            state = sb("state", [P, 2, NCH, DV], F32, own)
            probs = sb("probs", [P, 2, 2, P], F32, own)
            ptmp = sb("ptmp", [P, 2, 2, P], F32, own)
            scan_mask = sb("scan_mask", [P, T], F32, own)
        with ExitStack() as own:
            mx = sb("mx", [P, 2, QB], F32, own)
            neg_diag = sb("neg_diag", [P, 2, QB], F32R, own)
            pexp = sb("pexp", [P, 2, TT * QB], F32, own)
            kk_hi = sb("kk_hi", [P, 2, T], F32R, own)
            kk_lo = sb("kk_lo", [P, 2, T], F32R, own)
            qq = sb("qq", [P, 2, 2, T], F32R, own)
            v_ones = sb("v_ones", [P, TT, 2, P], F32, own)
            rsum = sb("rsum", [HD, 2, QB], F32, own)
        h_hi = sb("h_hi", [P, KT, T], F32R)
        h_lo = sb("h_lo", [P, KT, T], F32R)
        with ExitStack() as own:
            u_hi = sb("u_hi", [P, KT, T], F32R, own)
            u_lo = sb("u_lo", [P, KT, T], F32R, own)
            u_full = sb("u_full", [P, 2, T], F32, own)
        with ExitStack() as own:
            nout = sb("nout", [P, 2, LAT], F32, own)
        ret_q = sb("ret_q", [P, T])
        ret_k = sb("ret_k", [P, T])
        gla_q = sb("gla_q", [P, T])
        gla_k = sb("gla_k", [P, T])
        low = sb("low", [32, T])
        ret_v = sb("ret_v", [P, TT, 256])
        gla_v = sb("gla_v", [P, TT, 256])
        att_v = sb("att_v", [P, TT, P])
        att_k = sb("att_k", [P, T])
        y = sb("y", [P, 8, T])

        psum = ctx.enter_context(nc.psum_tensor("psum", [P, 8 * 512], F32))
        pair = [psum[:, 1024 * i:1024 * (i + 1)] for i in range(4)]

        raw_ready = [sem(f"raw_ready{i}") for i in range(RING)]
        cols_ready, consts_ready, x_ready = sem("cols_ready"), sem("consts_ready"), sem("x_ready")
        w_hi_ready, w_lo_ready = sem("w_hi_ready"), sem("w_lo_ready")
        unit_done, unit_evacuated = sem("unit_done"), sem("unit_evacuated")
        mod_done, mod_evacuated = sem("mod_done"), sem("mod_evacuated")
        mod_acc_ready, mod_acc_step = sem("mod_acc_ready"), sem("mod_acc_step")
        h_hi_ready, h_lo_ready = sem("h_hi_ready"), sem("h_lo_ready")
        relu_ready, u_hi_ready, u_lo_ready = sem("relu_ready"), sem("u_hi_ready"), sem("u_lo_ready")
        dve_step, act_step = sem("dve_step"), sem("act_step")
        steps = {"dve": 0, "act": 0}

        def dve_link(ins):
            steps["dve"] += 1
            ins.then_inc(dve_step, 1)
            nc.vector.wait_ge(dve_step, steps["dve"])

        def act_link(ins):
            steps["act"] += 1
            ins.then_inc(act_step, 1)
            nc.scalar.wait_ge(act_step, steps["act"])

        def at(phase, j, i):
            n = first_slab[phase] + j
            per = len(phases[phase])
            kinds = [s[0] for s in phases[phase]]
            assert repeats[phase] == 1 or per % RING == 0
            per_w = kinds.count("w")
            w = first_w[phase] + kinds[:j].count("w") + i * per_w
            m = first_m[phase] + j - kinds[:j].count("w") + i * (per - per_w)
            return n % RING, 16 * (n // RING + 1) + 16 * (per // RING) * i, 2 * w, m

        units_before_norm = {1: 2 * first_w["mlp0"], 2: 2 * first_w["in1"], 3: 2 * first_w["mlp1"],
                             4: 2 * (first_w["mlp1"] + 8 * NFG)}

        def cuts(t_from):
            return ((t_from, 512 - t_from), (512, T - 512))

        def spans(layer, item, half):
            if layer == 1 and not (item[1] == "in" and (item[2], half) in CTX_UNITS):
                return [(CTX, LAT, 0)]
            return [(0, 512, 0), (512, 256, 512)]

        CTX_UNITS = {(RET_V, 0), (RET_V, 1), (RET_QK, 1), (GLA_V, 0), (GLA_V, 1), (GLA_QK, 1), (GLA_LOW, 0), (ATT_KV, 0),
                     (ATT_KV, 1)}
        value_place = [0, 1, 2, 3, 3]
        turned = [ret_v[:, :, 0:P], ret_v[:, :, P:2 * P], gla_v[:, :, 0:P], gla_v[:, :, P:2 * P], att_v[:]]
        work = {p: work_items(phases[p]) for p in order}

        OUT_BANK, MAX_BANK = 6 * 512, 7 * 512

        def score_place(n):
            return psum[:, 3 * 512 * (n % 2):3 * 512 * (n % 2 + 1)]

        def attention_items(layer):
            return [(h, b, CTX // P if b == 0 else TT) for p in range(HQ // 2) for b in range(layer, T // QB)
                    for h in (2 * p, 2 * p + 1)]

        def before(layer, name):
            per_layer = {"qsq_ready": 5, "qsum_ready": 5, "qrs_ready": 5, "qrs_used": 5, "q_ready": 4, "qq_hi_ready": 4,
                         "qq_lo_ready": 4, "k_ready": 1, "kk_hi_ready": 1, "kk_lo_ready": 1, "v_ones_ready": 1}
            return layer * per_layer.get(name, len(attention_items(0)))

        def ahead(kind, phase, j, i):
            return flat[:first_slab[phase] + j].count(kind) + i * [s[0] for s in phases[phase]].count(kind)

        def joint_units(phase, i):
            return phase.startswith("in") or phase.startswith("mlp") and isinstance(i, int) and i == 0

        def norm_fed(phase, item, i):
            if item[1] == "out":
                return 2 * int(phase[-1]) + 1
            if item[1] == "2" and isinstance(i, int) and i == NFG - 1:
                return 2 * int(phase[-1]) + 2
            return None

        def behind_norm(split, n):
            phase = ("in0", "mlp0", "in1", "mlp1", None)[n]
            if phase is not None:
                for half in ((0, 1) if n == 0 else (1,)):
                    split(phase, first_weights(phase), 0, half)

        def first_weights(phase):
            return [s[0] for s in phases[phase]].index("w")

        def split_next(split, phase, n, i):
            if joint_units(phase, i):
                second = [m for m, o in enumerate(work[phase]) if o[0] == "u"][1]
                if n == second:
                    return
                n = max(n, second)
            later = [o for o in work[phase][n + 1:] if o[0] == "u"]
            if later:
                split(phase, later[0][1], i, later[0][2])
            elif repeats[phase] > 1 and not (isinstance(i, int) and i == repeats[phase] - 1):
                split(phase, first_weights(phase), i + 1, 0)
            elif phase != "in0" and order.index(phase) + 1 < len(order):
                following = order[order.index(phase) + 1]
                split(following, first_weights(following), 0, 0)

        def place_states(copy, h, dr):
            rows = slice(32 * h, 32 * h + 32)
            return copy(s_diag[rows, dr, :, DV * (h % 2):DV * (h % 2) + DV], state[rows, dr])

        def normed_tile(layer, n):
            p = f"in{layer}"
            j = phases[p].index(("w", "in", (ATT_KV, ATT_Q01, ATT_Q01, ATT_Q23, ATT_Q23)[n]))
            return (y[:, 3 + n] if n else att_k[:]), (CTX * layer if n else 0), at(p, j, 0)[2] + (0, 0, 1, 0, 1)[n]

        def value_unit(layer, n):
            p = f"in{layer}"
            j = phases[p].index(("w", "in", (RET_V, RET_V, GLA_V, GLA_V, ATT_KV)[n]))
            return at(p, j, 0)[2] + (0, 1, 0, 1, 1)[n]

        def mod_number(phase, j):
            return j - [s[0] for s in phases[phase]][:j].count("w")

        block = ctx.enter_context(nc.Block())

        @block.sync
        def _(sp):
            sp.dma_start(cols[:], d["cols"]).then_inc(cols_ready, 16)
            sp.dma_start(squares[:], d["squares"]).then_inc(cols_ready, 16)

            def load(phase, j, i):
                item = phases[phase][j]
                slot, _, _, _ = at(phase, j, i)
                n = first_slab[phase] + j
                if n >= RING:
                    used = lambda kind, r: flat[:n + r * len(phases[phase]) - RING + 1].count(kind)
                    if isinstance(i, int):
                        before, step = {kind: used(kind, i) for kind in "wmp"}, {kind: 0 for kind in "wmp"}
                    else:
                        step = {kind: used(kind, 2) - used(kind, 1) for kind in "wmp"}
                        before = {kind: used(kind, 1) - step[kind] for kind in "wmp"}
                    waits = [(sm, each * before[kind] + each * step[kind] * i)
                             for sm, each, kind in ((mod_acc_ready, 1, "m"), (w_lo_ready, 2, "w")) if before[kind]]
                    if before["p"]:
                        last = [m for m, kind in enumerate(k for k in flat if k != "w") if kind == "p"][before["p"] - 1]
                        waits.append((mod_done, last + 1))
                layer = int(phase[-1]) if phase != "start" else 0
                dst = raw[:, slot].rearrange("p k c -> p (k c)")
                if item[0] != "w":
                    src = d["mod_w"][item[1], item[2] + (4 * i if phase == "mlp0" else 0)]
                elif item[1] == "in":
                    c0, wd = W_IN_SLABS[item[2]]
                    dst, src = dst[:, 0:KT * wd], d["w_in"][layer, :, KT * c0:KT * (c0 + wd)]
                elif item[1] == "out":
                    src = d["w_out"][layer, item[2]]
                else:
                    src = d["w_" + item[1]][layer * NFG + i, item[2]]
                if not isinstance(i, int):
                    for _, value in waits:
                        if not isinstance(value, int):
                            sp.compute_val(value)
                    sp.compute_val(src.offset * 4)
                if n >= RING:
                    for sm, value in waits:
                        sp.wait_ge(sm, value)
                sp.dma_start(dst, src).then_inc(raw_ready[slot], 16)

            for p in order:
                if repeats[p] > 1:
                    for j in range(len(phases[p])):
                        load(p, j, 0)
                    with sp.Fori(1, repeats[p]) as i:
                        for j in range(len(phases[p])):
                            load(p, j, i)
                else:
                    for j in range(len(phases[p])):
                        load(p, j, 0)
                        if p == "start" and j == 5:
                            sp.dma_start(xT[:], d["xT"]).then_inc(x_ready, 16)
                        if p == "in0" and j == 2:
                            sp.dma_start(gate_w[:], d["gate_w"]).then_inc(consts_ready, 16)
                            sp.dma_start(rope[:], d["rope"]).then_inc(consts_ready, 16)
            for k in range(KT):
                sp.wait_ge(sem("out_ready"), k + 1)
                sp.dma_start(d["out"][:, k, :], nout[:, k % 2, :]).then_inc(sem(f"out_stored{k % 2}"), 16)
            sp.wait_ge(sem("out_stored0"), 16 * KT // 2)
            sp.wait_ge(sem("out_stored1"), 16 * KT // 2)

        @block.tensor
        def _(pe):
            mm = nc.tensor.matmul

            def mod_slab(phase, j, i):
                slot, ready, _, m = at(phase, j, i)
                kind = phases[phase][j][0]
                if phase == "start" and j == 0:
                    pe.wait_ge(sem("silu_c_ready"), 1)
                if kind == "p":
                    pe.wait_ge(raw_ready[slot], ready)
                if phase != "start" or j >= 2:
                    pe.wait_ge(mod_evacuated, m - 1)
                par = (first_m[phase] + mod_number(phase, j)) % 2
                if kind == "m":
                    pe.wait_ge(mod_acc_ready, ahead("m", phase, j, i) + 1)
                    acc = mod_acc[:, ahead("m", phase, j, 0) % 2]
                    for t in range(2):
                        for s in range(2):
                            last = mm(pair[3][:, 512 * par + 2 * t + s:512 * par + 2 * t + s + 1],
                                      acc[:, s, t * P:(t + 1) * P], ones[:, 0:1], start=True, stop=True)
                    last.then_inc(mod_done, 1)
                    return
                for t in range(2):
                    o = pair[3][:, 512 * par + 2 * t:512 * par + 2 * t + 2]
                    for k in range(KT):
                        last = mm(o, raw[:, slot, k, t * P:(t + 1) * P], silu_c[:, k, :], start=(k == 0), stop=(k == KT - 1))
                last.then_inc(mod_done, 1)

            def unit(phase, j, i, halves, first):
                item = phases[phase][j]
                layer = int(phase[-1])
                _, _, u, _ = at(phase, j, i)
                u = u + halves[0]
                pe.wait_ge(w_lo_ready, u + len(halves))
                if not (phase == "in0" and item[2] == 0):
                    pe.wait_ge(unit_evacuated, u - 2 + len(halves))
                a_hi, a_lo = (u_hi, u_lo) if item[1] == "2" else (h_hi, h_lo)
                m = 32 if units_of(item) == 1 else P
                for k in range(KT):
                    if first:
                        if item[1] == "2":
                            pe.wait_ge(u_lo_ready, (KT * NFG * layer + k + 1) + KT * i)
                        else:
                            pe.wait_ge(h_lo_ready, KT * h_count[phase] + k + 1)
                    for half in halves:
                        for n, (w, a) in enumerate(((w_hi, a_hi), (w_hi, a_lo), (w_lo, a_hi))):
                            for t0, width, c0 in spans(layer, item, half):
                                last = mm(pair[half][0:m, c0:c0 + width], w[:, half, k, 0:m], a[:, k, t0:t0 + width],
                                          start=(k == 0 and n == 0), stop=(k == KT - 1 and n == 2))
                        if k == KT - 1:
                            last.then_inc(unit_done, 2 if units_of(item) == 1 else 1)

            h_count = {"in0": 0, "out0": 1, "mlp0": 2, "in1": 3, "out1": 4, "mlp1": 5}

            def turn_values(layer, n):
                u_made = value_unit(layer, n)
                pe.wait_ge(unit_evacuated, u_made + 1)
                if n or layer:
                    pe.wait_ge(sem("values_copied"), 5 * layer + n)
                if n == 4:
                    pe.wait_ge(sem("qrs_ready"), before(layer, "qrs_ready") + 1)
                for t in range(TT):
                    last = nc.tensor.transpose(pair[2][:, t * P:(t + 1) * P], y[:, value_place[n], t * P:(t + 1) * P], ident)
                last.then_inc(sem("values_turned"), 1)

            def head_sums(layer, n):
                pe.wait_ge(sem("qsq_ready"), before(layer, "qsq_ready") + n + 1)
                pe.wait_ge(sem("values_copied"), 5 * layer + (5 if n else 4))
                if n:
                    pe.wait_ge(sem("qrs_ready"), before(layer, "qrs_ready") + n)
                for t0, width in cuts(normed_tile(layer, n)[1]):
                    last = mm(pair[2][:, t0:t0 + width], blocks, nsq[:, 0, t0:t0 + width], start=True, stop=True)
                last.then_inc(sem("qsum_ready"), 1)

            def products(phase, i=0):
                joint = joint_units(phase, i)
                for kind, j, *half in work[phase]:
                    if kind == "t":
                        turn_values(int(phase[-1]), j)
                    elif kind == "u":
                        first = phases[phase][j][2] == 0
                        if first and joint:
                            if half[0] == 0:
                                unit(phase, j, i, (0, 1), True)
                        else:
                            unit(phase, j, i, half, first and half[0] == 0)
                    elif kind == "a":
                        head_sums(int(phase[-1]), j)
                    elif kind != "s":
                        mod_slab(phase, j, i)

            def norm_sum(n):
                pe.wait_ge(sem("norm_sq_used"), KT * (n + 1))
                for t0, width in cuts(CTX if n >= 3 else 0):
                    last = mm(pair[2][:, t0:t0 + width], ones, nacc[:, t0:t0 + width], start=True, stop=True)
                last.then_inc(sem("norm_sum_ready"), 1)

            def scans(layer, ty):
                S = lambda name: sem(f"{name}_{layer}_{ty}")
                v = (ret_v, gla_v)[ty]
                first = 0 if layer == 0 else CTX // P
                if ty == 0:
                    pe.wait_ge(unit_evacuated, 2 * first_w[f"in{layer}"] + 20)
                    pe.wait_ge(sem("values_copied"), 5 * (layer + 1))
                    pe.wait_ge(sem("qrs_ready"), before(layer, "qrs_ready") + 5)
                    for dr in range(2):
                        for t0, width in ((0, 512), (512, 256)):
                            last = mm(pair[2 + dr][:, t0:t0 + width], gate_w[:, layer, dr, :], low[:, t0:t0 + width],
                                      start=True, stop=True)
                        last.then_inc(sem("z_ready"), 1)
                else:
                    pe.wait_ge(sem(f"y_done_{layer}_0"), 1)
                    if layer == 0:
                        mod_slab("prep0", 0, 0)
                for dr in range(2):
                    pe.wait_ge(S("k2_ready"), dr + 1)
                    for t in range(TT):
                        last = nc.tensor.transpose(pair[dr][:, t * P:(t + 1) * P], bcum[:, dr, t * P:(t + 1) * P], ident)
                    last.then_inc(S("k2T_in_psum"), 1)
                for dr in range(2):
                    pe.wait_ge(S(f"k2T_ready{dr}"), 1)
                    if ty == 0:
                        pe.wait_ge(sem("z_kept"), 2 * layer + dr + 1)
                    elif layer == 0 and dr == 1:
                        pe.wait_ge(mod_evacuated, first_m["prep0"] + 1)
                    for c in range(NCH):
                        r0 = CH * (c % 2)
                        for h in range(4):
                            o = pair[2 + dr][32 * h:32 * h + 32, 512 * (c % 2) + DV * (c // 2):512 * (c % 2) + DV * (c // 2) + DV]
                            last = mm(o, k2T[r0:r0 + CH, dr, c // 2, 32 * h:32 * h + 32],
                                      v[r0:r0 + CH, c // 2, DV * h:DV * h + DV], start=True, stop=True,
                                      skip_group_check=True)
                    last.then_inc(S("kv_ready"), 1)
                rounds = [(t, hp) for t in range(first, TT) for hp in range(2)]

                def scores(r):
                    t, hp = rounds[r]
                    if r >= 2:
                        pe.wait_ge(S("probs_ready"), r - 1)
                    for h in (2 * hp, 2 * hp + 1):
                        rows = slice(32 * h, 32 * h + 32)
                        for dr in range(2):
                            c0 = 512 * (h % 2) + P * dr
                            last = mm(pair[hp][:, c0:c0 + P], k_dec[rows, dr, t * P:(t + 1) * P],
                                      q_dec[rows, dr, t * P:(t + 1) * P], start=True, stop=True, skip_group_check=True)
                    last.then_inc(S("scores_ready"), 1)

                def outputs(r):
                    t, hp = rounds[r]
                    pe.wait_ge(S("probs_ready"), r + 1)
                    opens = t == first or t == 4
                    for h in (2 * hp, 2 * hp + 1):
                        last = mm(pair[2 + hp][64 * (h % 2):64 * (h % 2) + 64, t * P:(t + 1) * P],
                                  v[:, t, DV * h:DV * h + DV], probs[:, r % 2, h % 2, :], start=opens, stop=False,
                                  skip_group_check=True)
                    last.then_inc(S("probs_used"), 1)
                    rows = slice(64 * hp, 64 * hp + 64)
                    for c in (2 * t, 2 * t + 1):
                        for dr in range(2):
                            if c == (0, CTX // CH - 1)[dr]:
                                continue
                            last = mm(pair[2 + hp][:, c * CH:(c + 1) * CH], s_diag[rows, dr, c, :],
                                      q_dec[rows, dr, c * CH:(c + 1) * CH], start=False, stop=True,
                                      skip_group_check=True)
                    if r == len(rounds) - 1:
                        last.then_inc(S("o_ready"), 1)

                pe.wait_ge(S("k2T_ready0"), 1)
                pe.wait_ge(S("k2T_ready1"), 1)
                scores(0)
                scores(1)
                pe.wait_ge(S("s_diag_ready"), 2)
                pe.wait_ge(S("s_diag_ready_a"), 6)
                for r in range(len(rounds)):
                    if 1 <= r < len(rounds) - 1:
                        scores(r + 1)
                    outputs(r)
                for n in range(2 if ty == 0 else 1):
                    for hp in range(2):
                        pe.wait_ge(S("stat_in_ready"), 2 * n + hp + 1)
                        src = (g2, k2T.rearrange("p d t c -> p d (t c)"))[n] if ty == 0 else bcum
                        for t0, width in cuts(CTX * layer):
                            last = mm(pair[hp][:, t0:t0 + width], blocks, src[:, hp, t0:t0 + width], start=True, stop=True)
                        last.then_inc(S("stat_ready"), 1)

            def attention(layer):
                S = lambda name: sem(name)
                pe.wait_ge(sem("ones_r_ready"), 1)
                if layer == 0:
                    pe.wait_ge(sem("y_done_0_1"), 1)
                    mod_slab("prep0", 1, 0)
                    pe.wait_ge(mod_evacuated, first_m["out0"])
                items = attention_items(layer)

                def scores(n):
                    h, b, tiles = items[n]
                    if n == 0:
                        pe.wait_ge(S("kk_lo_ready"), before(layer, "kk_lo_ready") + 1)
                    pe.wait_ge(S("qq_lo_ready"), before(layer, "qq_lo_ready") + h // 2 + 1)
                    if n >= 2:
                        pe.wait_ge(S("exp_ready"), before(layer, "exp_ready") + n - 1)
                    for k in range(tiles):
                        for m, kk in enumerate((kk_hi, kk_lo)):
                            last = mm(score_place(n)[:, k * QB:(k + 1) * QB], kk[:, h // 4, k * P:(k + 1) * P],
                                      qq[:, h // 2 % 2, h % 2, b * QB:(b + 1) * QB], start=(k % 2 == 0 and m == 0),
                                      stop=False, skip_group_check=True)
                    last.then_inc(S("att_scores_ready"), 1)

                def turn_max(n):
                    pe.wait_ge(S("mx_ready"), before(layer, "mx_ready") + n + 1)
                    if n >= 1:
                        pe.wait_ge(S("neg_diag_ready"), before(layer, "neg_diag_ready") + n)
                    for i in range(2):
                        last = nc.tensor.transpose(psum[:, MAX_BANK + P * i:MAX_BANK + P * (i + 1)],
                                                   mx[:, n % 2, P * i:P * (i + 1)], ident)
                    last.then_inc(S("mx_turned"), 1)

                def subtract_max(n):
                    pe.wait_ge(S("neg_diag_ready"), before(layer, "neg_diag_ready") + n + 1)
                    for k in range(items[n][2]):
                        last = mm(score_place(n)[:, k * QB:(k + 1) * QB], ones_r[:], neg_diag[:, n % 2, :], start=False,
                                  stop=True, skip_group_check=True)
                    last.then_inc(S("shifted"), 1)

                def weigh(n, part):
                    h, b, tiles = items[n]
                    if part == 0:
                        pe.wait_ge(S("exp_ready"), before(layer, "exp_ready") + n + 1)
                        if n == 0:
                            pe.wait_ge(S("v_ones_ready"), before(layer, "v_ones_ready") + 1)
                            pe.wait_ge(sem("v_ones_set"), layer + 1)
                        else:
                            pe.wait_ge(S("sums_read"), before(layer, "sums_read") + n)
                            pe.wait_ge(S("out_read"), before(layer, "out_read") + n)
                    for k in range(part * tiles // 2, (part + 1) * tiles // 2):
                        last = mm(psum[:, OUT_BANK:OUT_BANK + QB], v_ones[:, k, h // 4, :],
                                  pexp[:, n % 2, k * QB:(k + 1) * QB], start=(k == 0), stop=(k == tiles - 1),
                                  skip_group_check=True)
                    if part == 1:
                        last.then_inc(S("att_out_ready"), 1)

                scores(0)
                for n in range(len(items) + 2):
                    if n < len(items):
                        turn_max(n)
                    if n >= 2:
                        weigh(n - 2, 0)
                    if n + 1 < len(items):
                        scores(n + 1)
                    if n >= 2:
                        weigh(n - 2, 1)
                    if n < len(items):
                        subtract_max(n)

            pe.wait_ge(cols_ready, 32)
            products("start")
            pe.wait_ge(consts_ready, 32)
            norm_sum(0)
            for layer in range(DEPTH):
                products(f"in{layer}")
                pe.wait_ge(unit_evacuated, 2 * first_w[f"in{layer}"] + 20)
                pe.wait_ge(mod_evacuated, first_m["prep0" if layer == 0 else "out1"])
                scans(layer, 0)
                scans(layer, 1)
                attention(layer)
                products(f"out{layer}")
                norm_sum(2 * layer + 1)
                products(f"mlp{layer}", 0)
                with pe.Fori(1, NFG - 1) as i:
                    products(f"mlp{layer}", i)
                products(f"mlp{layer}", NFG - 1)
                norm_sum(2 * layer + 2)

        @block.scalar
        def _(act):
            F = nc.scalar.activation

            def split_hi(phase, j, i, half):
                item = phases[phase][j]
                slot, ready, u, _ = at(phase, j, i)
                u = u + half
                act.wait_ge(raw_ready[slot], ready)
                if not (phase == "in0" and item[2] == 0):
                    act.wait_ge(unit_done, u - 1)
                if units_of(item) == 1:
                    src = raw[:, slot].rearrange("p k c -> p (k c)")[:, 0:KT * 32].rearrange("p (k c) -> p k c", k=KT)
                    F(w_hi[:, 0, :, 0:32], src, ACT.Copy).then_inc(w_hi_ready, 2)
                else:
                    F(w_hi[:, half], raw[:, slot, :, half * P:(half + 1) * P], ACT.Copy).then_inc(w_hi_ready, 1)

            def run(phase, i=0):
                t_from = 0 if phase.endswith("0") else CTX
                layer = int(phase[-1]) if phase != "start" else 0
                tile = None
                for n, (kind, j, *half) in enumerate(work[phase]):
                    if kind == "t":
                        act.wait_ge(sem("values_turned"), 5 * layer + j + 1)
                        F(turned[j], pair[2][:, 0:T].rearrange("p (t c) -> p t c", t=TT), ACT.Copy).then_inc(
                            sem("values_copied"), 1)
                        continue
                    if kind == "a":
                        head_squares(int(phase[-1]), j)
                        tile = j
                    if kind != "u":
                        continue
                    half = half[0]
                    split_next(split_hi, phase, n, i)
                    if tile is not None:
                        head_root(int(phase[-1]), tile)
                        tile = None
                    item = phases[phase][j]
                    fed = norm_fed(phase, item, i)
                    if fed is not None and 2 * item[2] + half >= 1:
                        square(fed, 2 * item[2] + half - 1, fed >= 3)
                    if item[1] == "1":
                        m = 2 * item[2] + half
                        cnt = (KT * NFG * layer + m + 1) + KT * i
                        _, _, u, _ = at(phase, j, i)
                        act.wait_ge(unit_done, u + half + 1)
                        full = u_full[:, half, t_from:]
                        if not (layer == 0 and m < 2):
                            act.wait_ge(u_lo_ready, cnt - 2)
                        F(full, pair[half][:, 0:T - t_from], ACT.Relu).then_inc(relu_ready, 1)
                        act.wait_ge(unit_evacuated, u + half + 1)
                        F(u_hi[:, m, t_from:], full, ACT.Copy).then_inc(u_hi_ready, 1)

            def square(n, k, lat_only):
                t_from = CTX if lat_only else 0
                if n == 0:
                    act.wait_ge(x_ready, 16)
                else:
                    act.wait_ge(unit_evacuated, units_before_norm[n] - KT + k + 1)
                if k >= 2:
                    act.wait_ge(sem("norm_sq_used"), KT * n + k - 1)
                F(nsq[:, k % 2, t_from:], xT[:, k, t_from:], ACT.Square).then_inc(sem("norm_sq_ready"), 1)

            def norm(n, lat_only, final=False):
                t_from = CTX if lat_only else 0
                for k in range(KT) if n == 0 else (KT - 1,):
                    square(n, k, lat_only)
                behind_norm(split_hi, n)
                act.wait_ge(sem("norm_sum_ready"), n + 1)
                act_link(F(nrs[:, t_from:], pair[2][:, t_from:T], ACT.Ln, bias=EPS, scale=1.0 / D))
                F(nrs[:, t_from:], nrs[:, t_from:], ACT.Exp, scale=-0.5).then_inc(sem("norm_rs_ready"), 1)
                if final:
                    return
                l, sh = n // 2, (SH_A, SH_M)[n % 2]
                for k in range(KT):
                    act.wait_ge(sem("norm_t_ready"), KT * n + k + 1)
                    for t0, t1, s in ([] if lat_only else [(0, CTX, 1)]) + [(CTX, T, 0)]:
                        last = F(h_hi[:, k, t0:t1], nsq[:, k % 2, t0:t1], ACT.Identity, bias=modv[:, l, sh + k, s:s + 1])
                    last.then_inc(h_hi_ready, 1)

            def scans(layer, ty):
                S = lambda name: sem(f"{name}_{layer}_{ty}")
                t_from = 0 if layer == 0 else CTX
                if ty == 1:
                    act.wait_ge(sem(f"y_done_{layer}_0"), 1)
                s = 1.0 if ty == 0 else 1.0 / TAU
                for dr in range(2):
                    act.wait_ge(S("bcum_ready"), dr + 1)
                    F(q_dec[:, dr], bcum[:, dr], ACT.Exp, scale=s).then_inc(S("decays_ready"), 1)
                    F(k_dec[:, dr], bcum[:, dr], ACT.Exp, scale=-s).then_inc(S("decays_ready"), 1)
                if ty == 0:
                    gb = COLS_L + L_N * layer + L_GB
                    act.wait_ge(S("k2_ready"), 2)
                    for dr in range(2):
                        act.wait_ge(sem("z_ready"), 2 * layer + dr + 1)
                        F((ret_q, ret_k)[dr][:], pair[2 + dr][:, 0:T], ACT.Identity, bias=cols[:, gb + dr:gb + dr + 1]).then_inc(
                            sem("z_kept"), 1)
                act.wait_ge(S("k2T_in_psum"), 2)
                F(k2T[:, 1].rearrange("p t c -> p (t c)"), pair[1][:, 0:T], ACT.Copy).then_inc(S("k2T_ready1"), 1)
                act.wait_ge(sem("s_diag_clear"), layer + 1)
                for dr in range(2):
                    act.wait_ge(S("state_ready"), dr + 1)
                    for h in range(3):
                        place_states(lambda o, i: F(o, i, ACT.Copy), h, dr).then_inc(S("s_diag_ready_a"), 1)
                act.wait_ge(S("s_diag_ready"), 2)
                act.wait_ge(S("s_diag_ready_a"), 6)
                for hp in range(2):
                    F(state[:, hp].rearrange("p c e -> p (c e)")[:, t_from:], y[:, 2 * ty + hp, t_from:], ACT.Exp,
                      scale=-1.0).then_inc(S("gate_exp_ready"), 1)
                if ty == 0:
                    for dr in range(2):
                        act.wait_ge(sem("negabs_ready"), 2 * layer + dr + 1)
                        act_link(F(bcum[:, dr], bcum[:, dr], ACT.Exp))
                        F(bcum[:, dr], bcum[:, dr], ACT.Ln, bias=1.0).then_inc(sem("softplus_ready"), 1)
                act.wait_ge(S("o_ready"), 1)
                for hp in range(2):
                    if ty == 0:
                        F(g2[:, hp, t_from:], pair[2 + hp][:, t_from:T], ACT.Copy).then_inc(S("stat_in_ready"), 1)
                    else:
                        F(bcum[:, hp, t_from:], pair[2 + hp][:, t_from:T], ACT.Square).then_inc(S("stat_in_ready"), 1)
                if ty == 0:
                    for hp in range(2):
                        act.wait_ge(S("centred_ready"), hp + 1)
                        F(k2T[:, hp].rearrange("p t c -> p (t c)")[:, t_from:], g2[:, hp, t_from:], ACT.Square).then_inc(
                            S("stat_in_ready"), 1)
                base = 2 if ty == 0 else 0
                for hp in range(2):
                    act.wait_ge(S("stat_ready"), base + hp + 1)
                    act_link(F(q_dec[:, hp, t_from:], pair[hp][:, t_from:T], ACT.Ln, bias=EPS))
                    F(q_dec[:, hp, t_from:], q_dec[:, hp, t_from:], ACT.Exp, scale=-0.5).then_inc(S("head_rs_ready"), 1)

            def attention(layer):
                S = lambda name: sem(name)
                act.wait_ge(sem(f"y_done_{layer}_1"), 1)
                F(v_ones[:, :, :, 0:HD], att_v.rearrange("p t (g e) -> p t g e", g=2), ACT.Copy).then_inc(S("v_ones_ready"), 1)
                act.wait_ge(S("k_ready"), before(layer, "k_ready") + 1)
                for kv in range(2):
                    for half in range(2):
                        last = F(kk_hi[64 * half:64 * half + 64, kv], att_k[64 * kv:64 * kv + 64], ACT.Copy)
                last.then_inc(S("kk_hi_ready"), 1)
                items = attention_items(layer)
                per = len(items) // 4

                def split_q(p):
                    act.wait_ge(S("q_ready"), before(layer, "q_ready") + p + 1)
                    if p >= 2:
                        act.wait_ge(S("att_scores_ready"), before(layer, "att_scores_ready") + per * (p - 1))
                    for half in range(2):
                        rows = slice(64 * half, 64 * half + 64)
                        last = F(qq[rows, p % 2, half, CTX * layer:], y[rows, 4 + p, CTX * layer:], ACT.Copy)
                    last.then_inc(S("qq_hi_ready"), 1)

                split_q(0)
                for n in range(len(items) + 2):
                    if n >= 2:
                        act.wait_ge(S("att_out_ready"), before(layer, "att_out_ready") + n - 1)
                        if n >= 4:
                            act.wait_ge(S("y_att_ready"), before(layer, "y_att_ready") + n - 3)
                        F(rsum[:, n % 2], psum[HD:P, OUT_BANK:OUT_BANK + QB], ACT.Ln).then_inc(S("sums_read"), 1)
                    if n < len(items):
                        act.wait_ge(S("shifted"), before(layer, "shifted") + n + 1)
                        width = QB * items[n][2]
                        F(pexp[:, n % 2, 0:width], score_place(n)[:, 0:width], ACT.Exp, scale=HD ** -0.5).then_inc(
                            S("exp_ready"), 1)
                    if n >= 2:
                        act.wait_ge(S("sums_read"), before(layer, "sums_read") + n - 1)
                        F(rsum[:, n % 2], rsum[:, n % 2], ACT.Exp, scale=-1.0).then_inc(S("rsum_ready"), 1)
                    if n % per == 1 and n // per + 1 < HQ // 2:
                        split_q(n // per + 1)

            def head_squares(layer, n):
                src, t_from, made = normed_tile(layer, n)
                if n == 0:
                    act.wait_ge(h_lo_ready, (KT, 4 * KT)[layer])
                else:
                    act.wait_ge(sem("qsum_ready"), before(layer, "qsum_ready") + n)
                act.wait_ge(unit_evacuated, made + 1)
                F(nsq[:, 0, t_from:], src[:, t_from:], ACT.Square).then_inc(sem("qsq_ready"), 1)

            def head_root(layer, n):
                t_from = normed_tile(layer, n)[1]
                act.wait_ge(sem("qsum_ready"), before(layer, "qsum_ready") + n + 1)
                if n:
                    act.wait_ge(sem("qrs_used"), before(layer, "qrs_used") + n)
                act_link(F(nsq[:, 1, t_from:], pair[2][:, t_from:T], ACT.Ln, bias=EPS))
                F(nsq[:, 1, t_from:], nsq[:, 1, t_from:], ACT.Exp, scale=-0.5).then_inc(sem("qrs_ready"), 1)

            def split_y(layer):
                t_from = 0 if layer == 0 else CTX
                if layer == 0:
                    split_hi("out0", first_weights("out0"), 0, 0)
                act.wait_ge(sem("y_att_ready"), before(layer, "y_att_ready") + len(attention_items(layer)))
                for k in range(KT):
                    F(h_hi[:, k, t_from:], y[:, k, t_from:], ACT.Copy).then_inc(h_hi_ready, 1)

            nc.scalar.preload_act_table_set("natural_log_exp_and_others")
            act.wait_ge(cols_ready, 32)
            F(ones_r[:], ones, ACT.Copy).then_inc(sem("ones_r_ready"), 1)
            act.wait_ge(sem("ln_first"), 1)
            act_link(F(lgam[:, :, :], small[:, 0:4].rearrange("p (l d) -> p l d", l=2), ACT.Exp))
            F(lgam[:, :, :], lgam[:, :, :], ACT.Ln, bias=1.0).then_inc(sem("lgam_softplus"), 1)
            F(silu_c[:], cols[:, 0:16].rearrange("p (k s) -> p k s", s=2), ACT.Exp, scale=-1.0).then_inc(sem("exp_c_ready"), 1)
            norm(0, False)
            for layer in range(DEPTH):
                run(f"in{layer}")
                scans(layer, 0)
                scans(layer, 1)
                attention(layer)
                split_y(layer)
                run(f"out{layer}")
                norm(2 * layer + 1, layer == 1)
                run(f"mlp{layer}", 0)
                with act.Fori(1, NFG - 1) as i:
                    run(f"mlp{layer}", i)
                run(f"mlp{layer}", NFG - 1)
                norm(2 * layer + 2, layer == 1, final=(layer == 1))

        @block.vector
        def _(dve):
            V = nc.vector
            shuffles = {w: [(p // (2 * w)) * 2 * w + (p % (2 * w) + w) % (2 * w) for p in range(32)] for w in (8, 16)}

            def split_lo(phase, j, i, half):
                item = phases[phase][j]
                slot, ready, u, _ = at(phase, j, i)
                u = u + half
                dve.wait_ge(raw_ready[slot], ready)
                if units_of(item) == 1:
                    dve.wait_ge(w_hi_ready, u + 2)
                    src = raw[:, slot].rearrange("p k c -> p (k c)")[:, 0:KT * 32].rearrange("p (k c) -> p k c", k=KT)
                    V.tensor_tensor(w_lo[:, 0, :, 0:32], src, w_hi[:, 0, :, 0:32].bitcast(F32),
                                    ALU.subtract).then_inc(w_lo_ready, 2)
                else:
                    dve.wait_ge(w_hi_ready, u + 1)
                    V.tensor_tensor(w_lo[:, half], raw[:, slot, :, half * P:(half + 1) * P], w_hi[:, half].bitcast(F32),
                                    ALU.subtract).then_inc(w_lo_ready, 1)

            def in_target(s, half):
                if s == ATT_KV:
                    return att_k[:] if half == 0 else y[:, value_place[4]]
                if s in (RET_QK, GLA_QK):
                    return {RET_QK: (ret_q, ret_k), GLA_QK: (gla_q, gla_k)}[s][half][:]
                return y[:, {RET_V: 0, GLA_V: 2, RET_G: 0, GLA_G: 2, ATT_Q01: 4, ATT_Q23: 6}[s] + half]

            def evacuate(phase, j, i, half):
                item = phases[phase][j]
                layer = int(phase[-1])
                _, _, u, _ = at(phase, j, i)
                u = u + half
                ps = pair[half]
                sp = spans(layer, item, half)
                lat = len(sp) == 1
                if item[1] == "in":
                    if units_of(item) == 1:
                        dve.wait_ge(unit_done, u + 2)
                        V.tensor_copy(low[:], ps[0:32, 0:T]).then_inc(unit_evacuated, 2)
                        return
                    dve.wait_ge(unit_done, u + 1)
                    dst = in_target(item[2], half)
                    if item[2] in (ATT_KV, RET_G, GLA_G):
                        dve.wait_ge(sem("values_turned"), 5 * layer + (4 if item[2] == ATT_KV else 5))
                    if lat:
                        V.tensor_copy(dst[:, CTX:T], ps[:, 0:LAT]).then_inc(unit_evacuated, 1)
                    else:
                        V.tensor_copy(dst, ps[:, 0:T]).then_inc(unit_evacuated, 1)
                    if item[2] == RET_G:
                        dve.wait_ge(unit_evacuated, at(phase, phases[phase].index(("w", "in", RET_QK)), 0)[2] + half + 1)
                        rotate((ret_q, ret_k)[half], 0, 8, sem("retention_rotated"), nacc[:, 0:LAT], nrs[:, 0:LAT])
                        dve.wait_ge(sem("retention_rotated"), 2 * layer + half + 1)
                    return
                m = 2 * item[2] + half
                dve.wait_ge(unit_done, u + 1)
                t_from = CTX if lat else 0
                if item[1] == "1":
                    cnt = (KT * NFG * layer + m + 1) + KT * i
                    dve.wait_ge(relu_ready, cnt)
                    full = u_full[:, half, t_from:]
                    V.tensor_tensor(full, full, ps[:, 0:T - t_from], ALU.mult).then_inc(unit_evacuated, 1)
                    dve.wait_ge(u_hi_ready, cnt)
                    V.tensor_tensor(u_lo[:, m, t_from:], full, u_hi[:, m, t_from:].bitcast(F32),
                                    ALU.subtract).then_inc(u_lo_ready, 1)
                    return
                gt = (GT_A if item[1] == "out" else GT_M) + m
                for t0, t1, s in ([] if lat else [(0, CTX, 1)]) + [(CTX, T, 0)]:
                    c0 = t0 - t_from
                    last = V.scalar_tensor_tensor(out=xT[:, m, t0:t1], in0=ps[:, c0:c0 + t1 - t0],
                                                  scalar=modv[:, layer, gt, s:s + 1], in1=xT[:, m, t0:t1],
                                                  op0=ALU.mult, op1=ALU.add)
                last.then_inc(unit_evacuated, 1)

            def sum_mod(phase, j, i):
                slot, ready, _, m = at(phase, j, i)
                n = ahead("m", phase, j, i)
                if repeats[phase] > 1:
                    dve.wait_ge(mod_done, m - 1)
                else:
                    mods = [k for k in flat if k != "w"]
                    earlier = [x for x in range(m) if mods[x] == "m"]
                    if len(earlier) >= 2:
                        dve.wait_ge(mod_done, earlier[-2] + 1)
                    elif not earlier:
                        dve.wait_ge(sem("silu_c_ready"), 1)
                dve.wait_ge(raw_ready[slot], ready)
                for k in range(KT):
                    for s in range(2):
                        a = mod_acc[:, ahead("m", phase, j, 0) % 2, s, :]
                        if k == 0:
                            ins = V.tensor_scalar(a, raw[:, slot, k, :], silu_c[:, k, s:s + 1], None, ALU.mult)
                        else:
                            dve.wait_ge(mod_acc_step, 2 * (KT - 1) * n + 2 * (k - 1) + s + 1)
                            ins = V.scalar_tensor_tensor(out=a, in0=raw[:, slot, k, :], scalar=silu_c[:, k, s:s + 1],
                                                         in1=a, op0=ALU.mult, op1=ALU.add)
                        if k < KT - 1:
                            ins.then_inc(mod_acc_step, 1)
                ins.then_inc(mod_acc_ready, 1)

            def evacuate_mod(phase, j, i):
                item = phases[phase][j]
                _, _, _, m = at(phase, j, i)
                par = (first_m[phase] + mod_number(phase, j)) % 2
                dve.wait_ge(mod_done, m + 1)
                l = item[1]
                ps = pair[3][:, 512 * par:512 * par + 4].rearrange("p (t s) -> p t s", s=2)
                base = COLS_L + L_N * l + L_MODB
                n = item[2] + (4 * i if phase == "mlp0" else 0)
                if phase == "mlp0":
                    out = modv[:, l].rearrange("p (n t) s -> p n (t s)", t=2)[:, bass.ds(n, 1), :].rearrange("p n (t s) -> p (n t) s", s=2)
                    bias = cols[:, base:base + N_MOD].rearrange("p (n t) -> p n t", t=2)[:, bass.ds(n, 1), :]
                    bias = bias.rearrange("p n (t s) -> p (n t) s", s=1)
                else:
                    out = modv[:, l, 2 * n:2 * n + 2, :]
                    bias = cols[:, base + 2 * n:base + 2 * n + 2].rearrange("p (t s) -> p t s", s=1)
                V.tensor_tensor(out, ps, bias.to_broadcast([P, 2, 2]), ALU.add).then_inc(mod_evacuated, 1)

            def run(phase, i=0):
                todo = None
                items = work[phase]
                tile = None
                early = None
                for n, (kind, j, *half) in enumerate(items):
                    if kind == "u":
                        split_next(split_lo, phase, n, i)
                        if todo is not None:
                            evacuate_mod(phase, todo, i)
                            todo = None
                        behind = [later[0] for later in items[n + 1:]]
                        if "s" in behind and "u" not in behind[:behind.index("s")]:
                            early = n + 1 + behind.index("s")
                            sum_mod(phase, items[early][1], i)
                        if tile is not None:
                            head_norm(int(phase[-1]), tile)
                            tile = None
                        evacuate(phase, j, i, half[0])
                        fed = norm_fed(phase, phases[phase][j], i)
                        if fed is not None and 2 * phases[phase][j][2] + half[0] >= 2:
                            add_square(fed, 2 * phases[phase][j][2] + half[0] - 1, fed >= 3)
                    elif kind == "a":
                        tile = j
                    elif kind == "s" and n != early:
                        sum_mod(phase, j, i)
                        if phase == "start" and j == 7:
                            for k in range(1, KT):
                                add_square(0, k, False)
                    elif kind in "mp":
                        if todo is not None:
                            evacuate_mod(phase, todo, i)
                        todo = j
                if todo is not None:
                    evacuate_mod(phase, todo, i)

            def add_square(n, k, lat_only):
                rows = slice(CTX if lat_only else 0, T)
                dve.wait_ge(sem("norm_sq_ready"), KT * n + k + 1)
                a = nsq[:, 0, rows] if k == 1 else nacc[:, rows]
                ins = V.tensor_tensor(nacc[:, rows], a, nsq[:, k % 2, rows], ALU.add)
                ins.then_inc(sem("norm_sq_used"), 2 if k == 1 else 1)
                dve.wait_ge(sem("norm_sq_used"), KT * n + k + 1)

            def norm(n, lat_only, final=False):
                l, sc = n // 2, (SC_A, SC_M)[n % 2]
                if n:
                    add_square(n, KT - 1, lat_only)
                behind_norm(split_lo, n)
                if not final:
                    g = cols[:, COLS_L + L_N * l + (L_AG, L_MG)[n % 2]:][:, 0:KT].rearrange("p (k s) -> p k s", s=1)
                    dve.wait_ge(mod_evacuated, {0: 8, 1: 24, 2: 44, 3: 48}[n])
                    dve_link(V.scalar_tensor_tensor(out=gain[:], in0=modv[:, l, sc:sc + KT, :], scalar=1.0,
                                                    in1=g.to_broadcast([P, KT, 2]), op0=ALU.add, op1=ALU.mult))
                dve.wait_ge(sem("norm_rs_ready"), n + 1)
                for k in range(KT):
                    if final:
                        if k >= 2:
                            dve.wait_ge(sem(f"out_stored{k % 2}"), 16 * (k // 2))
                        V.scalar_tensor_tensor(out=nout[:, k % 2, :], in0=xT[:, k, CTX:T],
                                               scalar=cols[:, COLS_FG + k:COLS_FG + k + 1], in1=nrs[:, CTX:T],
                                               op0=ALU.mult, op1=ALU.mult).then_inc(sem("out_ready"), 1)
                        continue
                    segs = ([] if lat_only else [(0, CTX, 1)]) + [(CTX, T, 0)]
                    if k >= 2:
                        dve.wait_ge(h_lo_ready, h_base[n] + k - 1)
                    for t0, t1, s in segs:
                        last = V.scalar_tensor_tensor(out=nsq[:, k % 2, t0:t1], in0=xT[:, k, t0:t1],
                                                      scalar=gain[:, k, s:s + 1], in1=nrs[:, t0:t1],
                                                      op0=ALU.mult, op1=ALU.mult)
                    last.then_inc(sem("norm_t_ready"), 1)
                    if k >= 1:
                        low_part(n, k - 1, segs)
                if not final:
                    low_part(n, KT - 1, segs)

            def low_part(n, k, segs):
                l, sh = n // 2, (SH_A, SH_M)[n % 2]
                dve.wait_ge(h_hi_ready, h_base[n] + k + 1)
                for t0, t1, s in segs:
                    last = V.scalar_tensor_tensor(out=h_lo[:, k, t0:t1], in0=nsq[:, k % 2, t0:t1],
                                                  scalar=modv[:, l, sh + k, s:s + 1], in1=h_hi[:, k, t0:t1].bitcast(F32),
                                                  op0=ALU.add, op1=ALU.subtract)
                last.then_inc(h_lo_ready, 1)

            h_base = {0: 0, 1: 16, 2: 24, 3: 40}

            def head_norm(layer, n):
                x, t0, _ = normed_tile(layer, n)
                gc = COLS_L + L_N * layer + (L_QG if n else L_KG)
                dve.wait_ge(sem("qrs_ready"), before(layer, "qrs_ready") + n + 1)
                V.scalar_tensor_tensor(out=x[:, t0:], in0=x[:, t0:], scalar=cols[:, gc:gc + 1], in1=nsq[:, 1, t0:],
                                       op0=ALU.mult, op1=ALU.mult).then_inc(sem("qrs_used"), 1)
                dve.wait_ge(sem("qrs_used"), before(layer, "qrs_used") + n + 1)
                done = "q_ready" if n else "k_ready"
                rotate(x, 2, 16, sem(done), nacc[:, 0:LAT], nrs[:, 0:LAT])
                dve.wait_ge(sem(done), before(layer, done) + (n or 1))

            def rotate(x, table, width, done, sw, tt):
                lat = x[:, CTX:T]
                dve_link(V.stream_shuffle(sw, lat, shuffles[width]))
                dve_link(V.tensor_tensor(tt, lat, rope[:, table, :], ALU.mult))
                dve_link(V.tensor_tensor(sw, sw, rope[:, table + 1, :], ALU.mult))
                V.tensor_tensor(lat, tt, sw, ALU.add).then_inc(done, 1)

            def accumulate(g, ready):
                V.tensor_tensor_scan(bcum[:, 0], scan_mask[:], g[0], 0.0, ALU.mult, ALU.add).then_inc(ready, 1)
                V.tensor_tensor_scan(bcum[:, 1, ::-1], scan_mask[:], g[1][:, ::-1], 0.0, ALU.mult, ALU.add).then_inc(ready, 1)

            def gate_decays(layer, stage):
                z = (ret_q, ret_k)
                if stage == 0:
                    dve.wait_ge(sem(f"k2T_in_psum_{layer}_0"), 2)
                for dr in range(2):
                    if stage == 0:
                        dve.wait_ge(sem("z_kept"), 2 * layer + dr + 1)
                        V.scalar_tensor_tensor(out=bcum[:, dr], in0=z[dr][:], scalar=-1.0, in1=z[dr][:], op0=ALU.mult,
                                               op1=ALU.min).then_inc(sem("negabs_ready"), 1)
                    elif stage == 1:
                        dve.wait_ge(sem("softplus_ready"), 2 * layer + dr + 1)
                        dve_link(V.scalar_tensor_tensor(out=z[dr][:], in0=z[dr][:], scalar=0.0, in1=bcum[:, dr],
                                                        op0=ALU.min, op1=ALU.subtract))
                if stage == 2:
                    accumulate((z[0][:], z[1][:]), sem(f"bcum_ready_{layer}_1"))

            def scans(layer, ty):
                S = lambda name: sem(f"{name}_{layer}_{ty}")
                t_from = 0 if layer == 0 else CTX
                q, k = ((ret_q, ret_k), (gla_q, gla_k))[ty]
                if ty == 0:
                    for dr in range(2):
                        dve_link(V.tensor_copy(g2[:, dr], lgam[:, layer, dr:dr + 1].to_broadcast([P, T])))
                    dve.wait_ge(sem("scan_mask_ready"), layer + 1)
                    accumulate((g2[:, 0], g2[:, 1]), S("bcum_ready"))
                qs, ks = ((1.0, KSCALE), (KSCALE, 1.0))[ty]
                for dr in range(2):
                    dve.wait_ge(S("decays_ready"), 2 * dr + 2)
                    whole = (CH - 1, 0)[dr]
                    dve_link(V.tensor_copy(decs[:, dr, :], q_dec[:, dr].rearrange("p (c i) -> p c i", i=CH)[:, :, whole]))
                    V.scalar_tensor_tensor(out=q_dec[:, dr, t_from:], in0=q[:, t_from:], scalar=qs, in1=q_dec[:, dr, t_from:],
                                           op0=ALU.mult, op1=ALU.mult)
                    dve_link(V.scalar_tensor_tensor(out=k_dec[:, dr], in0=k[:], scalar=ks, in1=k_dec[:, dr],
                                                    op0=ALU.mult, op1=ALU.mult))
                    V.tensor_tensor(bcum[:, dr].rearrange("p (c i) -> p c i", i=CH),
                                    k_dec[:, dr].rearrange("p (c i) -> p c i", i=CH),
                                    decs[:, dr, :].rearrange("p (c i) -> p c i", i=1).to_broadcast([P, NCH, CH]),
                                    ALU.mult).then_inc(S("k2_ready"), 1)
                dve.wait_ge(S("k2T_in_psum"), 1)
                V.tensor_copy(k2T[:, 0].rearrange("p t c -> p (t c)"), pair[0][:, 0:T]).then_inc(S("k2T_ready0"), 1)
                if layer == 0 and ty == 1:
                    evacuate_mod("prep0", 0, 0)
                for dr in range(2):
                    dve.wait_ge(S("kv_ready"), dr + 1)
                    path = list(range(NCH)) if dr == 0 else [3, 2, 1, 0] + list(range(NCH - 1, 3, -1))
                    dve_link(V.memset(state[:, dr, path[0], :], 0.0))
                    for a, b in zip(path, path[1:]):
                        kv = pair[2 + dr][:, 512 * (a % 2) + DV * (a // 2):512 * (a % 2) + DV * (a // 2) + DV]
                        ins = V.scalar_tensor_tensor(out=state[:, dr, b, :], in0=state[:, dr, a, :],
                                                     scalar=decs[:, dr, a:a + 1], in1=kv, op0=ALU.mult, op1=ALU.add)
                        if b == path[-1]:
                            ins.then_inc(S("state_ready"), 1)
                        else:
                            dve_link(ins)
                rounds = 2 * (T - t_from) // P
                for r in range(rounds):
                    dve.wait_ge(S("scores_ready"), r + 1)
                    for dr in range(2):
                        src = pair[r % 2][:, :].rearrange("p (b c) -> p b c", b=2)[:, :, P * dr:P * dr + P]
                        msk = (mask_f, mask_b)[dr].rearrange("p (b c) -> p b c", b=1).to_broadcast([P, 2, P])
                        last = V.tensor_tensor(ptmp[:, dr], src, msk, ALU.mult)
                    dve_link(last)
                    if r >= 2:
                        dve.wait_ge(S("probs_used"), r - 1)
                    V.tensor_tensor(probs[:, r % 2], ptmp[:, 0], ptmp[:, 1], ALU.add).then_inc(S("probs_ready"), 1)
                    dve.wait_ge(S("probs_ready"), r + 1)
                    if 1 <= r <= 4:
                        hp, part = (r - 1) // 2, (r - 1) % 2
                        w = (T - t_from) // 2
                        c0 = t_from + w * part
                        e = state[:, hp].rearrange("p c e -> p (c e)")[:, c0:c0 + w]
                        gt = y[:, 2 * ty + hp, c0:c0 + w]
                        dve.wait_ge(S("gate_exp_ready"), hp + 1)
                        dve_link(V.tensor_scalar(e, e, 1.0, None, ALU.add))
                        dve_link(V.reciprocal(e, e))
                        dve_link(V.tensor_tensor(gt, gt, e, ALU.mult))
                    if ty == 0 and 5 <= r <= 7:
                        gate_decays(layer, r - 5)
                rows = slice(t_from, T)
                if ty == 0:
                    for hp in range(2):
                        dve.wait_ge(S("stat_ready"), hp + 1)
                        V.tensor_tensor(g2[:, hp, rows], g2[:, hp, rows], pair[hp][:, rows],
                                        ALU.subtract).then_inc(S("centred_ready"), 1)
                for hp in range(2):
                    gt = y[:, 2 * ty + hp, rows]
                    dve.wait_ge(S("head_rs_ready"), hp + 1)
                    dve_link(V.tensor_tensor(gt, gt, q_dec[:, hp, rows], ALU.mult))
                    o = g2[:, hp, rows] if ty == 0 else pair[2 + hp][:, rows]
                    last = V.tensor_tensor(gt, gt, o, ALU.mult)
                last.then_inc(sem(f"y_done_{layer}_{ty}"), 1)
                dve.wait_ge(sem(f"y_done_{layer}_{ty}"), 1)

            def attention(layer):
                S = lambda name: sem(name)
                dve.wait_ge(S("kk_hi_ready"), before(layer, "kk_hi_ready") + 1)
                for kv in range(2):
                    src = slice(64 * kv, 64 * kv + 64)
                    for half in range(2):
                        last = V.tensor_tensor(kk_lo[64 * half:64 * half + 64, kv], att_k[src], kk_hi[src, kv].bitcast(F32),
                                               ALU.subtract)
                last.then_inc(S("kk_lo_ready"), 1)
                if layer == 0:
                    evacuate_mod("prep0", 1, 0)
                items = attention_items(layer)
                per = len(items) // 4

                def split_q(p):
                    dve.wait_ge(S("qq_hi_ready"), before(layer, "qq_hi_ready") + p + 1)
                    for half in range(2):
                        rows, other = slice(64 * half, 64 * half + 64), slice(64 - 64 * half, 128 - 64 * half)
                        last = V.tensor_tensor(qq[other, p % 2, half, CTX * layer:], y[rows, 4 + p, CTX * layer:],
                                               qq[rows, p % 2, half, CTX * layer:].bitcast(F32), ALU.subtract)
                    last.then_inc(S("qq_lo_ready"), 1)

                def largest(n):
                    dve.wait_ge(S("att_scores_ready"), before(layer, "att_scores_ready") + n + 1)
                    width = QB * items[n][2]
                    V.tensor_reduce(mx[:, n % 2], score_place(n)[:, 0:width].rearrange("p (k q) -> p q k", q=QB), AX.X,
                                    ALU.max).then_inc(S("mx_ready"), 1)

                def negate_max(n):
                    dve.wait_ge(S("mx_turned"), before(layer, "mx_turned") + n + 1)
                    top = small[:, 2 * (n % 2):2 * (n % 2) + 2]
                    dve_link(V.tensor_reduce(top, psum[:, MAX_BANK:MAX_BANK + 2 * P].rearrange("p (i k) -> p i k", i=2),
                                             AX.X, ALU.max))
                    if n >= 2:
                        dve.wait_ge(S("shifted"), before(layer, "shifted") + n - 1)
                    for i in range(2):
                        last = V.tensor_scalar(neg_diag[:, n % 2, P * i:P * (i + 1)], ident, top[:, i:i + 1], -1.0,
                                               ALU.mult, ALU.mult)
                    last.then_inc(S("neg_diag_ready"), 1)

                def out_place(n):
                    h, b, _ = items[n]
                    return y[64 * (h % 2):64 * (h % 2) + 64, 4 + h // 2, b * QB:(b + 1) * QB]

                def take_out(n):
                    dve.wait_ge(S("att_out_ready"), before(layer, "att_out_ready") + n + 1)
                    V.tensor_copy(out_place(n), psum[0:HD, OUT_BANK:OUT_BANK + QB]).then_inc(S("out_read"), 1)

                def divide(n):
                    dst = out_place(n)
                    dve.wait_ge(S("out_read"), before(layer, "out_read") + n + 1)
                    dve.wait_ge(S("rsum_ready"), before(layer, "rsum_ready") + n + 1)
                    V.tensor_tensor(dst, dst, rsum[:, n % 2], ALU.mult).then_inc(S("y_att_ready"), 1)

                split_q(0)
                largest(0)
                for n in range(len(items) + 3):
                    if n < len(items):
                        negate_max(n)
                    if n + 1 < len(items):
                        largest(n + 1)
                    if 2 <= n < len(items) + 2:
                        take_out(n - 2)
                    if n >= 3:
                        divide(n - 3)
                    if n % per == 1 and n // per + 1 < HQ // 2:
                        split_q(n // per + 1)
                dve.wait_ge(S("y_att_ready"), before(layer, "y_att_ready") + len(items))

            def split_y(layer):
                t_from = 0 if layer == 0 else CTX
                if layer == 0:
                    split_lo("out0", first_weights("out0"), 0, 0)
                for k in range(KT):
                    dve.wait_ge(h_hi_ready, (8, 32)[layer] + k + 1)
                    V.tensor_tensor(h_lo[:, k, t_from:], y[:, k, t_from:], h_hi[:, k, t_from:].bitcast(F32),
                                    ALU.subtract).then_inc(h_lo_ready, 1)

            V.memset(small[:], 0.0).then_inc(sem("small_clear"), 1)
            dve.wait_ge(sem("small_clear"), 1)
            dve.wait_ge(cols_ready, 32)
            for l in range(DEPTH):
                rd = COLS_L + L_N * l + L_RD
                last = V.scalar_tensor_tensor(out=small[:, 2 * l:2 * l + 2], in0=cols[:, rd:rd + 2], scalar=-1.0,
                                              in1=cols[:, rd:rd + 2], op0=ALU.mult, op1=ALU.min)
            last.then_inc(sem("ln_first"), 1)
            dve.wait_ge(sem("exp_c_ready"), 1)
            dve_link(V.tensor_scalar(silu_c[:], silu_c[:], 1.0, None, ALU.add))
            dve_link(V.reciprocal(silu_c[:], silu_c[:]))
            V.tensor_tensor(silu_c[:], silu_c[:], cols[:, 0:16].rearrange("p (k s) -> p k s", s=2),
                            ALU.mult).then_inc(sem("silu_c_ready"), 1)
            dve.wait_ge(sem("lgam_softplus"), 1)
            for l in range(DEPTH):
                rd = COLS_L + L_N * l + L_RD
                dve_link(V.scalar_tensor_tensor(out=lgam[:, l, :], in0=cols[:, rd:rd + 2], scalar=0.0, in1=lgam[:, l, :],
                                                op0=ALU.min, op1=ALU.subtract))
            run("start")
            norm(0, False)
            dve.wait_ge(consts_ready, 32)
            for layer in range(DEPTH):
                run(f"in{layer}")
                dve.wait_ge(unit_evacuated, 2 * first_w[f"in{layer}"] + 20)
                scans(layer, 0)
                scans(layer, 1)
                attention(layer)
                split_y(layer)
                dve.wait_ge(mod_evacuated, first_m[f"out{layer}"])
                run(f"out{layer}")
                norm(2 * layer + 1, layer == 1)
                run(f"mlp{layer}", 0)
                with dve.Fori(1, NFG - 1) as i:
                    run(f"mlp{layer}", i)
                run(f"mlp{layer}", NFG - 1)
                norm(2 * layer + 2, layer == 1, final=(layer == 1))

        @block.gpsimd
        def _(pool):
            for layer in range(DEPTH):
                pool.wait_ge(sem("retention_rotated"), 2 * layer + 2)
                nc.gpsimd.memset(s_diag[:], 0.0).then_inc(sem("s_diag_clear"), 1)
                pool.wait_ge(sem("s_diag_clear"), layer + 1)
                pool.wait_ge(unit_done, 2 * first_w[f"in{layer}"] + 20)
                nc.gpsimd.memset(scan_mask[:], 1.0).then_inc(sem("scan_mask_filled"), 1)
                pool.wait_ge(sem("scan_mask_filled"), layer + 1)
                nc.gpsimd.memset(scan_mask.rearrange("p (c i) -> p c i", i=CH)[:, :, 0], 0.0).then_inc(sem("scan_mask_ready"), 1)
                for ty in range(2):
                    for dr in range(2):
                        pool.wait_ge(sem(f"state_ready_{layer}_{ty}"), dr + 1)
                        place_states(nc.gpsimd.tensor_copy, 3, dr).then_inc(sem(f"s_diag_ready_{layer}_{ty}"), 1)
                pool.wait_ge(sem(f"y_done_{layer}_1"), 1)
                nc.gpsimd.memset(v_ones[:, :, :, HD:P], 1.0).then_inc(sem("v_ones_set"), 1)


def kernel(**inputs):
    import numpy as np
    import concourse.bacc as bacc
    from concourse import mybir
    from concourse.bass_utils import run_bass_kernel_spmd as run

    a = {k: np.asarray(v) for k, v in inputs.items()}
    f = np.float32

    def tiles(m):
        return np.ascontiguousarray(m.reshape(KT, P, -1).transpose(1, 0, 2))

    def slabs(w, groups):
        lead, cols = w.shape[:-2], w.shape[-1]
        w = w.reshape(lead + (groups, KT, P, cols // SLAB, SLAB))
        n = len(lead)
        w = w.transpose(tuple(range(n + 1)) + (n + 3, n + 2, n + 1, n + 4))
        return np.ascontiguousarray(w).reshape(lead + (groups, cols // SLAB, P, KT * SLAB))

    arrays = {}
    arrays["xT"] = tiles(np.concatenate([a["ctx"][0], a["x"][0]], axis=0).T)
    arrays["mod_w"] = slabs(a["mod_w"], 1)[:, 0]
    arrays["w_out"] = slabs(a["w_out"], 1)[:, 0]
    w1 = a["mlp_w1"].reshape(DEPTH, D, NFG, D).transpose(0, 2, 1, 3)
    arrays["w_1"] = slabs(w1, 1)[:, :, 0].reshape(DEPTH * NFG, 4, P, KT * SLAB)
    arrays["w_2"] = slabs(a["mlp_w2"], NFG).reshape(DEPTH * NFG, 4, P, KT * SLAB)
    win = a["w_in"].reshape(DEPTH, KT, P, W_IN).transpose(0, 2, 1, 3)
    arrays["w_in"] = np.concatenate([win[..., c:c + w].reshape(DEPTH, P, KT * w) for c, w in sorted(W_IN_SLABS)], axis=2)

    def col(v):
        return v.reshape(-1, P).T
    parts = [np.stack([col(a["c"][0]), col(a["c_ctx"])], axis=2).reshape(P, 2 * KT), col(a["final_norm_g"])]
    for l in range(DEPTH):
        parts += [col(a["mod_b"][l]), col(a["attn_norm_g"][l]), col(a["mlp_norm_g"][l]),
                  np.tile(a["qk_norm_g"][l, 0], 2)[:, None], np.tile(a["qk_norm_g"][l, 1], 2)[:, None],
                  a["gla_gate_b"][l].T, np.repeat(a["ret_decay_logit"][l].T, DK, axis=0)]
    arrays["cols"] = np.ascontiguousarray(np.concatenate(parts, axis=1))
    gw = np.zeros((32, DEPTH, 2, P), f)
    gw[0:16, :, 0] = a["gla_gate_w"][:, 0].transpose(1, 0, 2)
    gw[16:32, :, 1] = a["gla_gate_w"][:, 1].transpose(1, 0, 2)
    arrays["gate_w"] = gw

    tok = np.arange(LAT)
    row, column = (tok // 64).astype(f), (tok % 64).astype(f)
    table = np.zeros((P, 4, LAT), f)
    for n, width in ((0, 8), (2, 16)):
        freq = (f(10000.0) ** (-np.arange(width, dtype=f) / f(width))).astype(f)
        for p in range(P):
            q = p % (4 * width)
            ang = (row if q < 2 * width else column) * freq[q % width]
            table[p, n] = np.cos(ang)
            table[p, n + 1] = np.sin(ang) * (-1 if q % (2 * width) < width else 1)
    arrays["rope"] = table
    i, j = np.meshgrid(np.arange(P), np.arange(P), indexing="xy")
    same = i // CH == j // CH
    arrays["squares"] = np.ascontiguousarray(np.stack(
        [same & (j <= i), same & (j > i), i == j, np.ones((P, P)), (i // 64 == j // 64) / 64.0], axis=1).astype(f))

    nc = bacc.Bacc("TRN2", target_bir_lowering=False, num_devices=1)
    drams = {k: nc.dram_tensor(f"in_{k}", v.shape, mybir.dt.float32, kind="ExternalInput").ap() for k, v in arrays.items()}
    drams["out"] = nc.dram_tensor("out", (P, KT, LAT), mybir.dt.float32, kind="ExternalOutput").ap()
    build(nc, drams)
    r = run(nc, [{f"in_{k}": v for k, v in arrays.items()}], core_ids=[0])
    return r.results[0]["out"].transpose(2, 1, 0).reshape(1, LAT, D)
```
